# Optimizing a Trainium2 kernel written in Bass

```python
import math
import jax
import jax.numpy as jnp
from jax import lax
import numpy as np
import jax, jax.numpy as jnp

D_MODEL = 1024
BATCH = 1
SEQ = 512
DEPTH = 1

GRID_W = 64
CTX_LEN = 256

DA_HEADS = 4
DA_HEAD_DIM = 64
DA_V_DIM = 2 * DA_HEAD_DIM
DA_WIDTH = DA_HEADS * DA_V_DIM
HG_HEADS = 4
HG_HEAD_DIM = 128
HG_WIDTH = HG_HEADS * HG_HEAD_DIM
MIX_WIDTH = DA_WIDTH + HG_WIDTH
IN_WIDTH = 3 * DA_WIDTH + 5 * HG_WIDTH
SPLITS = (DA_WIDTH, 2 * DA_WIDTH, 3 * DA_WIDTH, 3 * DA_WIDTH + HG_WIDTH,
          3 * DA_WIDTH + 2 * HG_WIDTH, 3 * DA_WIDTH + 3 * HG_WIDTH, 3 * DA_WIDTH + 4 * HG_WIDTH)
CTX_KV_END = 3 * DA_WIDTH + 3 * HG_WIDTH
CTX_SPLITS = (DA_WIDTH, 2 * DA_WIDTH, 2 * DA_WIDTH + HG_WIDTH, 2 * DA_WIDTH + 2 * HG_WIDTH)
CHUNK = 64
Q_BLOCK = 128
N_EXPERTS = 16
CAPACITY_FACTOR = 2
EXPERT_FF = 1024
ROPE_THETA = 10000.0
NORM_EPS = 1e-6


def rmsnorm(x, g):
    xf = x.astype(jnp.float32)
    y = xf * lax.rsqrt(jnp.mean(xf * xf, axis=-1, keepdims=True) + NORM_EPS)
    return (y * g.astype(jnp.float32)).astype(x.dtype)

def modulate(h, shift, scale):
    return h * (1.0 + scale) + shift

def axial_rope_tables(rows):
    half = DA_HEAD_DIM // 2
    inv_freq = 1.0 / (ROPE_THETA ** (jnp.arange(0, half, 2, dtype=jnp.float32) / half))
    r, col = jnp.meshgrid(jnp.arange(rows, dtype=jnp.float32),
                          jnp.arange(GRID_W, dtype=jnp.float32), indexing="ij")
    ang_r = r.reshape(-1)[:, None] * inv_freq
    ang_c = col.reshape(-1)[:, None] * inv_freq
    ang = jnp.concatenate([ang_r, ang_r, ang_c, ang_c], axis=-1)
    return jnp.cos(ang), jnp.sin(ang)

def apply_axial_rope(x, cos, sin):
    xf = x.astype(jnp.float32)
    x1, x2, x3, x4 = jnp.split(xf, 4, axis=-1)
    rot = jnp.concatenate([-x2, x1, -x4, x3], axis=-1)
    return (xf * cos + rot * sin).astype(x.dtype)

def qk_heads(a):
    b, t = a.shape[:2]
    return a.reshape(b, t, DA_HEADS, 2, DA_HEAD_DIM).transpose(0, 2, 3, 1, 4)

def to_heads(a, n_heads, dim):
    b, t = a.shape[:2]
    return a.reshape(b, t, n_heads, dim).transpose(0, 2, 1, 3)

def merge_heads(o):
    b, h, t, d = o.shape
    return o.transpose(0, 2, 1, 3).reshape(b, t, h * d)

def diff_attend(q, k, v, lam):
    s = jnp.einsum("bhiqd,bhikd->bhiqk", q, k).astype(jnp.float32) * (DA_HEAD_DIM ** -0.5)
    p = jax.nn.softmax(s, axis=-1)
    a = p[:, :, 0] - lam * p[:, :, 1]
    return jnp.einsum("bhqk,bhkd->bhqd", a.astype(v.dtype), v)

def hgrn2_chunk_scan(k, v, log_f, s0, q=None):
    b_, h_, t_, _ = k.shape
    dv = v.shape[-1]
    n = t_ // CHUNK

    def chunks(a):
        return jnp.moveaxis(a.astype(jnp.float32).reshape(b_, h_, n, CHUNK, a.shape[-1]), 2, 0)

    lower = jnp.tril(jnp.ones((CHUNK, CHUNK), dtype=bool))[:, :, None]

    def step(S, inp):
        kc, vc, lc = inp[0], inp[1], inp[2]
        bcum = jnp.cumsum(lc, axis=2)
        b_end = bcum[:, :, -1:, :]
        S_next = (jnp.exp(b_end[:, :, 0, :, None]) * S
                  + jnp.einsum("bhsk,bhsv->bhkv", kc * jnp.exp(b_end - bcum), vc))
        if q is None:
            return S_next, None
        qc = inp[3]
        rel = bcum[:, :, :, None, :] - bcum[:, :, None, :, :]
        decay = jnp.exp(jnp.where(lower, rel, -jnp.inf))
        scores = jnp.einsum("bhrk,bhsk,bhrsk->bhrs", qc, kc, decay)
        o = (jnp.einsum("bhrk,bhkv->bhrv", qc * jnp.exp(bcum), S)
             + jnp.einsum("bhrs,bhsv->bhrv", scores, vc))
        return S_next, o

    xs = (chunks(k), chunks(v), chunks(log_f))
    if q is not None:
        xs = xs + (chunks(q),)
    S_fin, o = lax.scan(step, s0, xs)
    if q is not None:
        o = jnp.moveaxis(o, 0, 2).reshape(b_, h_, t_, dv).astype(v.dtype)
    return o, S_fin

def forget_gate(z, lb):
    f = lb + (1.0 - lb) * jax.nn.sigmoid(z.astype(jnp.float32))
    return jnp.log(f), 1.0 - f

def token_mixer(h_lat, h_ctx, w_in, w_out, lam, lambda_init, da_subln, lb, hg_norm, cos, sin, ctx_out):
    b_ = h_lat.shape[0]
    da_q, da_k, da_v, hg_ff, hg_fb, hg_i, hg_q, hg_g = jnp.split(h_lat @ w_in, SPLITS, axis=-1)
    c_da_k, c_da_v, c_ff, c_fb, c_i = jnp.split(h_ctx @ w_in[:, DA_WIDTH:CTX_KV_END], CTX_SPLITS, axis=-1)
    if ctx_out:
        c_da_q = h_ctx @ w_in[:, :DA_WIDTH]
        c_hg_q, c_hg_g = jnp.split(h_ctx @ w_in[:, CTX_KV_END:], 2, axis=-1)

    q = apply_axial_rope(qk_heads(da_q), cos, sin)
    k_ctx = qk_heads(c_da_k)
    k_all = jnp.concatenate([k_ctx, apply_axial_rope(qk_heads(da_k), cos, sin)], axis=3)
    v_ctx = to_heads(c_da_v, DA_HEADS, DA_V_DIM)
    v_all = jnp.concatenate([v_ctx, to_heads(da_v, DA_HEADS, DA_V_DIM)], axis=2)
    t_ = q.shape[3]
    n_blk = t_ // Q_BLOCK
    q_blocks = jnp.moveaxis(q.reshape(b_, DA_HEADS, 2, n_blk, Q_BLOCK, DA_HEAD_DIM), 3, 0)
    o_blocks = lax.map(lambda qb: diff_attend(qb, k_all, v_all, lam), q_blocks)
    o_da = jnp.moveaxis(o_blocks, 0, 2).reshape(b_, DA_HEADS, t_, DA_V_DIM)
    out_da = merge_heads(rmsnorm(o_da, da_subln) * (1.0 - lambda_init))

    v_lat = to_heads(hg_i, HG_HEADS, HG_HEAD_DIM)
    v_c = to_heads(c_i, HG_HEADS, HG_HEAD_DIM)
    q_lat = to_heads(hg_q, HG_HEADS, HG_HEAD_DIM)
    q_c = to_heads(c_hg_q, HG_HEADS, HG_HEAD_DIM) if ctx_out else None
    s0 = jnp.zeros((b_, HG_HEADS, HG_HEAD_DIM, HG_HEAD_DIM), jnp.float32)
    o_hg_lat = None
    o_hg_ctx = None
    for d, (z_lat, z_ctx) in enumerate(((hg_ff, c_ff), (hg_fb, c_fb))):
        flip = (lambda a: a) if d == 0 else (lambda a: jnp.flip(a, axis=2))
        lf_l, k_l = forget_gate(z_lat, lb[d])
        lf_c, k_c = forget_gate(z_ctx, lb[d])
        k_l, lf_l = to_heads(k_l, HG_HEADS, HG_HEAD_DIM), to_heads(lf_l, HG_HEADS, HG_HEAD_DIM)
        k_c, lf_c = to_heads(k_c, HG_HEADS, HG_HEAD_DIM), to_heads(lf_c, HG_HEADS, HG_HEAD_DIM)
        o_c, S_c = hgrn2_chunk_scan(flip(k_c), flip(v_c), flip(lf_c), s0,
                                    q=None if q_c is None else flip(q_c))
        o_l, _ = hgrn2_chunk_scan(flip(k_l), flip(v_lat), flip(lf_l), S_c, q=flip(q_lat))
        o_hg_lat = flip(o_l) if o_hg_lat is None else o_hg_lat + flip(o_l)
        if ctx_out:
            o_hg_ctx = flip(o_c) if o_hg_ctx is None else o_hg_ctx + flip(o_c)
    out_hg = merge_heads(rmsnorm(o_hg_lat, hg_norm)) * jax.nn.silu(hg_g)

    y_lat = jnp.concatenate([out_da, out_hg], axis=-1) @ w_out
    if not ctx_out:
        return y_lat, None
    o_c_da = diff_attend(qk_heads(c_da_q), k_ctx, v_ctx, lam)
    out_c_da = merge_heads(rmsnorm(o_c_da, da_subln) * (1.0 - lambda_init))
    out_c_hg = merge_heads(rmsnorm(o_hg_ctx, hg_norm)) * jax.nn.silu(c_hg_g)
    y_ctx = jnp.concatenate([out_c_da, out_c_hg], axis=-1) @ w_out
    return y_lat, y_ctx

def expert_choice_ffn(h, w_router, w_gate, w_up, w_down):
    b_, t_, d_ = h.shape
    cap = CAPACITY_FACTOR * t_ // N_EXPERTS
    aff = jax.nn.softmax(jnp.einsum("btd,de->bte", h, w_router).astype(jnp.float32), axis=-1)
    top_aff, top_idx = lax.top_k(jnp.swapaxes(aff, 1, 2), cap)
    xin = jax.vmap(lambda hb, ib: hb[ib])(h, top_idx)
    g = jnp.einsum("becd,edf->becf", xin, w_gate)
    u = jnp.einsum("becd,edf->becf", xin, w_up)
    y = jnp.einsum("becf,efd->becd", jax.nn.silu(g) * u, w_down) * top_aff[..., None].astype(h.dtype)
    return jax.vmap(lambda yb, ib: jnp.zeros((t_, d_), h.dtype).at[ib.reshape(-1)].add(yb.reshape(-1, d_)))(y, top_idx)

def first_inputs(seed: int = 0) -> dict:
    key = jax.random.key(seed)
    ks = jax.random.split(key, 24)
    D = D_MODEL

    def nrm(k, shape, scale):
        return jax.random.normal(k, shape, jnp.float32) * scale

    return {
        "x": nrm(ks[0], (BATCH, SEQ, D), 1.0),
        "c": nrm(ks[1], (BATCH, D), 1.0),
        "ctx": nrm(ks[2], (BATCH, CTX_LEN, D), 1.0),
        "c_ctx": nrm(ks[3], (D,), 1.0),
        "w_ada": nrm(ks[4], (DEPTH, D, 6 * D), 0.5 * D ** -0.5),
        "b_ada": nrm(ks[5], (DEPTH, 6 * D), 0.02),
        "norm_pre_mix": 1.0 + nrm(ks[6], (DEPTH, D), 0.05),
        "norm_post_mix": 1.0 + nrm(ks[7], (DEPTH, D), 0.05),
        "norm_pre_ffn": 1.0 + nrm(ks[8], (DEPTH, D), 0.05),
        "norm_post_ffn": 1.0 + nrm(ks[9], (DEPTH, D), 0.05),
        "w_in": nrm(ks[10], (DEPTH, D, IN_WIDTH), D ** -0.5),
        "da_lambda_q1": nrm(ks[11], (DEPTH, DA_HEAD_DIM), 0.1),
        "da_lambda_k1": nrm(ks[12], (DEPTH, DA_HEAD_DIM), 0.1),
        "da_lambda_q2": nrm(ks[13], (DEPTH, DA_HEAD_DIM), 0.1),
        "da_lambda_k2": nrm(ks[14], (DEPTH, DA_HEAD_DIM), 0.1),
        "da_subln": 1.0 + nrm(ks[15], (DEPTH, DA_V_DIM), 0.05),
        "hg_lower_bound": nrm(ks[16], (DEPTH + 1, 2, HG_WIDTH), 0.5),
        "hg_norm": 1.0 + nrm(ks[17], (DEPTH, HG_HEAD_DIM), 0.05),
        "w_out": nrm(ks[18], (DEPTH, MIX_WIDTH, D), MIX_WIDTH ** -0.5),
        "w_router": nrm(ks[19], (DEPTH, D, N_EXPERTS), D ** -0.5),
        "w_gate": nrm(ks[20], (DEPTH, N_EXPERTS, D, EXPERT_FF), D ** -0.5),
        "w_up": nrm(ks[21], (DEPTH, N_EXPERTS, D, EXPERT_FF), D ** -0.5),
        "w_down": nrm(ks[22], (DEPTH, N_EXPERTS, EXPERT_FF, D), EXPERT_FF ** -0.5),
    }

def first_block(x, c, ctx, c_ctx, w_ada, b_ada, norm_pre_mix, norm_post_mix, norm_pre_ffn, norm_post_ffn,
              w_in, da_lambda_q1, da_lambda_k1, da_lambda_q2, da_lambda_k2, da_subln, hg_lower_bound,
              hg_norm, w_out, w_router, w_gate, w_up, w_down):
    T = x.shape[1]
    ROWS = T // GRID_W
    cos, sin = axial_rope_tables(ROWS)
    lb_all = jnp.cumsum(jax.nn.softmax(hg_lower_bound.astype(jnp.float32), axis=0), axis=0)
    x_lat, x_ctx = x, ctx
    for l in range(DEPTH):
        last = l == DEPTH - 1
        lambda_init = 0.8 - 0.6 * math.exp(-0.3 * l)
        lam = (jnp.exp(jnp.sum(da_lambda_q1[l].astype(jnp.float32) * da_lambda_k1[l].astype(jnp.float32)))
               - jnp.exp(jnp.sum(da_lambda_q2[l].astype(jnp.float32) * da_lambda_k2[l].astype(jnp.float32)))
               + lambda_init)
        mod_lat = jax.nn.silu(c) @ w_ada[l] + b_ada[l]
        mod_ctx = jax.nn.silu(c_ctx) @ w_ada[l] + b_ada[l]
        sh1, sc1, gt1, sh2, sc2, gt2 = jnp.split(mod_lat[:, None, :], 6, axis=-1)
        csh1, csc1, cgt1, csh2, csc2, cgt2 = jnp.split(mod_ctx, 6, axis=-1)

        h_lat = modulate(rmsnorm(x_lat, norm_pre_mix[l]), sh1, sc1)
        h_ctx = modulate(rmsnorm(x_ctx, norm_pre_mix[l]), csh1, csc1)
        y_lat, y_ctx = token_mixer(h_lat, h_ctx, w_in[l], w_out[l], lam, lambda_init, da_subln[l],
                                   lb_all[l], hg_norm[l], cos, sin, not last)
        x_lat = x_lat + gt1 * rmsnorm(y_lat, norm_post_mix[l])
        h_lat = modulate(rmsnorm(x_lat, norm_pre_ffn[l]), sh2, sc2)
        f_lat = expert_choice_ffn(h_lat, w_router[l], w_gate[l], w_up[l], w_down[l])
        x_lat = x_lat + gt2 * rmsnorm(f_lat, norm_post_ffn[l])
        if not last:
            x_ctx = x_ctx + cgt1 * rmsnorm(y_ctx, norm_post_mix[l])
            h_ctx = modulate(rmsnorm(x_ctx, norm_pre_ffn[l]), csh2, csc2)
            f_ctx = expert_choice_ffn(h_ctx, w_router[l], w_gate[l], w_up[l], w_down[l])
            x_ctx = x_ctx + cgt2 * rmsnorm(f_ctx, norm_post_ffn[l])
    return x_lat


N_MIXERS = 3
N_LAYERS_A = len(range(0, DEPTH, N_MIXERS))
N_LAYERS_B = len(range(1, DEPTH, N_MIXERS))
N_LAYERS_C = len(range(2, DEPTH, N_MIXERS))
RMS_EPS = 1e-6
D_FF = 4 * D_MODEL
CONV_W = 4

GDN_DK = 128
GDN_DV = 128
GDN_HEADS = D_MODEL // GDN_DK
GDN_QK = GDN_HEADS * GDN_DK
GDN_V = GDN_HEADS * GDN_DV
GDN_CONV_CH = 2 * GDN_QK + GDN_V
GDN_IN = GDN_CONV_CH + GDN_V + 2 * GDN_HEADS

S5_GROUP = 16
S5_GROUPS = D_MODEL // S5_GROUP
S5_STATE = 64

M2_INNER = 2 * D_MODEL
M2_HEAD_DIM = 64
M2_HEADS = M2_INNER // M2_HEAD_DIM
M2_GROUPS = 8
M2_HPG = M2_HEADS // M2_GROUPS
M2_STATE = 128
M2_BC = M2_GROUPS * M2_STATE
M2_CONV_CH = M2_INNER + 2 * M2_BC
M2_IN = M2_INNER + M2_CONV_CH + M2_HEADS


def rmsnorm_2(x, g):
    xf = x.astype(jnp.float32)
    y = xf * lax.rsqrt(jnp.mean(xf * xf, axis=-1, keepdims=True) + RMS_EPS)
    return (y * g.astype(jnp.float32)).astype(x.dtype)

def causal_dwconv(x, w):
    return lax.conv_general_dilated(
        x, w[:, None, :], window_strides=(1,), padding=[(w.shape[0] - 1, 0)],
        dimension_numbers=("NWC", "WIO", "NWC"), feature_group_count=x.shape[-1])

def l2norm(t):
    return t * lax.rsqrt(jnp.sum(t * t, axis=-1, keepdims=True) + 1e-6)

def gated_deltanet(h, w_in, conv_w, a_log, dt_bias, o_norm_g, w_out):
    bsz, L, _ = h.shape
    nc = L // CHUNK
    f32 = jnp.float32
    proj = h @ w_in
    qkv, gate, a_raw, b_raw = jnp.split(
        proj, [GDN_CONV_CH, GDN_CONV_CH + GDN_V, GDN_CONV_CH + GDN_V + GDN_HEADS], axis=-1)
    qkv = jax.nn.silu(causal_dwconv(qkv, conv_w)).astype(f32)
    q, k, v = jnp.split(qkv, [GDN_QK, 2 * GDN_QK], axis=-1)
    q = l2norm(q.reshape(bsz, L, GDN_HEADS, GDN_DK)) * (GDN_DK ** -0.5)
    k = l2norm(k.reshape(bsz, L, GDN_HEADS, GDN_DK))
    v = v.reshape(bsz, L, GDN_HEADS, GDN_DV)
    g = -jnp.exp(a_log.astype(f32)) * jax.nn.softplus(a_raw.astype(f32) + dt_bias.astype(f32))
    beta = jax.nn.sigmoid(b_raw.astype(f32))

    def to_chunks(t):
        return t.reshape(bsz, nc, CHUNK, GDN_HEADS, -1).transpose(0, 3, 1, 2, 4)

    qc, kc, vc = to_chunks(q), to_chunks(k), to_chunks(v)
    gc = g.reshape(bsz, nc, CHUNK, GDN_HEADS).transpose(0, 3, 1, 2)
    bc = beta.reshape(bsz, nc, CHUNK, GDN_HEADS).transpose(0, 3, 1, 2)
    G = jnp.cumsum(gc, axis=-1)
    idx = jnp.arange(CHUNK)
    causal = idx[:, None] >= idx[None, :]
    strict = idx[:, None] > idx[None, :]
    decay = jnp.exp(jnp.where(causal, G[..., :, None] - G[..., None, :], -jnp.inf))
    kk = jnp.einsum('bhcid,bhcjd->bhcij', kc, kc)
    tri = jnp.where(strict, bc[..., :, None] * kk * decay, 0.0) + jnp.eye(CHUNK, dtype=f32)
    rhs = jnp.concatenate([vc * bc[..., None], kc * (bc * jnp.exp(G))[..., None]], axis=-1)
    sol = lax.linalg.triangular_solve(tri, rhs, left_side=True, lower=True, unit_diagonal=True)
    u, w = sol[..., :GDN_DV], sol[..., GDN_DV:]
    qk = jnp.einsum('bhcid,bhcjd->bhcij', qc, kc) * decay
    q_dec = qc * jnp.exp(G)[..., None]
    k_dec = kc * jnp.exp(G[..., -1:] - G)[..., None]
    chunk_decay = jnp.exp(G[..., -1])
    xs = tuple(jnp.moveaxis(t, 2, 0) for t in (u, w, qk, q_dec, k_dec, chunk_decay))

    def step(S, inp):
        u_c, w_c, qk_c, qd_c, kd_c, cd_c = inp
        v_new = u_c - jnp.einsum('bhid,bhde->bhie', w_c, S)
        o = jnp.einsum('bhid,bhde->bhie', qd_c, S) + jnp.einsum('bhij,bhje->bhie', qk_c, v_new)
        S = cd_c[..., None, None] * S + jnp.einsum('bhid,bhie->bhde', kd_c, v_new)
        return S, o

    S0 = jnp.zeros((bsz, GDN_HEADS, GDN_DK, GDN_DV), f32)
    _, o = lax.scan(step, S0, xs)
    o = o.transpose(1, 0, 3, 2, 4).reshape(bsz, L, GDN_HEADS, GDN_DV)
    o = rmsnorm_2(o, o_norm_g) * jax.nn.silu(gate.astype(f32).reshape(bsz, L, GDN_HEADS, GDN_DV))
    return o.reshape(bsz, L, GDN_V).astype(h.dtype) @ w_out

def s5_mixer(h, w_in, lam_re, lam_im, log_dt, b_re, b_im, c_re, c_im, d_skip, w_out):
    bsz, L, _ = h.shape
    f32 = jnp.float32
    u = (h @ w_in).astype(f32)
    ug = u.reshape(bsz, L, S5_GROUPS, S5_GROUP).transpose(1, 0, 2, 3)
    lam = lax.complex(lam_re.astype(f32), lam_im.astype(f32))
    dt = jnp.exp(log_dt.astype(f32))[:, None]
    lam_bar = jnp.exp(lam * dt)
    b_bar = ((lam_bar - 1.0) / lam)[..., None] * lax.complex(b_re.astype(f32), b_im.astype(f32))
    bu = jnp.einsum('gpk,lbgk->lbgp', b_bar, ug.astype(jnp.complex64))
    a = jnp.broadcast_to(lam_bar[None, None], (L, 1, S5_GROUPS, S5_STATE))

    def combine(e1, e2):
        a1, b1 = e1
        a2, b2 = e2
        return a1 * a2, a2 * b1 + b2

    _, states = lax.associative_scan(combine, (a, bu), axis=0)
    c = lax.complex(c_re.astype(f32), c_im.astype(f32))
    y = jnp.real(jnp.einsum('gkp,lbgp->lbgk', c, states)) \
        + d_skip.astype(f32).reshape(S5_GROUPS, S5_GROUP) * ug
    y = jax.nn.gelu(y.transpose(1, 0, 2, 3).reshape(bsz, L, D_MODEL)).astype(h.dtype)
    ag = y @ w_out
    val, gt = jnp.split(ag, 2, axis=-1)
    return val * jax.nn.sigmoid(gt)

def mamba2_mixer(h, w_in, conv_w, conv_b, dt_bias, a_log, d_skip, norm_g, w_out):
    bsz, L, _ = h.shape
    nc = L // CHUNK
    f32 = jnp.float32
    proj = h @ w_in
    z, xbc, dt_raw = jnp.split(proj, [M2_INNER, M2_INNER + M2_CONV_CH], axis=-1)
    xbc = jax.nn.silu(causal_dwconv(xbc, conv_w) + conv_b).astype(f32)
    xs, Bm, Cm = jnp.split(xbc, [M2_INNER, M2_INNER + M2_BC], axis=-1)
    x = xs.reshape(bsz, L, M2_HEADS, M2_HEAD_DIM)
    dt = jax.nn.softplus(dt_raw.astype(f32) + dt_bias.astype(f32))
    dA = dt * (-jnp.exp(a_log.astype(f32)))
    xdt = (x * dt[..., None]).reshape(bsz, nc, CHUNK, M2_GROUPS, M2_HPG, M2_HEAD_DIM)
    Bc = Bm.reshape(bsz, nc, CHUNK, M2_GROUPS, M2_STATE)
    Cc = Cm.reshape(bsz, nc, CHUNK, M2_GROUPS, M2_STATE)
    cum = jnp.cumsum(dA.reshape(bsz, nc, CHUNK, M2_GROUPS, M2_HPG), axis=2)
    idx = jnp.arange(CHUNK)
    causal = (idx[:, None] >= idx[None, :])[:, :, None, None]
    seg = cum[:, :, :, None] - cum[:, :, None, :]
    Lmat = jnp.exp(jnp.where(causal, seg, -jnp.inf))
    cb = jnp.einsum('bclgn,bcsgn->bclsg', Cc, Bc)
    y_diag = jnp.einsum('bclsgr,bcsgrp->bclgrp', cb[..., None] * Lmat, xdt)
    decay_states = jnp.exp(cum[:, :, -1:] - cum)
    states = jnp.einsum('bclgn,bclgrp->bcgrpn', Bc, xdt * decay_states[..., None])
    chunk_decay = jnp.exp(cum[:, :, -1])

    def step(S, inp):
        cd, st = inp
        return cd[..., None, None] * S + st, S

    S0 = jnp.zeros((bsz, M2_GROUPS, M2_HPG, M2_HEAD_DIM, M2_STATE), f32)
    _, S_prev = lax.scan(step, S0, (jnp.moveaxis(chunk_decay, 1, 0), jnp.moveaxis(states, 1, 0)))
    S_prev = jnp.moveaxis(S_prev, 0, 1)
    y_off = jnp.einsum('bclgn,bcgrpn->bclgrp', Cc, S_prev) * jnp.exp(cum)[..., None]
    y = (y_diag + y_off).reshape(bsz, L, M2_HEADS, M2_HEAD_DIM) + d_skip.astype(f32)[:, None] * x
    y = y.reshape(bsz, L, M2_INNER) * jax.nn.silu(z.astype(f32))
    y = rmsnorm_2(y.reshape(bsz, L, M2_GROUPS, M2_INNER // M2_GROUPS),
                norm_g.reshape(M2_GROUPS, M2_INNER // M2_GROUPS))
    return y.reshape(bsz, L, M2_INNER).astype(h.dtype) @ w_out

def sq_relu_mlp(h, w1, w2):
    return jnp.square(jax.nn.relu(h @ w1)) @ w2

def _inv_softplus_dt(key, shape):
    dt = jnp.exp(jax.random.uniform(key, shape, minval=math.log(1e-3), maxval=math.log(1e-1)))
    return dt + jnp.log(-jnp.expm1(-dt))

def second_inputs(seed: int = 0) -> dict:
    key = jax.random.key(seed)
    ks = jax.random.split(key, 32)
    nrm = jax.random.normal
    f32 = jnp.float32
    nA, nB, nC = N_LAYERS_A, N_LAYERS_B, N_LAYERS_C
    return {
        "x": nrm(ks[0], (BATCH, SEQ, D_MODEL), f32),
        "norm_mix_g": 1.0 + 0.02 * nrm(ks[1], (DEPTH, D_MODEL), f32),
        "norm_mlp_g": 1.0 + 0.02 * nrm(ks[2], (DEPTH, D_MODEL), f32),
        "mlp_w1": nrm(ks[3], (DEPTH, D_MODEL, D_FF), f32) * D_MODEL ** -0.5,
        "mlp_w2": nrm(ks[4], (DEPTH, D_FF, D_MODEL), f32) * D_FF ** -0.5,
        "gdn_w_in": nrm(ks[5], (nA, D_MODEL, GDN_IN), f32) * D_MODEL ** -0.5,
        "gdn_conv_w": nrm(ks[6], (nA, CONV_W, GDN_CONV_CH), f32) * CONV_W ** -0.5,
        "gdn_a_log": jnp.log(jax.random.uniform(ks[7], (nA, GDN_HEADS), minval=1.0, maxval=16.0)),
        "gdn_dt_bias": _inv_softplus_dt(ks[8], (nA, GDN_HEADS)),
        "gdn_o_norm_g": 1.0 + 0.02 * nrm(ks[9], (nA, GDN_DV), f32),
        "gdn_w_out": nrm(ks[10], (nA, GDN_V, D_MODEL), f32) * GDN_V ** -0.5,
        "s5_w_in": nrm(ks[11], (nB, D_MODEL, D_MODEL), f32) * D_MODEL ** -0.5,
        "s5_lam_re": -0.5 + 0.01 * nrm(ks[12], (nB, S5_GROUPS, S5_STATE), f32),
        "s5_lam_im": math.pi * jnp.arange(S5_STATE, dtype=f32) + 0.01 * nrm(ks[13], (nB, S5_GROUPS, S5_STATE), f32),
        "s5_log_dt": jax.random.uniform(ks[14], (nB, S5_GROUPS), minval=math.log(1e-3), maxval=math.log(1e-1)),
        "s5_b_re": nrm(ks[15], (nB, S5_GROUPS, S5_STATE, S5_GROUP), f32) * (2 * S5_GROUP) ** -0.5,
        "s5_b_im": nrm(ks[16], (nB, S5_GROUPS, S5_STATE, S5_GROUP), f32) * (2 * S5_GROUP) ** -0.5,
        "s5_c_re": nrm(ks[17], (nB, S5_GROUPS, S5_GROUP, S5_STATE), f32) * (2 * S5_STATE) ** -0.5 * 4.0,
        "s5_c_im": nrm(ks[18], (nB, S5_GROUPS, S5_GROUP, S5_STATE), f32) * (2 * S5_STATE) ** -0.5 * 4.0,
        "s5_d": nrm(ks[19], (nB, D_MODEL), f32),
        "s5_w_out": nrm(ks[20], (nB, D_MODEL, 2 * D_MODEL), f32) * D_MODEL ** -0.5,
        "m2_w_in": nrm(ks[21], (nC, D_MODEL, M2_IN), f32) * D_MODEL ** -0.5,
        "m2_conv_w": nrm(ks[22], (nC, CONV_W, M2_CONV_CH), f32) * CONV_W ** -0.5,
        "m2_conv_b": 0.02 * nrm(ks[23], (nC, M2_CONV_CH), f32),
        "m2_dt_bias": _inv_softplus_dt(ks[24], (nC, M2_HEADS)),
        "m2_a_log": jnp.log(jax.random.uniform(ks[25], (nC, M2_HEADS), minval=1.0, maxval=16.0)),
        "m2_d": 1.0 + 0.02 * nrm(ks[26], (nC, M2_HEADS), f32),
        "m2_norm_g": 1.0 + 0.02 * nrm(ks[27], (nC, M2_INNER), f32),
        "m2_w_out": nrm(ks[28], (nC, M2_INNER, D_MODEL), f32) * M2_INNER ** -0.5,
        "final_norm_g": 1.0 + 0.02 * nrm(ks[29], (D_MODEL,), f32),
    }

def second_block(x, norm_mix_g, norm_mlp_g, mlp_w1, mlp_w2,
              gdn_w_in, gdn_conv_w, gdn_a_log, gdn_dt_bias, gdn_o_norm_g, gdn_w_out,
              s5_w_in, s5_lam_re, s5_lam_im, s5_log_dt, s5_b_re, s5_b_im, s5_c_re, s5_c_im, s5_d, s5_w_out,
              m2_w_in, m2_conv_w, m2_conv_b, m2_dt_bias, m2_a_log, m2_d, m2_norm_g, m2_w_out,
              final_norm_g):
    h = x
    for i in range(DEPTH):
        kind, j = i % N_MIXERS, i // N_MIXERS
        hn = rmsnorm_2(h, norm_mix_g[i])
        if kind == 0:
            m = gated_deltanet(hn, gdn_w_in[j], gdn_conv_w[j], gdn_a_log[j], gdn_dt_bias[j],
                               gdn_o_norm_g[j], gdn_w_out[j])
        elif kind == 1:
            m = s5_mixer(hn, s5_w_in[j], s5_lam_re[j], s5_lam_im[j], s5_log_dt[j], s5_b_re[j],
                         s5_b_im[j], s5_c_re[j], s5_c_im[j], s5_d[j], s5_w_out[j])
        else:
            m = mamba2_mixer(hn, m2_w_in[j], m2_conv_w[j], m2_conv_b[j], m2_dt_bias[j], m2_a_log[j],
                             m2_d[j], m2_norm_g[j], m2_w_out[j])
        h = h + m.astype(h.dtype)
        h = h + sq_relu_mlp(rmsnorm_2(h, norm_mlp_g[i]), mlp_w1[i], mlp_w2[i]).astype(h.dtype)
    return rmsnorm_2(h, final_norm_g)


def setup_inputs(seed=0):
    out = dict(first_inputs(seed))
    for name, value in second_inputs(seed + 1).items():
        if name != "x":
            out[name + "_2"] = value
    return out


def reference(
    x, c, ctx, c_ctx, w_ada, b_ada, norm_pre_mix, norm_post_mix, norm_pre_ffn, norm_post_ffn,
    w_in, da_lambda_q1, da_lambda_k1, da_lambda_q2, da_lambda_k2, da_subln, hg_lower_bound,
    hg_norm, w_out, w_router, w_gate, w_up, w_down, norm_mix_g_2, norm_mlp_g_2, mlp_w1_2,
    mlp_w2_2, gdn_w_in_2, gdn_conv_w_2, gdn_a_log_2, gdn_dt_bias_2, gdn_o_norm_g_2, gdn_w_out_2,
    s5_w_in_2, s5_lam_re_2, s5_lam_im_2, s5_log_dt_2, s5_b_re_2, s5_b_im_2, s5_c_re_2,
    s5_c_im_2, s5_d_2, s5_w_out_2, m2_w_in_2, m2_conv_w_2, m2_conv_b_2, m2_dt_bias_2,
    m2_a_log_2, m2_d_2, m2_norm_g_2, m2_w_out_2, final_norm_g_2,
):
    x = first_block(
        x, c, ctx, c_ctx, w_ada, b_ada, norm_pre_mix, norm_post_mix, norm_pre_ffn,
        norm_post_ffn, w_in, da_lambda_q1, da_lambda_k1, da_lambda_q2, da_lambda_k2, da_subln,
        hg_lower_bound, hg_norm, w_out, w_router, w_gate, w_up, w_down,
    )
    return second_block(
        x, norm_mix_g_2, norm_mlp_g_2, mlp_w1_2, mlp_w2_2, gdn_w_in_2, gdn_conv_w_2,
        gdn_a_log_2, gdn_dt_bias_2, gdn_o_norm_g_2, gdn_w_out_2, s5_w_in_2, s5_lam_re_2,
        s5_lam_im_2, s5_log_dt_2, s5_b_re_2, s5_b_im_2, s5_c_re_2, s5_c_im_2, s5_d_2,
        s5_w_out_2, m2_w_in_2, m2_conv_w_2, m2_conv_b_2, m2_dt_bias_2, m2_a_log_2, m2_d_2,
        m2_norm_g_2, m2_w_out_2, final_norm_g_2,
    )


_drawn_inputs = setup_inputs


def setup_inputs(seed=0):
    import zlib

    import numpy as np

    out = dict(_drawn_inputs(seed))
    spreads = {}
    factors = {'norm_post_ffn': 3.047,
     'norm_mix_g_2': 3.326,
     'norm_mlp_g_2': 11.962,
     'gdn_o_norm_g_2': 18.12,
     'final_norm_g_2': 7.689}
    for name, (base, spread) in spreads.items():
        noise = np.random.default_rng([zlib.crc32(name.encode()), seed]).standard_normal(out[name].shape)
        drawn = base * np.exp(spread * noise) if base else spread * noise
        out[name] = jnp.asarray(drawn.astype(out[name].dtype))
    for name, factor in factors.items():
        out[name] = (out[name] * factor).astype(out[name].dtype)
    return out
```

```python
import math

import numpy as np
import concourse.bass as bass
import concourse.mybir as mybir

F32 = mybir.dt.float32
U8 = mybir.dt.uint8
ALU = mybir.AluOpType
ACT = mybir.ActivationFunctionType
AX = mybir.AxisListType

P = 128
D = 1024
KD = D // P
T = 512
TC = 256
TT = T // P
CT = TC // P
TA = T + TC
AT = TA // P
COLS = 512
GRID_W = 64
HEADS = 4
HD = 64
LAMBDA_INIT = 0.8 - 0.6 * math.exp(0.0)
EPS = 1e-6
EXPERTS = 16
CAP = 2 * T // EXPERTS
FF = 1024
D_FF = 4096
GH = 8
CONV_W = 4
LEVELS = [1, 2, 4, 8, 16, 32, 64]
KB = 1024

V_C, V_CCTX, V_PREMIX, V_PREFFN, V_MIX2, V_MLP2, V_BADA, V_LB = 0, 8, 16, 24, 32, 40, 48, 96
V_ROWS = 112
V_CONV = V_ROWS
V_ALL = V_ROWS + CONV_W * 24

S_ADA, S_IN, S_REST, S_OUT, S_EXP, S_GIN, S_GOUT, S_W1, S_W2, S_END = 0, 4, 12, 20, 22, 118, 126, 128, 136, 144
RING = 4


def shape_constants():
    i = np.arange(P)
    ident = np.eye(P, dtype=np.float32)
    rot = np.zeros((P, P), np.float32)
    for m in range(P):
        if m % 32 < 16:
            rot[m + 16, m] = -1.0
        else:
            rot[m - 16, m] = 1.0
    upto = (i[:, None] <= i[None, :]).astype(np.float32)
    after = (i[:, None] > i[None, :]).astype(np.float32)
    half = HD // 2
    inv_freq = (np.float32(1.0) / (np.float32(10000.0) ** (np.arange(0, half, 2, dtype=np.float32) / np.float32(half))))
    t = np.arange(T)
    ang_r = (t // GRID_W).astype(np.float32)[:, None] * inv_freq
    ang_c = (t % GRID_W).astype(np.float32)[:, None] * inv_freq
    ang = np.concatenate([ang_r, ang_r, ang_c, ang_c] * 2, axis=-1).T.astype(np.float32)
    slot = np.broadcast_to(np.arange(1, CAP + 1, dtype=np.float32), (P, CAP))
    slot_col = (i % CAP + 1).astype(np.float32)[:, None]
    table = np.concatenate([ident, rot, upto, after, np.cos(ang), np.sin(ang), slot, slot_col], axis=1)
    pairs = np.zeros((EXPERTS, EXPERTS // 2, P), np.float32)
    for e in range(EXPERTS):
        pairs[e, e // 2, (e % 2) * CAP:(e % 2 + 1) * CAP] = 1.0
    masks = []
    for L in LEVELS:
        b = i // L
        masks.append((b[:, None] % 2 == 0) & (b[None, :] == b[:, None] + 1))
    up = np.stack(masks, axis=1).astype(np.float32)
    low = np.stack([m.T for m in masks], axis=1).astype(np.float32)
    return {
        "k_table": np.ascontiguousarray(table.astype(np.float32)),
        "k_pairs": pairs.reshape(EXPERTS, -1),
        "k_masks": np.ascontiguousarray(np.concatenate([up, low], axis=1).reshape(P, -1)),
    }


class Shared:
    pass


TABLE = 4 * P + 2 * T + CAP + 1


def allocate(nc):
    base = (nc.sbuf_base + 31) // 32 * 32

    def place(name, shape, at, dtype=F32):
        return nc.alloc_sbuf_tensor_at(name, shape, dtype, offset=base + at)

    m = Shared()
    m.ring = place("ring", [P, RING, KD, COLS], 0)
    m.table = place("table", [P, TABLE], 64 * KB)
    m.ident = m.table[:, 0:P]
    m.rot = m.table[:, P:2 * P]
    m.upto = m.table[:, 2 * P:3 * P]
    m.after = m.table[:, 3 * P:4 * P]
    m.cos = m.table[:, 4 * P:4 * P + T]
    m.sin = m.table[:, 4 * P + T:4 * P + 2 * T]
    m.slot = m.table[:, 4 * P + 2 * T:4 * P + 2 * T + CAP]
    m.slot_col = m.table[:, TABLE - 1:TABLE]
    at = 64 * KB + (TABLE * 4 + 31) // 32 * 32
    m.masks = place("masks", [P, 2 * len(LEVELS), P], at, U8)
    at += 2 * len(LEVELS) * P
    m.vecs = place("vecs", [P, V_ALL], at)
    at += V_ALL * 4
    m.mod = place("mod", [P, 32, 2], at)
    at += 256
    m.a1 = place("a1", [P, KD, 2], at)
    m.a2 = place("a2", [P, KD], at + 64)
    m.silu_c = place("silu_c", [P, KD, 2], at + 96)
    m.ones = place("ones", [P, P], at + 160)
    at += 160 + 512
    gates = at
    m.gate1 = place("gate1", [P, D], at)
    m.gate2 = place("gate2", [P, D], at + 4 * KB)
    at += 8 * KB
    m.eps = place("eps", [P, 1], at)
    m.neg_lam = place("neg_lam", [P, 1], at + 32)
    at += 64
    work = (at + 31) // 32 * 32
    assert base + work + 122 * KB <= nc.sbuf_usable_end, (base + work, nc.sbuf_usable_end)

    def arena(name, shape, kb, dtype=F32):
        size = int(np.prod(shape[1:])) * (1 if dtype == U8 else 4)
        assert kb * KB + size <= 122 * KB + 0, name
        return place(name, shape, work + int(kb * KB), dtype)

    def scratch(name, shape, kb):
        return place(name, shape, kb * KB)

    def small(name, shape, at):
        return place(name, shape, gates + at)

    m.arena, m.scratch, m.small = arena, scratch, small
    m.bank = nc.alloc_psum_tensor("bank", [P, 8, COLS], F32)
    return m


def slab_source(I, s):
    def cut(w, n, r=0):
        return w[r * D:(r + 1) * D, n * COLS:(n + 1) * COLS].rearrange("(k p) n -> p k n", p=P)

    if s < S_IN:
        return cut(I["w_ada"][0], s)
    if s < S_REST:
        return cut(I["w_in"][0], s - S_IN)
    if s < S_OUT:
        return cut(I["w_ada"][0], s - S_REST + 4)
    if s < S_EXP:
        return cut(I["w_out"][0], s - S_OUT)
    if s < S_GIN:
        e, j = divmod(s - S_EXP, 6)
        return cut(I[("w_gate", "w_up", "w_down")[j // 2]][0, e], j % 2)
    if s < S_GOUT:
        return cut(I["gdn_w_in_2"][0], s - S_GIN)
    if s < S_W1:
        return cut(I["gdn_w_out_2"][0], s - S_GOUT)
    if s < S_W2:
        return cut(I["mlp_w1_2"][0], s - S_W1)
    r, n = divmod(s - S_W2, 2)
    return cut(I["mlp_w2_2"][0], n, r)


def stream(eng, m, I, first, last, freed=None):
    for s in range(first, last):
        if s >= RING:
            eng.wait_ge(*freed(s - RING))
        eng.dma_start(m.ring[:, s % RING], slab_source(I, s)).then_inc(m.slab_loaded[s % RING], 16)


def slab_wait(eng, m, s):
    eng.wait_ge(m.slab_loaded[s % RING], 16 * (s // RING + 1))


def chain(eng, sem):
    count = [0]

    def link(ins):
        count[0] += 1
        ins.then_inc(sem, 1)
        eng.wait_ge(sem, count[0])

    return link


def shift_scale(pe, m, out, w, j):
    for q in range(4):
        n = 4 * j + q
        for k in range(KD):
            mm = pe.matmul(out[:, 2 * n:2 * n + 2], w[:, k, q * P:(q + 1) * P], m.silu_c[:, k, :],
                           start=(k == 0), stop=(k == KD - 1))
    return mm


def add_bias(dve, m, src, half):
    b = m.vecs[:, V_BADA + 24 * half:V_BADA + 24 * half + 16].unsqueeze(2).to_broadcast([P, 16, 2])
    return dve.tensor_tensor(m.mod[:, 16 * half:16 * half + 16, :], src.rearrange("p (n s) -> p n s", s=2), b, ALU.add)


def modulation(nc, m, I):
    rows = m.arena("vec_rows", [V_ROWS, P], 72)
    conv_rows = m.arena("conv_rows", [CONV_W * 24, P], 72.5)
    sig = m.arena("sig_c", [P, 16], 73)
    sc = m.silu_c
    wide_masks = m.arena("wide_masks", [P, 2 * len(LEVELS), P], 88)
    x = m.arena("x_rows", [P, AT, D], 0)
    xn = m.xn1
    junk = m.arena("square1", [P, 2, D], 78)
    ss = m.arena("ss1", [P, AT], 86)
    sd = m.arena("sd1", [P, AT], 86.125)
    rstd = m.arena("rstd1", [P, AT], 86.25)
    bank = m.bank

    rows_in = m.sem("rows_in")
    table_in = m.sem("table_in")
    masks_in = m.sem("masks_in")
    x_in = [m.sem(f"x_in{t}") for t in range(2)]
    consts_set = m.sem("consts_set")
    vecs_turned = m.sem("vecs_turned")
    vecs_ready = m.sem("vecs_ready")
    sig_ready = m.sem("sig_ready")
    ada_done = m.sem("ada_done")
    silu_ready = m.sem("silu_ready")
    squares = m.sem("squares1")
    roots = m.sem("roots1")
    dve_step = m.sem("dve_step1")
    with nc.Block() as block:
        @block.sync
        def _(sp):
            spans = [("c", V_C), ("norm_pre_mix", V_PREMIX), ("norm_pre_ffn", V_PREFFN),
                     ("norm_mix_g_2", V_MIX2), ("norm_mlp_g_2", V_MLP2), ("b_ada", V_BADA)]
            for name, at in spans:
                src = I[name].rearrange("o (k p) -> (o k) p", p=P)
                sp.dma_start(rows[at:at + src.shape[0], :], src).then_inc(rows_in, 16)
            sp.dma_start(rows[V_CCTX:V_CCTX + KD, :], I["c_ctx"].rearrange("(k p) -> k p", p=P)).then_inc(rows_in, 16)
            sp.dma_start(rows[V_LB:V_ROWS, :], I["hg_lower_bound"].rearrange("l d (h p) -> (l d h) p", p=P)).then_inc(rows_in, 16)
            sp.dma_start(conv_rows[:, :], I["gdn_conv_w_2"][0].rearrange("j (k p) -> (j k) p", p=P)).then_inc(rows_in, 16)
            sp.dma_start(m.table[:, :], I["k_table"]).then_inc(table_in, 16)
            stream(sp, m, I, 0, 2)
            sp.dma_start(x[:, 0:CT, :], I["ctx"][0].rearrange("(t p) d -> p t d", p=P)).then_inc(x_in[0], 16)
            sp.dma_start(x[:, CT:AT, :], I["x"][0].rearrange("(t p) d -> p t d", p=P)).then_inc(x_in[1], 16)
            stream(sp, m, I, 2, 4)
            sp.dma_start(wide_masks[:, :, :], I["k_masks"].rearrange("p (n q) -> p n q", q=P)).then_inc(masks_in, 16)
            stream(sp, m, I, S_IN, S_IN + RING, lambda s: (ada_done, s + 1))

        @block.gpsimd
        def _(pool):
            pool.memset(m.eps[:, :], EPS).then_inc(consts_set, 1)
            pool.memset(m.ones[:, :], 1.0).then_inc(consts_set, 1)
            pool.wait_ge(masks_in, 16)
            pool.tensor_copy(m.masks[:, :, :], wide_masks[:, :, :])

        @block.tensor
        def _(pe):
            pe.wait_ge(rows_in, 9 * 16)
            pe.wait_ge(table_in, 16)
            pe.transpose(bank[:, 0, 0:V_ROWS], rows[:, :], m.ident[0:V_ROWS, 0:V_ROWS])
            pe.transpose(bank[:, 0, V_CONV:V_ALL], conv_rows[:, :], m.ident[0:CONV_W * 24, 0:CONV_W * 24]).then_inc(vecs_turned, 1)
            pe.wait_ge(silu_ready, 1)
            for s in range(S_IN):
                slab_wait(pe, m, s)
                shift_scale(pe, m, bank[:, 1, :], m.ring[:, s % RING], s).then_inc(ada_done, 1)

        @block.scalar
        def _(act):
            act.wait_ge(vecs_ready, 1)
            act.activation(sig[:, :], m.vecs[:, V_C:V_C + 16], ACT.Sigmoid).then_inc(sig_ready, 1)
            for t in range(AT):
                act.wait_ge(x_in[0 if t < CT else 1], 16)
                act.activation(junk[:, t % 2, :], x[:, t, :], ACT.Square, accum_out=ss[:, t:t + 1]).then_inc(squares, 1)
                if t >= 1:
                    act.wait_ge(squares, t)
            act.wait_ge(squares, AT)
            act.wait_ge(consts_set, 2)
            act.activation(sd[:, :], ss[:, :], ACT.Sqrt, bias=m.eps[:, :], scale=1.0 / D).then_inc(roots, 1)

        @block.vector
        def _(dve):
            link = chain(dve, dve_step)
            dve.wait_ge(vecs_turned, 1)
            dve.tensor_copy(m.vecs[:, :], bank[:, 0, 0:V_ALL]).then_inc(vecs_ready, 1)
            dve.wait_ge(sig_ready, 1)
            dve.wait_ge(vecs_ready, 1)
            dve.tensor_tensor(sc[:, :, :].rearrange("p k s -> p s k"),
                              m.vecs[:, V_C:V_C + 16].rearrange("p (s k) -> p s k", s=2),
                              sig[:, :].rearrange("p (s k) -> p s k", s=2), ALU.mult).then_inc(silu_ready, 1)
            dve.wait_ge(roots, 1)
            link(dve.reciprocal(rstd[:, :], sd[:, :]))
            for t in range(AT):
                dve.tensor_scalar(xn[:, t, :], x[:, t, :], rstd[:, t:t + 1], None, ALU.mult)
            dve.wait_ge(ada_done, S_IN)
            link(add_bias(dve, m, bank[:, 1, 0:32], 0))
            g = m.vecs[:, V_PREMIX:V_PREMIX + KD].unsqueeze(2).to_broadcast([P, KD, 2])
            dve.scalar_tensor_tensor(out=m.a1[:, :, :], in0=m.mod[:, 8:16, :], scalar=1.0, in1=g,
                                     op0=ALU.add, op1=ALU.mult)


def hidden_transposed(nc, m, I):
    bank, hT, xn = m.bank, m.hT, m.xn1
    turned = m.sem("h_turned")
    lat_out = m.sem("h_lat_out")
    ctx_out = m.sem("h_ctx_out")
    with nc.Block() as block:
        @block.tensor
        def _(pe):
            for k in range(KD):
                b = 2 * (k % 4)
                if k >= 4:
                    pe.wait_ge(lat_out, k - 3)
                    pe.wait_ge(ctx_out, k - 3)
                for t in range(AT):
                    o = bank[:, b + 1, t * P:(t + 1) * P] if t < CT else bank[:, b, (t - CT) * P:(t - CT + 1) * P]
                    mm = pe.transpose(o, xn[:, t, k * P:(k + 1) * P], m.ident)
                mm.then_inc(turned, 1)

        @block.vector
        def _(dve):
            for k in range(KD):
                dve.wait_ge(turned, k + 1)
                dve.tensor_scalar(hT[:, k, TC:TA], bank[:, 2 * (k % 4), :], m.a1[:, k, 0:1], m.mod[:, k, 0:1],
                                  ALU.mult, ALU.add).then_inc(lat_out, 1)

        @block.scalar
        def _(act):
            for k in range(KD):
                act.wait_ge(turned, k + 1)
                act.activation(hT[:, k, 0:TC], bank[:, 2 * (k % 4) + 1, 0:TC], ACT.Identity,
                               scale=m.a1[:, k, 1:2], bias=m.mod[:, k, 1:2]).then_inc(ctx_out, 1)


def project_in(nc, m, I):
    bank, hT = m.bank, m.hT
    units = []
    for s, (name, major, ctx) in enumerate((("qT", 1, 0), ("kT", 1, 1), ("v", 0, 1), ("zf", 1, 1), ("zb", 1, 1),
                                            ("hv", 0, 1), ("hqT", 1, 0), ("hg", 0, 0))):
        dst = m.proj[name]
        off = 0 if ctx else TC
        for j in range(4 if major else (AT if ctx else TT)):
            if major:
                units.append((s, 1, j, TC, T, dst[:, j, TC - off:TC - off + T]))
                if ctx:
                    units.append((s, 1, j, 0, TC, dst[:, j, 0:TC]))
            else:
                t0 = j * P + off
                units.append((s, 0, j, t0, COLS, dst[:, j, :]))
    product = m.sem("in_product")
    act_out = m.sem("in_act_out")
    dve_out = m.sem("in_dve_out")
    with nc.Block() as block:
        @block.sync
        def _(sp):
            stream(sp, m, I, S_IN + RING, S_REST + RING,
                   lambda s: (product, sum(u[0] <= s - S_IN for u in units)))

        @block.tensor
        def _(pe):
            for u, (s, major, j, t0, n, _) in enumerate(units):
                slab_wait(pe, m, S_IN + s)
                if u >= 8:
                    pe.wait_ge((act_out, dve_out)[u % 2], u // 2 - 3)
                w = m.ring[:, (S_IN + s) % RING]
                for k in range(KD):
                    if major:
                        mm = pe.matmul(bank[:, u % 8, 0:n], w[:, k, j * P:(j + 1) * P], hT[:, k, t0:t0 + n],
                                       start=(k == 0), stop=(k == KD - 1))
                    else:
                        mm = pe.matmul(bank[:, u % 8, :], hT[:, k, t0:t0 + P], w[:, k, :],
                                       start=(k == 0), stop=(k == KD - 1))
                mm.then_inc(product, 1)

        @block.scalar
        def _(act):
            for u in range(0, len(units), 2):
                act.wait_ge(product, u + 1)
                act.activation(units[u][5], bank[:, u % 8, 0:units[u][4]], ACT.Copy).then_inc(act_out, 1)

        @block.vector
        def _(dve):
            for u in range(1, len(units), 2):
                dve.wait_ge(product, u + 1)
                dve.tensor_copy(units[u][5], bank[:, u % 8, 0:units[u][4]]).then_inc(dve_out, 1)


def rotary(nc, m, I):
    bank, q, k = m.bank, m.proj["qT"], m.proj["kT"]
    tmp = m.arena("rot_sin", [P, 2, T], 92)
    lv = m.arena("lambda_vecs", [P, 4, HD], 96)
    lp = m.arena("lambda_prod", [P, 2, HD], 97)
    le = m.arena("lambda_exp", [P, 4], 97.5)
    units = [q[:, h, :] for h in range(HEADS)] + [k[:, h, TC:TA] for h in range(HEADS)]
    lam_in = m.sem("lam_in")
    turned = m.sem("rot_turned")
    by_cos = m.sem("rot_by_cos")
    by_sin = m.sem("rot_by_sin")
    lam_step = m.sem("lam_step")
    lam_exp = m.sem("lam_exp")
    with nc.Block() as block:
        @block.sync
        def _(sp):
            for n, name in enumerate(("q1", "k1", "q2", "k2")):
                sp.dma_start(lv[:, n, :], I["da_lambda_" + name].partition_broadcast(P)).then_inc(lam_in, 16)
            sp.wait_ge(lam_in, 64)

        @block.tensor
        def _(pe):
            for u, x in enumerate(units):
                pe.matmul(bank[:, u, :], m.rot, x, start=True, stop=True).then_inc(turned, 1)

        @block.gpsimd
        def _(pool):
            for u, x in enumerate(units):
                pool.wait_ge(turned, u + 1)
                pool.tensor_tensor(x, x, m.cos, ALU.mult).then_inc(by_cos, 1)

        @block.vector
        def _(dve):
            dve.wait_ge(lam_in, 64)
            pairs = lv[:, :, :].rearrange("p (a b) d -> p b a d", b=2)
            dve.tensor_tensor(lp[:, :, :], pairs[:, 0], pairs[:, 1], ALU.mult).then_inc(lam_step, 1)
            dve.wait_ge(lam_step, 1)
            dve.tensor_reduce(le[:, 0:2], lp[:, :, :], AX.X, ALU.add).then_inc(lam_step, 1)
            for u, x in enumerate(units):
                dve.wait_ge(turned, u + 1)
                dve.tensor_tensor(tmp[:, u % 2, :], bank[:, u, :], m.sin, ALU.mult).then_inc(by_sin, 1)
                dve.wait_ge(by_sin, u + 1)
                dve.wait_ge(by_cos, u + 1)
                dve.tensor_tensor(x, x, tmp[:, u % 2, :], ALU.add)
            dve.wait_ge(lam_exp, 1)
            dve.tensor_tensor(m.neg_lam[:, :], le[:, 3:4], le[:, 2:3], ALU.subtract).then_inc(lam_step, 1)
            dve.wait_ge(lam_step, 3)
            dve.tensor_scalar(m.neg_lam[:, :], m.neg_lam[:, :], -LAMBDA_INIT, None, ALU.add)

        @block.scalar
        def _(act):
            act.wait_ge(lam_step, 2)
            act.activation(le[:, 2:4], le[:, 0:2], ACT.Exp).then_inc(lam_exp, 1)


def attention(nc, m, I):
    bank, q, k, v, out = m.bank, m.proj["qT"], m.proj["kT"], m.proj["v"], m.mix_da
    HALF = TA // 2
    SCALE = HD ** -0.5
    units = [(h, t) for h in range(HEADS) for t in range(TT)]
    N = len(units)
    e = m.arena("exp_scores", [P, 2, 2, TA], 92)
    a2 = m.arena("second_softmax", [P, TA], 104)
    a = m.arena("softmax_diff", [P, 2, TA], 107)
    aT = m.arena("softmax_diff_T", [P, 2, TA], 113)
    st = m.arena("softmax_stats", [P, 5, N, 2], 119)
    mx, nb, rs, ri, rl = [st[:, i] for i in range(5)]
    scores_ready = m.sem("scores_ready")
    max_ready = m.sem("max_ready")
    bias_ready = m.sem("bias_ready")
    exp_ready = m.sem("exp_ready")
    inv_ready = m.sem("inv_ready")
    second_ready = m.sem("second_ready")
    diff_ready = m.sem("diff_ready")
    turned = m.sem("diff_turned")
    diffT_ready = m.sem("diffT_ready")
    pv_ready = m.sem("pv_ready")
    pv_out = m.sem("pv_out")
    with nc.Block() as block:
        @block.tensor
        def _(pe):
            for n in range(-1, N + 2):
                if n + 1 < N:
                    h, t = units[n + 1]
                    for i in range(2):
                        r = slice(HD * i, HD * (i + 1))
                        if n >= 0:
                            pe.wait_ge(exp_ready, 2 * n + 1 + i)
                        for half in range(2):
                            mm = pe.matmul(bank[:, 2 * i + half, 0:HALF], q[r, h, t * P:(t + 1) * P],
                                           k[r, h, half * HALF:(half + 1) * HALF], start=True, stop=True)
                        mm.then_inc(scores_ready, 1)
                if n >= 2:
                    w = n - 2
                    h = units[w][0]
                    pe.wait_ge(diffT_ready, w + 1)
                    if w >= 2:
                        pe.wait_ge(pv_out, w - 1)
                    for j in range(AT):
                        mm = pe.matmul(bank[:, 6 + w % 2, 0:P], aT[:, w % 2, j * P:(j + 1) * P], v[:, j, h * P:(h + 1) * P],
                                       start=(j == 0), stop=(j == AT - 1))
                    mm.then_inc(pv_ready, 1)
                if 1 <= n <= N:
                    w = n - 1
                    pe.wait_ge(diff_ready, w + 1)
                    for j in range(AT):
                        mm = pe.transpose(bank[:, 4 + j // 3, (j % 3) * P:(j % 3 + 1) * P], a[:, w % 2, j * P:(j + 1) * P], m.ident)
                    mm.then_inc(turned, 1)

        @block.scalar
        def _(act):
            def exp_of(n, i):
                act.wait_ge(bias_ready, 2 * n + i + 1)
                if n >= 2:
                    act.wait_ge(diff_ready, n - 1)
                act.activation(e[:, n % 2, i, :].rearrange("p (a n) -> p a n", a=2), bank[:, 2 * i:2 * i + 2, 0:HALF],
                               ACT.Exp, bias=nb[:, n, i:i + 1], scale=SCALE,
                               accum_out=rs[:, n, i:i + 1]).then_inc(exp_ready, 1)

            for n in range(-1, N + 2):
                if n + 1 < N:
                    exp_of(n + 1, 0)
                if 0 <= n < N:
                    act.wait_ge(inv_ready, 2 * n + 2)
                    if n >= 1:
                        act.wait_ge(diff_ready, n)
                    act.activation(a2[:, :], e[:, n % 2, 1, :], ACT.Copy, scale=rl[:, n, 1:2]).then_inc(second_ready, 1)
                if n + 1 < N:
                    exp_of(n + 1, 1)
                if n >= 2:
                    w = n - 2
                    h, t = units[w]
                    act.wait_ge(pv_ready, w + 1)
                    act.activation(out[:, t, h * P:(h + 1) * P], bank[:, 6 + w % 2, 0:P], ACT.Copy).then_inc(pv_out, 1)
                if 1 <= n <= N:
                    w = n - 1
                    act.wait_ge(turned, w + 1)
                    act.activation(aT[:, w % 2, :].rearrange("p (a n) -> p a n", a=2), bank[:, 4:6, 0:HALF],
                                   ACT.Copy).then_inc(diffT_ready, 1)

        @block.vector
        def _(dve):
            def bias_of(n, i):
                dve.wait_ge(scores_ready, 2 * n + i + 1)
                dve.tensor_reduce(mx[:, n, i:i + 1], bank[:, 2 * i:2 * i + 2, 0:HALF], AX.XY, ALU.max).then_inc(max_ready, 1)
                dve.wait_ge(max_ready, 2 * n + i + 1)
                dve.tensor_scalar(nb[:, n, i:i + 1], mx[:, n, i:i + 1], -SCALE, None, ALU.mult).then_inc(bias_ready, 1)

            for n in range(-1, N):
                if n + 1 < N:
                    bias_of(n + 1, 0)
                if n >= 0:
                    dve.wait_ge(exp_ready, 2 * n + 2)
                    dve.reciprocal(ri[:, n, :], rs[:, n, :]).then_inc(inv_ready, 1)
                    dve.wait_ge(inv_ready, 2 * n + 1)
                    dve.tensor_scalar(rl[:, n, 1:2], ri[:, n, 1:2], m.neg_lam[:, :], None, ALU.mult).then_inc(inv_ready, 1)
                if n + 1 < N:
                    bias_of(n + 1, 1)
                if n >= 0:
                    dve.wait_ge(second_ready, n + 1)
                    if n >= 2:
                        dve.wait_ge(turned, n - 1)
                    dve.scalar_tensor_tensor(out=a[:, n % 2, :], in0=e[:, n % 2, 0, :], scalar=ri[:, n, 0:1], in1=a2[:, :],
                                             op0=ALU.mult, op1=ALU.add).then_inc(diff_ready, 1)



def forget_gates(nc, m, I):
    z = (m.proj["zf"], m.proj["zb"])
    diff = m.arena("lb_diff", [P, 8], 0)
    lb = m.arena("lb", [P, 8], 0.125)
    rest = m.arena("lb_rest", [P, 8], 0.25)
    diff_ready = m.sem("lb_diff_ready")
    sig_ready = m.sem("forget_sig_ready")
    lb_step = m.sem("lb_step")
    scb = m.arena("silu_c_wide", [P, KD, P], 2)
    gb = m.arena("gate_bias", [P, 2, D], 6)
    gp = m.arena("gate_norm", [P, 2, D], 14)
    gates_in = m.sem("gates_in")
    wide_ready = m.sem("silu_wide_ready")
    rest_done = m.sem("rest_done")
    rest_step = m.sem("rest_step")
    bank = m.bank
    with nc.Block() as block:
        @block.sync
        def _(sp):
            for n, (at, name) in enumerate(((2, "norm_post_mix"), (5, "norm_post_ffn"))):
                sp.dma_start(gb[:, n, :], I["b_ada"][0:1, at * D:(at + 1) * D].partition_broadcast(P)).then_inc(gates_in, 16)
                sp.dma_start(gp[:, n, :], I[name][0:1, :].partition_broadcast(P)).then_inc(gates_in, 16)
            stream(sp, m, I, S_REST + RING, S_OUT + RING, lambda s: (rest_done, s - S_REST + 1))

        @block.tensor
        def _(pe):
            pe.wait_ge(wide_ready, 1)
            for s in range(S_REST, S_OUT):
                j = s - S_REST
                w = m.ring[:, s % RING]
                slab_wait(pe, m, s)
                if 2 <= j < 6:
                    mm = shift_scale(pe, m, bank[:, 4, :], w, j - 2)
                else:
                    for k in range(KD):
                        mm = pe.matmul(bank[:, j if j < 2 else j - 4, :], scb[:, k, :], w[:, k, :],
                                       start=(k == 0), stop=(k == KD - 1))
                mm.then_inc(rest_done, 1)

        @block.scalar
        def _(act):
            act.wait_ge(diff_ready, 1)
            act.activation(lb[:, :], diff[:, :], ACT.Sigmoid).then_inc(sig_ready, 1)
            for d in range(2):
                act.activation(z[d][:, :, :], z[d][:, :, :], ACT.Sigmoid).then_inc(sig_ready, 1)

        @block.vector
        def _(dve):
            dve.tensor_copy(scb[:, :, :], m.silu_c[:, :, 0:1].to_broadcast([P, KD, P])).then_inc(wide_ready, 1)
            dve.tensor_tensor(diff[:, :], m.vecs[:, V_LB:V_LB + 8], m.vecs[:, V_LB + 8:V_LB + 16], ALU.subtract).then_inc(diff_ready, 1)
            dve.wait_ge(sig_ready, 1)
            dve.tensor_scalar(rest[:, :], lb[:, :], -1.0, 1.0, ALU.mult, ALU.add).then_inc(lb_step, 1)
            dve.wait_ge(lb_step, 1)
            for d in range(2):
                dve.wait_ge(sig_ready, 2 + d)
                for h in range(HEADS):
                    n = HEADS * d + h
                    dve.tensor_scalar(z[d][:, h, :], z[d][:, h, :], rest[:, n:n + 1], lb[:, n:n + 1], ALU.mult, ALU.add)
            link = chain(dve, rest_step)
            dve.wait_ge(gates_in, 4 * 16)
            for half, (gate, b, slabs) in enumerate(((m.gate1, 0, 2), (m.gate2, 2, 8))):
                dve.wait_ge(rest_done, slabs)
                link(dve.tensor_tensor(gate[:, :], bank[:, b:b + 2, :].rearrange("p a n -> p (a n)"), gb[:, half, :], ALU.add))
                dve.tensor_tensor(gate[:, :], gate[:, :], gp[:, half, :], ALU.mult)
            link(add_bias(dve, m, bank[:, 4, 0:32], 1))
            dve.scalar_tensor_tensor(out=m.a2[:, :], in0=m.mod[:, 24:32, 0], scalar=1.0,
                                     in1=m.vecs[:, V_PREFFN:V_PREFFN + KD], op0=ALU.add, op1=ALU.mult)


def recurrence(nc, m, I, d):
    bank, q, hv = m.bank, m.proj["hqT"], m.proj["hv"]
    reach, other = (m.proj["zf"], m.proj["zb"]) if d == 0 else (m.proj["zb"], m.proj["zf"])
    k = m.arena(f"hk{d}", [P, HEADS, TA], 0)
    left = m.arena(f"left{d}", [P, HEADS, TA], 12)
    scores = m.scores
    X = m.arena(f"hX{d}", [P, 2, HEADS, T], 92)
    ends = m.arena(f"ends{d}", [P, HEADS, AT], 118.5 + d * 0.25)
    kT = m.arena(f"hkT{d}", [P, AT, COLS], 12)
    S = m.states[d]
    qh, kh = (1, 0) if d == 0 else (0, 1)
    nL = len(LEVELS)
    diag = 1 if d == 0 else 0
    rounds = diag + nL
    order = [0, 1, 2, 3, 4] if d == 0 else [1, 0, 5, 4, 3]

    def halves(t, L):
        return t[:, :, :].rearrange("p h t -> p (h t)").rearrange("p (n two l) -> p n two l", two=2, l=L)

    def lat_halves(t, L, at=0):
        return t[:, :, at:at + T].rearrange("p h (n two l) -> p h n two l", two=2, l=L)

    def total(t, L, half):
        at = L - 1 if d == 0 else 0
        v = halves(t, L)[:, :, half, at:at + 1]
        return v.to_broadcast([P, v.shape[1], L])

    def name(x):
        return m.sem(f"{x}{d}")

    k_ready, ones_set, diag_ready = name("hk_ready"), name("left_ones"), name("diag_ready")
    q_side, k_side, product, read_out = name("q_side"), name("k_side"), name("h_product"), name("h_read_out")
    left_grown, reach_grown, ends_kept = name("left_grown"), name("reach_grown"), name("ends_kept")
    k_last, k_turned, kT_ready, q_last = name("k_last"), name("k_turned"), name("hkT_ready"), name("q_last")
    gain, state = name("state_gain"), name("state_ready")
    with nc.Block() as block:
        @block.gpsimd
        def _(pool):
            pool.memset(left[:, :, :], 1.0).then_inc(ones_set, 1)
            pool.wait_ge(ones_set, 1)
            pool.wait_ge(k_ready, 1)
            for l, L in enumerate(LEVELS):
                r = l + diag
                if l >= 1:
                    pool.wait_ge(left_grown, l)
                if r >= 2:
                    pool.wait_ge(product, r - 1)
                x = X[:, r % 2].rearrange("p h (n two l) -> p h n two l", two=2, l=L)
                for h in range(HEADS):
                    ins = pool.tensor_tensor(x[:, h, :, kh, :], lat_halves(k, L, TC)[:, h, :, kh, :],
                                             lat_halves(left, L, TC)[:, h, :, kh, :], ALU.mult)
                ins.then_inc(k_side, 1)
                pool.wait_ge(k_side, l + 1)
                if l >= 1:
                    pool.wait_ge(reach_grown, l)
                pool.tensor_tensor(halves(left, L)[:, :, kh, :], halves(left, L)[:, :, kh, :],
                                   total(reach, L, qh), ALU.mult).then_inc(left_grown, 1)
            pool.wait_ge(left_grown, nL)
            pool.tensor_tensor(k[:, :, :], k[:, :, :], left[:, :, :], ALU.mult).then_inc(k_last, 1)

        @block.vector
        def _(dve):
            dve.tensor_scalar(k[:, :, :], reach[:, :, :], -1.0, 1.0, ALU.mult, ALU.add).then_inc(k_ready, 1)
            if diag:
                dve.wait_ge(k_ready, 1)
                dve.tensor_tensor(X[:, 0], k[:, :, TC:TA], other[:, :, TC:TA], ALU.subtract).then_inc(diag_ready, 1)
                dve.wait_ge(diag_ready, 1)
                dve.tensor_scalar(X[:, 0], X[:, 0], 1.0, None, ALU.add).then_inc(diag_ready, 1)

            def read(r):
                dve.wait_ge(product, r + 1)
                if r >= 1:
                    dve.wait_ge(read_out, r)
                for h in range(HEADS):
                    src = bank[:, 4 * (r % 2) + h, :].rearrange("p (c t) -> p c t", c=TT)
                    dst = scores[:, h, :].rearrange("p (c t) -> p c t", c=TT)
                    if r < diag:
                        ins = dve.tensor_tensor(dst, src, m.ident.unsqueeze(1).to_broadcast([P, TT, P]), ALU.mult)
                    else:
                        mask = m.masks[:, nL * d + r - diag, :].unsqueeze(1).to_broadcast([P, TT, P])
                        ins = dve.copy_predicated(dst, mask, src)
                ins.then_inc(read_out, 1)

            for l, L in enumerate(LEVELS):
                r = l + diag
                if l >= 1:
                    dve.wait_ge(reach_grown, l)
                if r >= 2:
                    dve.wait_ge(product, r - 1)
                x = X[:, r % 2].rearrange("p h (n two l) -> p h n two l", two=2, l=L)
                dve.tensor_tensor(x[:, :, :, qh, :], lat_halves(q, L)[:, :, :, qh, :],
                                  lat_halves(reach, L, TC)[:, :, :, qh, :], ALU.mult).then_inc(q_side, 1)
                if r >= 1:
                    read(r - 1)
                dve.wait_ge(left_grown, l + 1)
                dve.wait_ge(q_side, l + 1)
                dve.tensor_tensor(halves(reach, L)[:, :, qh, :], halves(reach, L)[:, :, qh, :],
                                  total(reach, L, kh), ALU.mult).then_inc(reach_grown, 1)
            read(rounds - 1)
            dve.wait_ge(reach_grown, nL)
            at = P - 1 if d == 0 else 0
            dve.tensor_copy(ends[:, :, :], reach[:, :, :].rearrange("p h (c t) -> p h c t", t=P)[:, :, :, at]).then_inc(ends_kept, 1)
            dve.wait_ge(ends_kept, 1)
            dve.tensor_tensor(reach[:, :, TC:TA], reach[:, :, TC:TA], q[:, :, :], ALU.mult).then_inc(q_last, 1)
            for j, c in enumerate(order):
                dve.wait_ge(gain, j + 1)
                if j == 0:
                    dve.tensor_copy(S[:, 0], bank[:, j, :]).then_inc(state, 1)
                    continue
                dve.wait_ge(state, j)
                for h in range(HEADS):
                    cut = slice(h * P, (h + 1) * P)
                    ins = dve.scalar_tensor_tensor(out=S[:, j, cut], in0=S[:, j - 1, cut], scalar=ends[:, h, c:c + 1],
                                                   in1=bank[:, j, cut], op0=ALU.mult, op1=ALU.add)
                ins.then_inc(state, 1)

        @block.tensor
        def _(pe):
            for r in range(rounds):
                if r < diag:
                    pe.wait_ge(diag_ready, 2)
                else:
                    pe.wait_ge(q_side, r - diag + 1)
                    pe.wait_ge(k_side, r - diag + 1)
                if r >= 2:
                    pe.wait_ge(read_out, r - 1)
                for h in range(HEADS):
                    for c in range(TT):
                        cut = slice(c * P, (c + 1) * P)
                        x = X[:, r % 2, h, cut]
                        mm = pe.matmul(bank[:, 4 * (r % 2) + h, cut], x, q[:, h, cut] if r < diag else x,
                                       start=True, stop=True)
                mm.then_inc(product, 1)
            pe.wait_ge(k_last, 1)
            pe.wait_ge(read_out, rounds)
            for c in range(AT):
                for h in range(HEADS):
                    mm = pe.transpose(bank[:, c, h * P:(h + 1) * P], k[:, h, c * P:(c + 1) * P], m.ident)
                mm.then_inc(k_turned, 1)
            for j, c in enumerate(order):
                pe.wait_ge(kT_ready, AT)
                for h in range(HEADS):
                    cut = slice(h * P, (h + 1) * P)
                    mm = pe.matmul(bank[:, j, cut], kT[:, c, cut], hv[:, c, cut], start=True, stop=True)
                mm.then_inc(gain, 1)

        @block.scalar
        def _(act):
            for c in range(AT):
                act.wait_ge(k_turned, c + 1)
                act.activation(kT[:, c, :], bank[:, c, :], ACT.Copy).then_inc(kT_ready, 1)


def recurrence_forward(nc, m, I):
    recurrence(nc, m, I, 0)


def recurrence_backward(nc, m, I):
    recurrence(nc, m, I, 1)


def mix_outputs(nc, m, I):
    bank, hv, hg, da = m.bank, m.proj["hv"], m.proj["hg"], m.mix_da
    nu = TT * HEADS
    sq = m.arena("mix_square", [P, 2, TT, COLS], 0)
    sg = m.arena("mix_sig", [P, TT, COLS], 16)
    o = m.arena("mix_o", [P, TT, COLS], 24)
    w = m.arena("mix_norm_w", [P, 2, P], 119.5)
    ss = m.arena("mix_ss", [P, 2, nu], 120.5)
    sd = m.arena("mix_sd", [P, 2, nu], 120.75)
    rstd = m.arena("mix_rstd", [P, 2, nu], 121)
    w_in = m.sem("mix_w_in")
    w_ready = m.sem("mix_w_ready")
    o_ready = m.sem("mix_o_ready")
    squared = m.sem("mix_squared")
    summed = m.sem("mix_summed")
    rooted = m.sem("mix_rooted")
    rstd_ready = m.sem("mix_rstd_ready")
    silu_ready = m.sem("mix_silu_ready")
    step = m.sem("mix_step")

    def heads(t):
        return t.rearrange("p t (h v) -> p (t h) v", v=P)

    def wide(v):
        return v.unsqueeze(2).to_broadcast([P, nu, P])

    with nc.Block() as block:
        @block.sync
        def _(sp):
            sp.dma_start(w[:, 0, :], I["da_subln"].partition_broadcast(P)).then_inc(w_in, 16)
            sp.dma_start(w[:, 1, :], I["hg_norm"].partition_broadcast(P)).then_inc(w_in, 16)
            sp.wait_ge(w_in, 32)

        @block.tensor
        def _(pe):
            for c in range(TT):
                lat = slice(TC + c * P, TC + (c + 1) * P)
                for h in range(HEADS):
                    cut = slice(h * P, (h + 1) * P)
                    pe.matmul(bank[:, c, cut], m.scores[:, h, c * P:(c + 1) * P], hv[:, CT + c, cut], start=True, stop=False)
                    pe.matmul(bank[:, c, cut], m.proj["zf"][:, h, lat], m.states[0][:, 1 + c, cut], start=False, stop=False)
                    mm = pe.matmul(bank[:, c, cut], m.proj["zb"][:, h, lat], m.states[1][:, 1 + TT - 1 - c, cut], start=False, stop=True)
            mm.then_inc(o_ready, 1)

        @block.scalar
        def _(act):
            act.activation(sq[:, 0], da[:, :, :], ACT.Square).then_inc(squared, 1)
            act.activation(sg[:, :, :], hg[:, :, :], ACT.Sigmoid).then_inc(silu_ready, 1)
            act.wait_ge(o_ready, 1)
            act.activation(sq[:, 1], bank[:, 0:TT, :], ACT.Square).then_inc(squared, 1)
            act.wait_ge(summed, 2)
            act.activation(sd[:, :, :], ss[:, :, :], ACT.Sqrt, bias=m.eps[:, :], scale=1.0 / P).then_inc(rooted, 1)

        @block.gpsimd
        def _(pool):
            pool.wait_ge(silu_ready, 1)
            pool.tensor_tensor(hg[:, :, :], hg[:, :, :], sg[:, :, :], ALU.mult).then_inc(silu_ready, 1)

        @block.vector
        def _(dve):
            link = chain(dve, step)
            dve.wait_ge(w_in, 32)
            dve.tensor_scalar(w[:, 0, :], w[:, 0, :], 1.0 - LAMBDA_INIT, None, ALU.mult).then_inc(w_ready, 1)
            for i in range(2):
                dve.wait_ge(squared, i + 1)
                dve.tensor_reduce(ss[:, i, :], heads(sq[:, i]), AX.X, ALU.add).then_inc(summed, 1)
            dve.wait_ge(rooted, 1)
            link(dve.reciprocal(rstd[:, :, :], sd[:, :, :]))
            dve.wait_ge(w_ready, 1)
            for src, dst, i in ((bank[:, 0:TT, :], o[:, :, :], 1), (da[:, :, :], da[:, :, :], 0)):
                link(dve.tensor_tensor(heads(dst), heads(src), wide(rstd[:, i, :]), ALU.mult))
                link(dve.tensor_tensor(heads(dst), heads(dst), w[:, i, :].unsqueeze(1).to_broadcast([P, nu, P]), ALU.mult))
            dve.wait_ge(silu_ready, 2)
            dve.tensor_tensor(hg[:, :, :], hg[:, :, :], o[:, :, :], ALU.mult)


def turn_features(nc, m, tag, sources, dst, scale=None, shift=None):
    bank = m.bank
    turned = m.sem(f"{tag}_turned")
    out = [m.sem(f"{tag}_out{i}") for i in range(2)]
    with nc.Block() as block:
        @block.tensor
        def _(pe):
            for k, tiles in enumerate(sources):
                for t, src in enumerate(tiles):
                    mm = pe.transpose(bank[:, k, t * P:(t + 1) * P], src, m.ident)
                mm.then_inc(turned, 1)

        @block.scalar
        def _(act):
            for k in range(0, KD, 2):
                act.wait_ge(turned, k + 1)
                if scale is None:
                    act.activation(dst[:, k, :], bank[:, k, :], ACT.Copy).then_inc(out[0], 1)
                elif shift is None:
                    act.activation(dst[:, k, :], bank[:, k, :], ACT.Copy, scale=scale[:, k:k + 1]).then_inc(out[0], 1)
                else:
                    act.activation(dst[:, k, :], bank[:, k, :], ACT.Identity, scale=scale[:, k:k + 1],
                                   bias=shift[:, k:k + 1]).then_inc(out[0], 1)

        @block.vector
        def _(dve):
            for k in range(1, KD, 2):
                dve.wait_ge(turned, k + 1)
                if scale is None:
                    dve.tensor_copy(dst[:, k, :], bank[:, k, :]).then_inc(out[1], 1)
                elif shift is None:
                    dve.tensor_scalar(dst[:, k, :], bank[:, k, :], scale[:, k:k + 1], None, ALU.mult).then_inc(out[1], 1)
                else:
                    dve.tensor_scalar(dst[:, k, :], bank[:, k, :], scale[:, k:k + 1], shift[:, k:k + 1],
                                      ALU.mult, ALU.add).then_inc(out[1], 1)


def rows_of(t, k):
    return [t[:, i, k * P:(k + 1) * P] for i in range(TT)]


def turn_mix(nc, m, I):
    turn_features(nc, m, "mixT", [rows_of(m.mix_da, k) for k in range(4)] + [rows_of(m.proj["hg"], k) for k in range(4)], m.mixT)


def residual(nc, m, I, tag, x, xn, products, loads, x_in=None, gate=None):
    bank = m.bank
    junk = m.arena(f"{tag}_square", [P, 2, D], 16)
    st = m.arena(f"{tag}_stats", [P, 6, TT], 121.5)
    add = m.arena(f"{tag}_add", [P, 2, D], 24)

    def name(n):
        return m.sem(f"{tag}_{n}")

    ready, squared, rooted, inverse, scaled, added = map(name, ("ready", "squared", "rooted", "inverse", "scaled", "added"))
    squared2, rooted2, inverse2 = map(name, ("squared2", "rooted2", "inverse2"))
    with nc.Block() as block:
        @block.sync
        def _(sp):
            loads(sp, ready)

        @block.tensor
        def _(pe):
            products(pe, ready)

        @block.scalar
        def _(act):
            def norm(t, src, row, squares, roots):
                act.activation(junk[:, t % 2, :], src, ACT.Square, accum_out=st[:, row, t:t + 1]).then_inc(squares, 1)
                act.wait_ge(squares, t + 1)
                act.activation(st[:, row + 1, t:t + 1], st[:, row, t:t + 1], ACT.Sqrt, bias=m.eps[:, :],
                               scale=1.0 / D).then_inc(roots, 1)

            for t in range(TT):
                if gate is not None:
                    act.wait_ge(ready, t + 1)
                    norm(t, bank[:, 2 * t:2 * t + 2, :].rearrange("p a n -> p (a n)"), 0, squared, rooted)
                if t >= 1:
                    act.wait_ge(added, t)
                    norm(t - 1, x[:, t - 1, :], 3, squared2, rooted2)
            act.wait_ge(added, TT)
            norm(TT - 1, x[:, TT - 1, :], 3, squared2, rooted2)

        @block.vector
        def _(dve):
            def normal(t):
                dve.wait_ge(rooted2, t + 1)
                dve.reciprocal(st[:, 5, t:t + 1], st[:, 4, t:t + 1]).then_inc(inverse2, 1)
                dve.wait_ge(inverse2, t + 1)
                dve.tensor_scalar(xn[:, t, :], x[:, t, :], st[:, 5, t:t + 1], None, ALU.mult)

            if x_in is not None:
                dve.wait_ge(*x_in)
            for t in range(TT):
                src = bank[:, 2 * t:2 * t + 2, :].rearrange("p a n -> p (a n)")
                dve.wait_ge(ready, t + 1)
                if gate is not None:
                    dve.wait_ge(rooted, t + 1)
                    dve.reciprocal(st[:, 2, t:t + 1], st[:, 1, t:t + 1]).then_inc(inverse, 1)
                    dve.wait_ge(inverse, t + 1)
                    dve.scalar_tensor_tensor(out=add[:, t % 2, :], in0=src, scalar=st[:, 2, t:t + 1], in1=gate[:, :],
                                             op0=ALU.mult, op1=ALU.mult).then_inc(scaled, 1)
                    dve.wait_ge(scaled, t + 1)
                    src = add[:, t % 2, :]
                dve.tensor_tensor(x[:, t, :], x[:, t, :], src, ALU.add).then_inc(added, 1)
                if t >= 1:
                    normal(t - 1)
            normal(TT - 1)


def project_out(nc, m, I):
    x_in = m.sem("x_again")

    def products(pe, ready):
        for t in range(TT):
            for n in range(2):
                slab_wait(pe, m, S_OUT + n)
                for k in range(KD):
                    mm = pe.matmul(m.bank[:, 2 * t + n, :], m.mixT[:, k, t * P:(t + 1) * P], m.ring[:, (S_OUT + n) % RING, k, :],
                                   start=(k == 0), stop=(k == KD - 1))
            mm.then_inc(ready, 1)

    def loads(sp, ready):
        sp.dma_start(m.x[:, :, :], I["x"][0].rearrange("(t p) d -> p t d", p=P)).then_inc(x_in, 16)
        stream(sp, m, I, S_OUT + RING, S_EXP + RING, lambda s: (ready, TT))

    residual(nc, m, I, "out1", m.x, m.xn2, products, loads, (x_in, 16), m.gate1)


def turn_ffn(nc, m, I):
    turn_features(nc, m, "h2T", [rows_of(m.xn2, k) for k in range(KD)], m.h2T, m.a2[:, :], m.mod[:, 16:24, 0])


def route(nc, m, I):
    bank = m.bank
    E = EXPERTS
    wr = m.arena("w_router", [P, KD, E], 80)
    lg = m.arena("logits", [P, TT, E], 81)
    ex = m.arena("logit_exp", [P, TT, E], 81.5)
    aff = m.arena("affinity", [P, TT, E], 82)
    st = m.arena("router_stats", [P, 3, TT], 82.5)
    pairs = m.arena("pair_rows", [E, EXPERTS // 2, P], 112)
    affT = m.arena("affT", [E, T], 116)
    left = m.arena("aff_left", [E, T], 118)
    chosen = m.arena("chosen", [E, T], 120)
    place = m.arena("place", [E, T], 83)
    ones = m.arena("ones_row", [E, T], 85)
    top = m.arena("top8", [E, 8], 87)
    posT = m.arena("placeT", [P, TT, E], 87.5)
    wide = m.arena("aff_wide", [P, 2, T], 88)

    w_in = m.sem("router_in")
    logits = m.sem("logits_ready")
    expd = m.sem("logit_exp_ready")
    step = m.sem("router_step")
    aff_ready = m.sem("aff_ready")
    aff_turned = m.sem("aff_turned")
    affT_ready = m.sem("affT_ready")
    place_ready = m.sem("place_ready")
    place_turned = m.sem("place_turned")
    pair_rows = m.sem("pair_rows_ready")
    wide_ready = m.sem("aff_wide_ready")
    spread_ready = m.sem("spread_ready")
    logit_less = m.sem("logit_less_max")
    with nc.Block() as block:
        @block.sync
        def _(sp):
            sp.dma_start(wr[:, :, :], I["w_router"][0].rearrange("(k p) e -> p k e", p=P)).then_inc(w_in, 16)
            sp.dma_start(pairs[:, :, :], I["k_pairs"].rearrange("e (n p) -> e n p", p=P)).then_inc(w_in, 16)
            sp.wait_ge(w_in, 32)

        @block.tensor
        def _(pe):
            pe.wait_ge(w_in, 32)
            for t in range(TT):
                for k in range(KD):
                    mm = pe.matmul(bank[:, 0, t * E:(t + 1) * E], m.h2T[:, k, t * P:(t + 1) * P], wr[:, k, :],
                                   start=(k == 0), stop=(k == KD - 1))
            mm.then_inc(logits, 1)
            pe.wait_ge(aff_ready, 1)
            for t in range(TT):
                mm = pe.transpose(bank[0:E, 1, t * P:(t + 1) * P], aff[:, t, :], m.ident)
            mm.then_inc(aff_turned, 1)
            pe.wait_ge(place_ready, 1)
            for t in range(TT):
                mm = pe.transpose(bank[:, 2, t * E:(t + 1) * E], place[:, t * P:(t + 1) * P], m.ident[0:E, 0:E])
            mm.then_inc(place_turned, 1)
            for n in range(EXPERTS // 2):
                b = 4 + 2 * (n % 2)
                if n >= 2:
                    pe.wait_ge(spread_ready, n - 1)
                pe.matmul(bank[:, b, :], pairs[:, n, :], place[:, :], start=True, stop=True)
                pe.matmul(bank[:, b + 1, :], pairs[:, n, :], affT[:, :], start=True, stop=True).then_inc(pair_rows, 1)

        @block.scalar
        def _(act):
            act.wait_ge(logit_less, 1)
            act.activation(ex[:, :, :], lg[:, :, :], ACT.Exp).then_inc(expd, 1)
            for n in range(EXPERTS // 2):
                act.wait_ge(pair_rows, n + 1)
                if n >= 2:
                    act.wait_ge(spread_ready, n - 1)
                act.activation(wide[:, n % 2, :], bank[:, 5 + 2 * (n % 2), :], ACT.Copy).then_inc(wide_ready, 1)

        @block.vector
        def _(dve):
            link = chain(dve, step)
            dve.memset(ones[:, :], 1.0)
            dve.wait_ge(logits, 1)
            raw = bank[:, 0, 0:TT * E].rearrange("p (t e) -> p t e", e=E)
            link(dve.tensor_reduce(st[:, 0, :], raw, AX.X, ALU.max))
            dve.tensor_tensor(lg[:, :, :], raw, st[:, 0, :].unsqueeze(2).to_broadcast([P, TT, E]), ALU.subtract).then_inc(logit_less, 1)
            dve.wait_ge(expd, 1)
            link(dve.tensor_reduce(st[:, 1, :], ex[:, :, :], AX.X, ALU.add))
            link(dve.reciprocal(st[:, 2, :], st[:, 1, :]))
            dve.tensor_tensor(aff[:, :, :], ex[:, :, :], st[:, 2, :].unsqueeze(2).to_broadcast([P, TT, E]), ALU.mult).then_inc(aff_ready, 1)
            dve.wait_ge(aff_turned, 1)
            dve.tensor_copy(affT[:, :], bank[0:E, 1, :]).then_inc(affT_ready, 1)
            link(dve.tensor_copy(left[:, :], bank[0:E, 1, :]))
            for _ in range(CAP // 8):
                link(dve.max(top[:, :], left[:, :]))
                link(dve.match_replace(left[:, :], top[:, :], left[:, :], -1.0))
            link(dve.tensor_scalar(chosen[:, :], left[:, :], 0.0, None, ALU.is_lt))
            link(dve.tensor_tensor_scan(place[:, :], ones[:, :], chosen[:, :], 0.0, ALU.mult, ALU.add))
            dve.tensor_tensor(place[:, :], place[:, :], chosen[:, :], ALU.mult).then_inc(place_ready, 1)
            dve.wait_ge(place_turned, 1)
            link(dve.tensor_copy(posT[:, :, :], bank[:, 2, 0:TT * E].rearrange("p (t e) -> p t e", e=E)))
            for t in range(TT):
                dve.tensor_tensor(m.onehot[:, t, :].rearrange("p (e c) -> p e c", c=CAP),
                                  m.slot.unsqueeze(1).to_broadcast([P, E, CAP]),
                                  posT[:, t, :].unsqueeze(2).to_broadcast([P, E, CAP]), ALU.is_equal)
            for n in range(EXPERTS // 2):
                dve.wait_ge(wide_ready, n + 1)
                dve.scalar_tensor_tensor(out=m.spread[:, n, :], in0=bank[:, 4 + 2 * (n % 2), :], scalar=m.slot_col,
                                         in1=wide[:, n % 2, :], op0=ALU.is_equal, op1=ALU.mult).then_inc(spread_ready, 1)


def experts(nc, m, I):
    bank = m.bank
    H = CAP
    PAIRS = EXPERTS // 2
    xin = m.arena("xinT", [P, KD, P], 16)
    sig = m.arena("gate_sig", [P, COLS], 20)
    hid = m.arena("expert_hidden", [P, COLS], 22)
    hidT = m.arena("expert_hiddenT", [P, 4, P], 24)

    gathered = m.sem("gathered")
    xin_a = m.sem("xin_by_act")
    xin_v = m.sem("xin_by_dve")
    g_ready = m.sem("expert_gate")
    u_ready = m.sem("expert_up")
    y_ready = m.sem("expert_down")
    sig_ready = m.sem("expert_sig")
    silu_ready = m.sem("expert_silu")
    hid_ready = m.sem("expert_hid")
    hid_turned = m.sem("expert_hid_turned")
    hidT_ready = m.sem("expert_hidT")
    y_free_a = m.sem("y_free_by_act")
    y_free_v = m.sem("y_free_by_dve")

    def landed(pe, i, j):
        s = S_EXP + j
        pe.wait_ge(m.slab_loaded[s % RING], i * (16 * 12 // RING) + 16 * (s // RING + 1))

    with nc.Block() as block:
        @block.sync
        def _(sp):
            done = (g_ready, u_ready, y_ready)
            with sp.Fori(0, PAIRS - 1) as i:
                for j in range(12):
                    sp.wait_ge(done[j % 6 // 2], i * 2 + (j // 6 + 1))
                    s = S_EXP + RING + j
                    e, q = divmod(RING + j, 6)
                    w = I[("w_gate", "w_up", "w_down")[q // 2]][0, bass.ds(i * 2 + e, 1), :, (q % 2) * COLS:(q % 2 + 1) * COLS]
                    sp.dma_start(m.ring[:, s % RING], w.rearrange("o (k p) n -> p (o k) n", p=P)).then_inc(m.slab_loaded[s % RING], 16)
            stream(sp, m, I, S_GIN - 12 + RING, S_GIN + RING,
                   lambda s: (done[(s - S_EXP) % 6 // 2], (s - S_EXP) // 6 + 1))

        @block.tensor
        def _(pe):
            def gather(i):
                for k in range(KD):
                    for t in range(TT):
                        mm = pe.matmul(bank[:, k // 4, (k % 4) * P:(k % 4 + 1) * P], m.xn2[:, t, k * P:(k + 1) * P],
                                       m.onehot[:, t, bass.ds(i * P, P)], start=(t == 0), stop=(t == TT - 1))
                mm.then_inc(gathered, 1)

            def pair(i, last):
                pe.wait_ge(xin_a, i + 1)
                pe.wait_ge(xin_v, i + 1)
                for r in range(2):
                    for q, (b, ready) in enumerate(((2, g_ready), (3, u_ready))):
                        landed(pe, i, 6 * r + 2 * q)
                        landed(pe, i, 6 * r + 2 * q + 1)
                        for k in range(KD):
                            for half in range(2):
                                w = m.ring[:, (S_EXP + 6 * r + 2 * q + half) % RING]
                                mm = pe.matmul(bank[half * H:(half + 1) * H, b, :], xin[:, k, r * H:(r + 1) * H], w[:, k, :],
                                               start=(k == 0), stop=(k == KD - 1), skip_group_check=True)
                        mm.then_inc(ready, 1)
                    if r == 1 and not last:
                        gather(i + 1)
                    pe.wait_ge(hid_ready, i * 2 + (r + 1))
                    for c in range(4):
                        mm = pe.transpose(bank[:, 6, c * P:(c + 1) * P], hid[:, c * P:(c + 1) * P], m.ident)
                    mm.then_inc(hid_turned, 1)
                    pe.wait_ge(hidT_ready, i * 2 + (r + 1))
                    landed(pe, i, 6 * r + 4)
                    landed(pe, i, 6 * r + 5)
                    pe.wait_ge(y_free_a, i * 2 + (r + 1))
                    pe.wait_ge(y_free_v, i * 2 + (r + 1))
                    for f in range(KD):
                        for half in range(2):
                            w = m.ring[:, (S_EXP + 6 * r + 4 + half) % RING]
                            mm = pe.matmul(bank[half * H:(half + 1) * H, 7, :], hidT[:, f % 4, (f // 4) * H:(f // 4 + 1) * H], w[:, f, :],
                                           start=(f == 0), stop=(f == KD - 1), skip_group_check=True)
                    mm.then_inc(y_ready, 1)

            gather(0)
            with pe.Fori(0, PAIRS - 1) as i:
                pair(i, False)
            pair(PAIRS - 1, True)

        @block.scalar
        def _(act):
            def take_in(i):
                act.wait_ge(gathered, i + 1)
                for k in range(4):
                    ins = act.activation(xin[:, k, :], bank[:, 0, k * P:(k + 1) * P], ACT.Identity,
                                         scale=m.a2[:, k:k + 1], bias=m.mod[:, 16 + k, 0:1])
                ins.then_inc(xin_a, 1)

            def pair(i, last):
                for r in range(2):
                    act.wait_ge(g_ready, i * 2 + (r + 1))
                    act.activation(sig[:, :], bank[:, 2, :], ACT.Sigmoid).then_inc(sig_ready, 1)
                    if r == 1 and not last:
                        take_in(i + 1)
                    act.wait_ge(hid_turned, i * 2 + (r + 1))
                    act.activation(hidT[:, :, :], bank[:, 6, :].rearrange("p (c n) -> p c n", c=4), ACT.Copy).then_inc(hidT_ready, 1)
                    act.wait_ge(y_ready, i * 2 + (r + 1))
                    act.activation(m.y[r * H:(r + 1) * H, bass.ds(i, 1), 0:COLS], bank[0:H, 7:8, :], ACT.Copy).then_inc(y_free_a, 1)

            act.sem_inc(y_free_a, 1)
            take_in(0)
            with act.Fori(0, PAIRS - 1) as i:
                pair(i, False)
            pair(PAIRS - 1, True)

        @block.vector
        def _(dve):
            def take_in(i):
                dve.wait_ge(gathered, i + 1)
                for k in range(4, KD):
                    ins = dve.tensor_scalar(xin[:, k, :], bank[:, 1, (k - 4) * P:(k - 3) * P], m.a2[:, k:k + 1],
                                            m.mod[:, 16 + k, 0:1], ALU.mult, ALU.add)
                ins.then_inc(xin_v, 1)

            def pair(i, last):
                for r in range(2):
                    dve.wait_ge(sig_ready, i * 2 + (r + 1))
                    dve.tensor_tensor(sig[:, :], sig[:, :], bank[:, 2, :], ALU.mult).then_inc(silu_ready, 1)
                    dve.wait_ge(silu_ready, i * 2 + (r + 1))
                    dve.wait_ge(u_ready, i * 2 + (r + 1))
                    dve.tensor_tensor(hid[:, :], sig[:, :], bank[:, 3, :], ALU.mult).then_inc(hid_ready, 1)
                    if r == 1 and not last:
                        take_in(i + 1)
                    dve.wait_ge(y_ready, i * 2 + (r + 1))
                    dve.tensor_copy(m.y[r * H:(r + 1) * H, bass.ds(i, 1), COLS:D], bank[H:P, 7:8, :]).then_inc(y_free_v, 1)

            dve.sem_inc(y_free_v, 1)
            take_in(0)
            with dve.Fori(0, PAIRS - 1) as i:
                pair(i, False)
            pair(PAIRS - 1, True)


def scatter(nc, m, I):
    def products(pe, ready):
        for t in range(TT):
            for n in range(2):
                for i in range(EXPERTS // 2):
                    mm = pe.matmul(m.bank[:, 2 * t + n, :], m.spread[:, i, t * P:(t + 1) * P], m.y[:, i, n * COLS:(n + 1) * COLS],
                                   start=(i == 0), stop=(i == EXPERTS // 2 - 1))
            mm.then_inc(ready, 1)

    residual(nc, m, I, "out2", m.x, m.xn3, products, lambda sp, ready: None, None, m.gate2)


def turn_gdn(nc, m, I):
    turn_features(nc, m, "h3T", [rows_of(m.xn3, k) for k in range(KD)], m.h3T, m.vecs[:, V_MIX2:V_MIX2 + KD])


def gdn_project(nc, m, I):
    bank, h = m.bank, m.h3T
    QKV = 3 * GH
    acc = m.arena("conv_acc", [P, 2, T], 112)
    sig = m.arena("conv_sig", [P, 2, T], 116)
    wab = m.arena("w_rates", [P, KD, 2 * GH], 120)
    NU = QKV + 2 * TT
    w_in = m.sem("w_rates_in")
    spilled = m.sem("x3_spilled")
    product = m.sem("gdn_product")
    conv = m.sem("gdn_conv")
    sig_ready = m.sem("gdn_conv_sig")
    stored = m.sem("gdn_conv_stored")
    gate_out = m.sem("gdn_gate_out")
    with nc.Block() as block:
        @block.sync
        def _(sp):
            sp.dma_start(wab[:, :, :], I["gdn_w_in_2"][0, :, 8 * COLS:8 * COLS + 2 * GH].rearrange("(k p) n -> p k n", p=P)).then_inc(w_in, 16)
            sp.dma_start(m.x_spill, m.x[:, :, :]).then_inc(spilled, 16)
            stream(sp, m, I, S_GIN + RING, S_GIN + 8, lambda s: (product, 4 * (s - S_GIN + 1)))
            stream(sp, m, I, S_GOUT, S_GOUT + 2, lambda s: (product, 4 * (s - S_GIN + 1)))
            sp.wait_ge(spilled, 16)

        @block.tensor
        def _(pe):
            for u in range(NU):
                s = S_GIN + u // 4
                w = m.ring[:, s % RING]
                slab_wait(pe, m, s)
                if 8 <= u < QKV + 8:
                    pe.wait_ge(conv, 4 * (u - 7))
                for k in range(KD):
                    if u < QKV:
                        mm = pe.matmul(bank[:, u % 8, :], w[:, k, (u % 4) * P:(u % 4 + 1) * P], h[:, k, :],
                                       start=(k == 0), stop=(k == KD - 1))
                    else:
                        mm = pe.matmul(bank[:, u % 8, :], h[:, k, (u % 4) * P:(u % 4 + 1) * P], w[:, k, :],
                                       start=(k == 0), stop=(k == KD - 1))
                mm.then_inc(product, 1)
            pe.wait_ge(w_in, 16)
            pe.wait_ge(gate_out, 1)
            for t in range(TT):
                for k in range(KD):
                    mm = pe.matmul(bank[:, 0, t * 2 * GH:(t + 1) * 2 * GH], h[:, k, t * P:(t + 1) * P], wab[:, k, :],
                                   start=(k == 0), stop=(k == KD - 1))
            mm.then_inc(product, 1)

        @block.vector
        def _(dve):
            for u in range(QKV):
                x, a = bank[:, u % 8, :], acc[:, u % 2, :]
                dve.wait_ge(product, u + 1)
                if u >= 2:
                    dve.wait_ge(stored, u - 1)

                def tap(j):
                    return m.vecs[:, V_CONV + j * QKV + u:V_CONV + j * QKV + u + 1]

                dve.tensor_scalar(a, x, tap(CONV_W - 1), None, ALU.mult).then_inc(conv, 1)
                for d in range(1, CONV_W):
                    dve.wait_ge(conv, 4 * u + d)
                    dve.scalar_tensor_tensor(out=a[:, d:], in0=x[:, :T - d], scalar=tap(CONV_W - 1 - d), in1=a[:, d:],
                                             op0=ALU.mult, op1=ALU.add).then_inc(conv, 1)

        @block.scalar
        def _(act):
            for u in range(QKV):
                act.wait_ge(conv, 4 * u + 4)
                if u >= 2:
                    act.wait_ge(stored, u - 1)
                act.activation(sig[:, u % 2, :], acc[:, u % 2, :], ACT.Sigmoid).then_inc(sig_ready, 1)
            for u in range(QKV, NU):
                act.wait_ge(product, u + 1)
                n, t = divmod(u - QKV, TT)
                act.activation(m.gate[:, t, n * COLS:(n + 1) * COLS], bank[:, u % 8, :], ACT.Copy).then_inc(gate_out, 1)
            act.wait_ge(product, NU + 1)
            act.activation(m.rates[:, :, :], bank[:, 0, 0:TT * 2 * GH].rearrange("p (t n) -> p t n", t=TT), ACT.Copy).then_inc(gate_out, 1)

        @block.gpsimd
        def _(pool):
            for u in range(QKV):
                pool.wait_ge(sig_ready, u + 1)
                pool.tensor_tensor(m.qkvT[:, u, :], acc[:, u % 2, :], sig[:, u % 2, :], ALU.mult).then_inc(stored, 1)


def gdn_norms(nc, m, I):
    bank = m.bank
    sq = m.arena("gdn_square", [P, 2, T], 112)
    sd = m.arena("gdn_length", [P, 2, T], 116)
    rb = m.arena("rate_bias", [P, 2, GH], 120)
    tm = m.arena("rate_tmp", [P, 4, TT, GH], 120.125)
    NQ = 2 * GH
    order = list(range(GH, 2 * GH)) + list(range(GH))
    rb_in = m.sem("rate_bias_in")
    squared = m.sem("gdn_squared")
    sums = m.sem("gdn_sums")
    rooted = m.sem("gdn_rooted")
    normed = m.sem("gdn_normed")
    turned = m.sem("gdn_turned")
    tok_out = m.sem("gdn_tok_out")
    step = m.sem("rate_step")
    act_step = m.sem("rate_act_step")
    g_ready = m.sem("g_ready")
    g_sums = m.sem("g_sums")
    g_exp = m.sem("g_exp")
    abs_ready = m.sem("rate_abs")
    with nc.Block() as block:
        @block.sync
        def _(sp):
            sp.dma_start(rb[:, 0, :], I["gdn_a_log_2"].partition_broadcast(P)).then_inc(rb_in, 16)
            sp.dma_start(rb[:, 1, :], I["gdn_dt_bias_2"].partition_broadcast(P)).then_inc(rb_in, 16)
            sp.wait_ge(rb_in, 32)

        @block.scalar
        def _(act):
            a, b = m.rates[:, :, 0:GH], m.rates[:, :, GH:2 * GH]
            act.wait_ge(rb_in, 32)
            act.activation(rb[:, 0, :], rb[:, 0, :], ACT.Exp).then_inc(act_step, 1)
            act.activation(m.beta[:, :, :], b, ACT.Sigmoid).then_inc(act_step, 1)
            act.wait_ge(abs_ready, 1)
            act.activation(tm[:, 2], tm[:, 1], ACT.Exp, scale=-1.0).then_inc(act_step, 1)
            act.wait_ge(act_step, 3)
            act.activation(tm[:, 3], tm[:, 2], ACT.Ln, bias=m.ones[:, 0:1]).then_inc(act_step, 1)
            act.wait_ge(g_sums, TT)
            act.activation(m.decays[:, :, :, :], bank[:, 7, 0:3 * TT * GH].rearrange("p (t s n) -> p s t n", t=TT, s=3),
                           ACT.Exp).then_inc(g_exp, 1)
            for u in range(NQ):
                if u >= 2:
                    act.wait_ge(sums, u - 1)
                act.activation(sq[:, u % 2, :], m.qkvT[:, order[u], :], ACT.Square).then_inc(squared, 1)
                act.wait_ge(sums, u + 1)
                if u >= 2:
                    act.wait_ge(normed, u - 1)
                act.activation(sd[:, u % 2, :], bank[:, u % 2, :], ACT.Sqrt, bias=m.eps[:, :]).then_inc(rooted, 1)
                if u < GH:
                    act.wait_ge(turned, 2 * u + 1)
                    act.activation(m.vtok[:, :, u * P:(u + 1) * P], bank[:, 2 + u % 2, :].rearrange("p (t n) -> p t n", t=TT),
                                   ACT.Copy).then_inc(tok_out, 1)
                    act.wait_ge(turned, 2 * u + 2)
                    act.activation(m.ktok[:, :, u * P:(u + 1) * P], bank[:, 4 + u % 2, :].rearrange("p (t n) -> p t n", t=TT),
                                   ACT.Copy).then_inc(tok_out, 1)

        @block.tensor
        def _(pe):
            pe.wait_ge(g_ready, 1)
            for t in range(TT):
                for i, tri in enumerate((m.upto, m.after, m.ones[:, :])):
                    at = (3 * t + i) * GH
                    mm = pe.matmul(bank[:, 7, at:at + GH], tri, m.g[:, t, :], start=True, stop=True)
                mm.then_inc(g_sums, 1)
            for u in range(NQ):
                pe.wait_ge(squared, u + 1)
                if u >= 2:
                    pe.wait_ge(rooted, u - 1)
                pe.matmul(bank[:, u % 2, :], m.ones[:, :], sq[:, u % 2, :], start=True, stop=True).then_inc(sums, 1)
                if u < GH:
                    if u >= 2:
                        pe.wait_ge(tok_out, 2 * u - 2)
                    for t in range(TT):
                        mm = pe.transpose(bank[:, 2 + u % 2, t * P:(t + 1) * P], m.qkvT[:, 2 * GH + u, t * P:(t + 1) * P], m.ident)
                    mm.then_inc(turned, 1)
                    pe.wait_ge(normed, u + 1)
                    for t in range(TT):
                        mm = pe.transpose(bank[:, 4 + u % 2, t * P:(t + 1) * P], m.qkvT[:, GH + u, t * P:(t + 1) * P], m.ident)
                    mm.then_inc(turned, 1)

        @block.vector
        def _(dve):
            link = chain(dve, step)
            dve.wait_ge(rb_in, 32)
            link(dve.tensor_tensor(tm[:, 0], m.rates[:, :, 0:GH], rb[:, 1, :].unsqueeze(1).to_broadcast([P, TT, GH]), ALU.add))
            dve.scalar_tensor_tensor(out=tm[:, 1], in0=tm[:, 0], scalar=-1.0, in1=tm[:, 0], op0=ALU.mult,
                                     op1=ALU.max).then_inc(abs_ready, 1)
            dve.wait_ge(abs_ready, 1)
            link(dve.tensor_scalar(tm[:, 0], tm[:, 0], 0.0, None, ALU.max))
            dve.wait_ge(act_step, 4)
            link(dve.tensor_tensor(tm[:, 0], tm[:, 0], tm[:, 3], ALU.add))
            link(dve.tensor_scalar(tm[:, 0], tm[:, 0], -1.0, None, ALU.mult))
            dve.tensor_tensor(m.g[:, :, :], tm[:, 0], rb[:, 0, :].unsqueeze(1).to_broadcast([P, TT, GH]), ALU.mult).then_inc(g_ready, 1)
            link(dve.tensor_scalar(m.neg_beta[:, :, :], m.beta[:, :, :], -1.0, None, ALU.mult))
            dve.wait_ge(g_exp, 1)
            dve.tensor_tensor(m.neg_beta_decay[:, :, :], m.neg_beta[:, :, :], m.decays[:, 0], ALU.mult)
            for u in range(NQ):
                x = m.qkvT[:, order[u], :]
                dve.wait_ge(rooted, u + 1)
                link(dve.reciprocal(sd[:, u % 2, :], sd[:, u % 2, :]))
                dve.scalar_tensor_tensor(out=x, in0=x, scalar=1.0 if order[u] >= GH else P ** -0.5, in1=sd[:, u % 2, :],
                                         op0=ALU.mult, op1=ALU.mult).then_inc(normed, 1)


def gdn_pairs(nc, m, I):
    bank = m.bank
    NB = TT * 2
    gm = m.arena("g_after", [P, 2, COLS], 112)
    ee = m.arena("pair_decay", [P, 2, COLS], 116)
    gm_ready = m.sem("g_after_ready")
    d_ready = m.sem("pair_sums")
    kk_ready = m.sem("pair_dots")
    e_ready = m.sem("pair_exp")
    nb_ready = m.sem("pair_neg_beta")
    step = m.sem("pair_step")
    done = m.sem("pair_done")
    masked = m.sem("pair_masked")

    def heads(v):
        return v.rearrange("p (h n) -> p h n", h=4)

    with nc.Block() as block:
        @block.gpsimd
        def _(pool):
            for b in range(NB):
                c, hh = divmod(b, 2)
                hs = slice(4 * hh, 4 * hh + 4)
                if b >= 2:
                    pool.wait_ge(d_ready, b - 1)
                pool.tensor_tensor(heads(gm[:, b % 2, :]), m.after.unsqueeze(1).to_broadcast([P, 4, P]),
                                   m.g[:, c, hs].unsqueeze(2).to_broadcast([P, 4, P]), ALU.mult).then_inc(gm_ready, 1)
                pool.tensor_tensor(m.negA[:, b], m.after.unsqueeze(1).to_broadcast([P, 4, P]),
                                   m.neg_beta[:, c, hs].unsqueeze(2).to_broadcast([P, 4, P]), ALU.mult).then_inc(nb_ready, 1)
                pool.wait_ge(done, 2 * b + 2)
                pool.tensor_tensor(m.qkT[:, b], m.qkT[:, b], m.upto.unsqueeze(1).to_broadcast([P, 4, P]), ALU.mult).then_inc(masked, 1)
                rows = m.vtok[:, c, hh * COLS:(hh + 1) * COLS]
                pool.tensor_tensor(heads(rows), heads(rows), m.beta[:, c, hs].unsqueeze(2).to_broadcast([P, 4, P]), ALU.mult)

        @block.tensor
        def _(pe):
            for b in range(NB):
                c, hh = divmod(b, 2)
                o = 4 * (b % 2)
                pe.wait_ge(gm_ready, b + 1)
                if b >= 2:
                    pe.wait_ge(done, 2 * b - 2)
                pe.matmul(bank[:, o, :], m.upto, gm[:, b % 2, :], start=True, stop=True)
                for h in range(4):
                    mm = pe.matmul(bank[:, o + 1, h * P:(h + 1) * P], gm[:, b % 2, h * P:(h + 1) * P], m.upto, start=True, stop=True)
                mm.then_inc(d_ready, 1)
                for h in range(4):
                    q = m.qkvT[:, 4 * hh + h, c * P:(c + 1) * P]
                    k = m.qkvT[:, GH + 4 * hh + h, c * P:(c + 1) * P]
                    pe.matmul(bank[:, o + 2, h * P:(h + 1) * P], k, k, start=True, stop=True)
                    mm = pe.matmul(bank[:, o + 3, h * P:(h + 1) * P], k, q, start=True, stop=True)
                mm.then_inc(kk_ready, 1)

        @block.scalar
        def _(act):
            for b in range(NB):
                o = 4 * (b % 2)
                act.wait_ge(d_ready, b + 1)
                for i in range(2):
                    if b >= 1:
                        act.wait_ge(done, 2 * b - 1 + i)
                    act.activation(ee[:, i, :], bank[:, o + i, :], ACT.Exp).then_inc(e_ready, 1)

        @block.vector
        def _(dve):
            link = chain(dve, step)
            for b in range(NB):
                o = 4 * (b % 2)
                dve.wait_ge(kk_ready, b + 1)
                dve.wait_ge(nb_ready, b + 1)
                dve.wait_ge(e_ready, 2 * b + 1)
                neg = m.negA[:, b].rearrange("p h n -> p (h n)")
                link(dve.tensor_tensor(neg, neg, bank[:, o + 2, :], ALU.mult))
                dve.tensor_tensor(neg, neg, ee[:, 0, :], ALU.mult).then_inc(done, 1)
                dve.wait_ge(e_ready, 2 * b + 2)
                dve.tensor_tensor(m.qkT[:, b].rearrange("p h n -> p (h n)"), ee[:, 1, :], bank[:, o + 3, :], ALU.mult).then_inc(done, 1)


def gdn_inverse(nc, m, I):
    bank = m.bank
    NB = TT * 2
    X = m.arena("inv_X", [P, 2, COLS], 112)
    nL = len(LEVELS)
    rounds = [(l, b) for l in range(nL) for b in range(NB)]
    id_set = m.sem("inv_identity")
    x_ready = m.sem("inv_x_ready")
    x_out = m.sem("inv_x_out")
    delta = m.sem("inv_delta")
    merged = m.sem("inv_merged")

    def flat(v):
        return v.rearrange("p h n -> p (h n)")

    with nc.Block() as block:
        @block.gpsimd
        def _(pool):
            for dst in (m.inv, m.invT):
                pool.tensor_copy(dst[:, :, :, :].rearrange("p b h n -> p (b h) n"),
                                 m.ident.unsqueeze(1).to_broadcast([P, 4 * NB, P])).then_inc(id_set, 1)

        @block.tensor
        def _(pe):
            pe.wait_ge(id_set, 2)

            def first(r):
                l, b = rounds[r]
                if l >= 1:
                    pe.wait_ge(merged, r - NB + 1)
                if r >= 2:
                    pe.wait_ge(x_out, r - 1)
                for h in range(4):
                    mm = pe.matmul(bank[:, r % 2, h * P:(h + 1) * P], m.negA[:, b, h, :], m.invT[:, b, h, :], start=True, stop=True)
                mm.then_inc(x_ready, 1)

            first(0)
            for r, (l, b) in enumerate(rounds):
                if r + 1 < len(rounds):
                    first(r + 1)
                pe.wait_ge(x_out, r + 1)
                if r >= 2:
                    pe.wait_ge(merged, r - 1)
                o = 2 + 2 * (r % 2)
                for h in range(4):
                    cut = slice(h * P, (h + 1) * P)
                    mm = pe.matmul(bank[:, o, cut], m.inv[:, b, h, :], X[:, r % 2, cut], start=True, stop=True)
                if l < nL - 1:
                    for h in range(4):
                        cut = slice(h * P, (h + 1) * P)
                        mm = pe.matmul(bank[:, o + 1, cut], X[:, r % 2, cut], m.inv[:, b, h, :], start=True, stop=True)
                mm.then_inc(delta, 1)

        @block.scalar
        def _(act):
            for r in range(len(rounds)):
                act.wait_ge(x_ready, r + 1)
                if r >= 2:
                    act.wait_ge(delta, r - 1)
                act.activation(X[:, r % 2, :], bank[:, r % 2, :], ACT.Copy).then_inc(x_out, 1)

        @block.vector
        def _(dve):
            dve.wait_ge(id_set, 2)
            for r, (l, b) in enumerate(rounds):
                o = 2 + 2 * (r % 2)
                dve.wait_ge(delta, r + 1)
                up = m.masks[:, l, :].unsqueeze(1).to_broadcast([P, 4, P])
                low = m.masks[:, nL + l, :].unsqueeze(1).to_broadcast([P, 4, P])
                ins = dve.copy_predicated(m.invT[:, b], up, bank[:, o, :].rearrange("p (h n) -> p h n", h=4))
                if l < nL - 1:
                    ins = dve.copy_predicated(m.inv[:, b], low, bank[:, o + 1, :].rearrange("p (h n) -> p h n", h=4))
                ins.then_inc(merged, 1)


def gdn_scan(nc, m, I):
    bank = m.bank
    NB = TT * 2
    S = m.arena("gdn_state", [P, 2, COLS], 112)
    new = m.arena("gdn_new", [P, 2, COLS], 116)
    oi = m.scratch("gdn_o_state", [P, 2, COLS], 0)
    late = m.scratch("gdn_new_decayed", [P, 2, COLS], 4)
    ks_ready, r_ready, new_ready, new_out, late_ready, qs_ready, o_ready, ds_ready, oi_ready, o_out, s_ready = [
        m.sem(f"scan_{n}") for n in ("ks", "r", "new", "new_out", "late", "qs", "o", "ds", "oi", "o_out", "s")]

    def cut(h):
        return slice(h * P, (h + 1) * P)

    with nc.Block() as block:
        @block.tensor
        def _(pe):
            for c in range(TT):
                tok = slice(c * P, (c + 1) * P)
                for g in range(2 if c else 0):
                    pe.wait_ge(s_ready, 2 * (c - 1) + g + 1)
                    for h in range(4):
                        mm = pe.matmul(bank[:, g, cut(h)], m.qkvT[:, GH + 4 * g + h, tok], S[:, g, cut(h)], start=True, stop=True)
                    mm.then_inc(ks_ready, 1)
                for g in range(2 if c else 0):
                    if c >= 2:
                        pe.wait_ge(oi_ready, 2 * (c - 2) + g + 1)
                    for h in range(4):
                        mm = pe.matmul(bank[:, 2 + g, cut(h)], m.qkvT[:, 4 * g + h, tok], S[:, g, cut(h)], start=True, stop=True)
                    mm.then_inc(qs_ready, 1)
                for g in range(2):
                    n = 2 * c + g
                    if c:
                        pe.wait_ge(r_ready, n - 1)
                    for h in range(4):
                        mm = pe.matmul(bank[:, 4 + g, cut(h)], m.invT[:, n, h, :], m.vtok[:, c, cut(4 * g + h)], start=True, stop=True)
                    mm.then_inc(new_ready, 1)
                for g in range(2):
                    n = 2 * c + g
                    pe.wait_ge(late_ready, n + 1)
                    for h in range(4):
                        mm = pe.matmul(bank[:, g, cut(h)], m.ktok[:, c, cut(4 * g + h)], late[:, g, cut(h)], start=True, stop=True)
                    mm.then_inc(ds_ready, 1)
                for g in range(2):
                    n = 2 * c + g
                    pe.wait_ge(new_out, n + 1)
                    if c:
                        pe.wait_ge(o_out, n - 1)
                    for h in range(4):
                        mm = pe.matmul(bank[:, 6 + g, cut(h)], m.qkT[:, n, h, :], new[:, g, cut(h)], start=True, stop=True)
                    mm.then_inc(o_ready, 1)

        @block.scalar
        def _(act):
            for c in range(TT):
                for g in range(2):
                    n = 2 * c + g
                    act.wait_ge(late_ready, n + 1)
                    if c:
                        act.wait_ge(o_ready, n - 1)
                    act.activation(new[:, g, :], bank[:, 4 + g, :], ACT.Copy).then_inc(new_out, 1)
                for g in range(2 if c else 0):
                    act.wait_ge(qs_ready, 2 * (c - 1) + g + 1)
                    if c >= 2:
                        act.wait_ge(o_out, 2 * (c - 1) + g + 1)
                    for h in range(4):
                        ins = act.activation(oi[:, g, cut(h)], bank[:, 2 + g, cut(h)], ACT.Copy,
                                             scale=m.decays[:, 0, c, 4 * g + h:4 * g + h + 1])
                    ins.then_inc(oi_ready, 1)

        @block.vector
        def _(dve):
            for c in range(TT):
                for g in range(2 if c else 0):
                    dve.wait_ge(ks_ready, 2 * (c - 1) + g + 1)
                    for h in range(4):
                        v = m.vtok[:, c, cut(4 * g + h)]
                        ins = dve.scalar_tensor_tensor(out=v, in0=bank[:, g, cut(h)],
                                                       scalar=m.neg_beta_decay[:, c, 4 * g + h:4 * g + h + 1], in1=v,
                                                       op0=ALU.mult, op1=ALU.add)
                    ins.then_inc(r_ready, 1)
                for g in range(2):
                    n = 2 * c + g
                    dve.wait_ge(new_ready, n + 1)
                    dve.tensor_tensor(late[:, g, :].rearrange("p (h n) -> p h n", h=4),
                                      bank[:, 4 + g, :].rearrange("p (h n) -> p h n", h=4),
                                      m.decays[:, 1, c, 4 * g:4 * g + 4].unsqueeze(2).to_broadcast([P, 4, P]),
                                      ALU.mult).then_inc(late_ready, 1)
                for g in range(2):
                    n = 2 * c + g
                    dve.wait_ge(ds_ready, n + 1)
                    if c == 0:
                        dve.tensor_copy(S[:, g, :], bank[:, g, :]).then_inc(s_ready, 1)
                    elif c < TT - 1:
                        dve.wait_ge(qs_ready, n - 1)
                        dve.wait_ge(s_ready, n - 1)
                        for h in range(4):
                            ins = dve.scalar_tensor_tensor(out=S[:, g, cut(h)], in0=S[:, g, cut(h)],
                                                           scalar=m.decays[:, 2, c, 4 * g + h:4 * g + h + 1],
                                                           in1=bank[:, g, cut(h)], op0=ALU.mult, op1=ALU.add)
                        ins.then_inc(s_ready, 1)
                for g in range(2):
                    n = 2 * c + g
                    dve.wait_ge(o_ready, n + 1)
                    o = m.vtok[:, c, 4 * g * P:4 * (g + 1) * P]
                    if c:
                        dve.wait_ge(oi_ready, n - 1)
                        dve.tensor_tensor(o, bank[:, 6 + g, :], oi[:, g, :], ALU.add).then_inc(o_out, 1)
                    else:
                        dve.tensor_copy(o, bank[:, 6 + g, :]).then_inc(o_out, 1)


def gdn_gate(nc, m, I):
    nu = TT * GH
    o, gate = m.vtok, m.gate
    sq = m.arena("gdn_o_square", [P, TT, D], 16)
    sg = m.arena("gdn_gate_sig", [P, TT, D], 48)
    w = m.arena("gdn_norm_w", [P, P], 112)
    ss = m.arena("gdn_o_ss", [P, TT, GH], 113)
    sd = m.arena("gdn_o_sd", [P, TT, GH], 114)
    rstd = m.arena("gdn_o_rstd", [P, TT, GH], 115)
    w_in, squared, summed, rooted, inverse, sig, gated, scaled = [
        m.sem(f"gdn_gate_{n}") for n in ("w_in", "squared", "summed", "rooted", "inverse", "sig", "gated", "scaled")]

    def heads(v):
        return v.rearrange("p (h n) -> p h n", n=P)

    with nc.Block() as block:
        @block.sync
        def _(sp):
            sp.dma_start(w[:, :], I["gdn_o_norm_g_2"].partition_broadcast(P)).then_inc(w_in, 16)
            sp.wait_ge(w_in, 16)

        @block.scalar
        def _(act):
            for t in range(TT):
                act.activation(sq[:, t, :], o[:, t, :], ACT.Square).then_inc(squared, 1)
            for t in range(TT):
                act.activation(sg[:, t, :], gate[:, t, :], ACT.Sigmoid).then_inc(sig, 1)
            act.wait_ge(summed, TT)
            act.activation(sd[:, :, :], ss[:, :, :], ACT.Sqrt, bias=m.eps[:, :], scale=1.0 / P).then_inc(rooted, 1)

        @block.gpsimd
        def _(pool):
            pool.wait_ge(w_in, 16)
            for t in range(TT):
                pool.wait_ge(sig, t + 1)
                pool.tensor_tensor(gate[:, t, :], gate[:, t, :], sg[:, t, :], ALU.mult).then_inc(gated, 1)
                pool.wait_ge(gated, 2 * t + 1)
                pool.tensor_tensor(heads(gate[:, t, :]), heads(gate[:, t, :]), w[:, :].unsqueeze(1).to_broadcast([P, GH, P]),
                                   ALU.mult).then_inc(gated, 1)

        @block.vector
        def _(dve):
            for t in range(TT):
                dve.wait_ge(squared, t + 1)
                dve.tensor_reduce(ss[:, t, :], heads(sq[:, t, :]), AX.X, ALU.add).then_inc(summed, 1)
            dve.wait_ge(rooted, 1)
            dve.reciprocal(rstd[:, :, :], sd[:, :, :]).then_inc(inverse, 1)
            dve.wait_ge(inverse, 1)
            for t in range(TT):
                dve.tensor_tensor(heads(o[:, t, :]), heads(o[:, t, :]), rstd[:, t, :].unsqueeze(2).to_broadcast([P, GH, P]),
                                  ALU.mult).then_inc(scaled, 1)
            for t in range(TT):
                dve.wait_ge(scaled, t + 1)
                dve.wait_ge(gated, 2 * t + 2)
                dve.tensor_tensor(o[:, t, :], o[:, t, :], gate[:, t, :], ALU.mult)


def turn_gdn_out(nc, m, I):
    turn_features(nc, m, "ogT", [rows_of(m.vtok, k) for k in range(KD)], m.ogT)


def gdn_project_out(nc, m, I):
    x_in = m.sem("x3_again")

    def products(pe, ready):
        for t in range(TT):
            for n in range(2):
                slab_wait(pe, m, S_GOUT + n)
                for k in range(KD):
                    mm = pe.matmul(m.bank[:, 2 * t + n, :], m.ogT[:, k, t * P:(t + 1) * P], m.ring[:, (S_GOUT + n) % RING, k, :],
                                   start=(k == 0), stop=(k == KD - 1))
            mm.then_inc(ready, 1)

    def loads(sp, ready):
        sp.dma_start(m.x[:, :, :], m.x_spill).then_inc(x_in, 16)
        stream(sp, m, I, S_W1, S_W1 + 2, lambda s: (x_in, 16))
        stream(sp, m, I, S_W1 + 2, S_W1 + 4, lambda s: (ready, TT))

    residual(nc, m, I, "out3", m.x, m.xn4, products, loads, (x_in, 16))


def turn_mlp(nc, m, I):
    turn_features(nc, m, "h4T", [rows_of(m.xn4, k) for k in range(KD)], m.h4T, m.vecs[:, V_MLP2:V_MLP2 + KD])


def mlp_up(nc, m, I):
    bank = m.bank
    NU = D_FF // P
    r = m.arena("mlp_relu", [P, 2, T], 112)
    product = m.sem("mlp_product")
    relu = m.sem("mlp_relu_ready")
    squared = m.sem("mlp_squared")
    with nc.Block() as block:
        @block.sync
        def _(sp):
            stream(sp, m, I, S_W1 + RING, S_W2 + RING, lambda s: (product, 4 * (s - S_W1 + 1)))

        @block.tensor
        def _(pe):
            for u in range(NU):
                slab_wait(pe, m, S_W1 + u // 4)
                if u >= 8:
                    pe.wait_ge(relu, u - 7)
                for k in range(KD):
                    mm = pe.matmul(bank[:, u % 8, :], m.ring[:, (S_W1 + u // 4) % RING, k, (u % 4) * P:(u % 4 + 1) * P],
                                   m.h4T[:, k, :], start=(k == 0), stop=(k == KD - 1))
                mm.then_inc(product, 1)

        @block.scalar
        def _(act):
            for u in range(NU):
                act.wait_ge(product, u + 1)
                if u >= 2:
                    act.wait_ge(squared, u - 1)
                act.activation(r[:, u % 2, :], bank[:, u % 8, :], ACT.Relu).then_inc(relu, 1)

        @block.vector
        def _(dve):
            for u in range(NU):
                dve.wait_ge(relu, u + 1)
                dve.tensor_tensor(m.up[:, u, :], r[:, u % 2, :], r[:, u % 2, :], ALU.mult).then_inc(squared, 1)


def mlp_down(nc, m, I):
    used = m.sem("mlp_down_used")

    def products(pe, ready):
        for s in range(S_W2, S_END):
            r, n = divmod(s - S_W2, 2)
            slab_wait(pe, m, s)
            for t in range(TT):
                for k in range(KD):
                    mm = pe.matmul(m.bank[:, 2 * t + n, :], m.up[:, r * KD + k, t * P:(t + 1) * P], m.ring[:, s % RING, k, :],
                                   start=(r == 0 and k == 0), stop=(r == D_FF // D - 1 and k == KD - 1))
                if s == S_END - 1:
                    mm.then_inc(ready, 1)
            if s < S_END - 1:
                mm.then_inc(used, 1)

    def loads(sp, ready):
        stream(sp, m, I, S_W2 + RING, S_END, lambda s: (used, s - S_W2 + 1))

    residual(nc, m, I, "out4", m.x, m.xn5, products, loads)


def store(nc, m, I, out):
    w = m.arena("final_norm_w", [P, D], 48)
    w_in = m.sem("final_w_in")
    done = m.sem("final_done")
    stored = m.sem("y_stored")
    y = out[0].rearrange("(t p) d -> p t d", p=P)
    with nc.Block() as block:
        @block.sync
        def _(sp):
            sp.dma_start(w[:, :], I["final_norm_g_2"].rearrange("(o d) -> o d", o=1).partition_broadcast(P)).then_inc(w_in, 16)
            for t in range(TT):
                sp.wait_ge(done, t + 1)
                sp.dma_start(y[:, t, :], m.xn5[:, t, :]).then_inc(stored, 16)
            sp.wait_ge(stored, 16 * TT)

        @block.vector
        def _(dve):
            dve.wait_ge(w_in, 16)
            for t in range(TT):
                dve.tensor_tensor(m.xn5[:, t, :], m.xn5[:, t, :], w[:, :], ALU.mult).then_inc(done, 1)


def build(nc, I, out, stop=None, dump=None):
    m = allocate(nc)
    m.slab_loaded = [nc.alloc_semaphore(f"slab_loaded{i}") for i in range(RING)]
    m.xn1 = m.arena("xn1", [P, AT, D], 24)
    m.hT = m.arena("hT", [P, KD, TA], 98)
    m.proj = {
        "qT": m.arena("qT", [P, HEADS, T], 0), "kT": m.arena("kT", [P, HEADS, TA], 8),
        "v": m.arena("v", [P, AT, COLS], 20), "zf": m.arena("zf", [P, HEADS, TA], 32),
        "zb": m.arena("zb", [P, HEADS, TA], 44), "hv": m.arena("hv", [P, AT, COLS], 56),
        "hqT": m.arena("hqT", [P, HEADS, T], 68), "hg": m.arena("hg", [P, TT, COLS], 76),
    }
    m.mix_da = m.arena("mix_da", [P, TT, COLS], 84)
    m.scores = m.arena("scores", [P, HEADS, T], 24)
    m.states = (m.arena("states0", [P, 5, COLS], 108), m.arena("states1", [P, 5, COLS], 92))
    m.mixT = m.arena("mixT", [P, KD, T], 0)
    m.x = m.arena("x", [P, TT, D], 32)
    m.xn2 = m.arena("xn2", [P, TT, D], 48)
    m.h2T = m.arena("h2T", [P, KD, T], 64)
    m.onehot = m.arena("onehot", [P, TT, D], 0)
    m.spread = m.arena("spread", [P, EXPERTS // 2, T], 96)
    m.y = m.arena("expert_out", [P, EXPERTS // 2, D], 64)
    m.xn3 = m.arena("xn3", [P, TT, D], 48)
    NB = 2 * TT
    m.x_spill = nc.dram_tensor("x3_spill", (P, TT, D), F32).ap()
    m.h3T = m.arena("h3T", [P, KD, T], 16)
    m.qkvT = m.arena("qkvT", [P, 3 * GH, T], 48)
    m.gate = m.arena("gdn_gate", [P, TT, D], 96)
    m.vtok = m.arena("gdn_vtok", [P, TT, D], 0)
    m.ktok = m.arena("gdn_ktok", [P, TT, D], 16)
    m.qkT = m.arena("gdn_qkT", [P, NB, 4, P], 32)
    m.invT = m.arena("gdn_invT", [P, NB, 4, P], 80)
    m.negA = m.scratch("gdn_negA", [P, NB, 4, P], 0)
    m.inv = m.scratch("gdn_inv", [P, NB, 4, P], 16)
    m.rates = m.small("rates", [P, TT, 2 * GH], 0)
    m.beta = m.small("beta", [P, TT, GH], 256)
    m.neg_beta = m.small("neg_beta", [P, TT, GH], 384)
    m.neg_beta_decay = m.small("neg_beta_decay", [P, TT, GH], 512)
    m.g = m.small("g_log", [P, TT, GH], 640)
    m.decays = m.small("decays", [P, 3, TT, GH], 768)
    m.ogT = m.arena("ogT", [P, KD, T], 64)
    m.xn4 = m.arena("xn4", [P, TT, D], 80)
    m.h4T = m.arena("h4T", [P, KD, T], 0)
    m.up = m.arena("mlp_up", [P, D_FF // P, T], 48)
    m.xn5 = m.arena("xn5", [P, TT, D], 0)
    held = []

    def sem(name):
        held.append(nc.alloc_semaphore(name))
        return held[-1]

    m.sem = sem
    for stage in STAGES:
        stage(nc, m, I)
        if stage in RELEASE:
            nc.clear_and_free_semaphores(held)
            nc.all_engine_barrier()
            held.clear()
        if stop == stage.__name__:
            dump(nc, m)
            return
    store(nc, m, I, out)


STAGES = [modulation, hidden_transposed, project_in, rotary, attention, forget_gates,
          recurrence_forward, recurrence_backward, mix_outputs, turn_mix, project_out, turn_ffn, route,
          experts, scatter, turn_gdn, gdn_project, gdn_norms, gdn_pairs, gdn_inverse, gdn_scan, gdn_gate,
          turn_gdn_out, gdn_project_out, turn_mlp, mlp_up, mlp_down]
RELEASE = (mix_outputs, scatter, gdn_pairs)


USED = ["x", "c", "ctx", "c_ctx", "w_ada", "b_ada", "norm_pre_mix", "norm_post_mix", "norm_pre_ffn", "norm_post_ffn",
        "w_in", "da_lambda_q1", "da_lambda_k1", "da_lambda_q2", "da_lambda_k2", "da_subln", "hg_lower_bound",
        "hg_norm", "w_out", "w_router", "w_gate", "w_up", "w_down", "norm_mix_g_2", "norm_mlp_g_2", "mlp_w1_2",
        "mlp_w2_2", "gdn_w_in_2", "gdn_conv_w_2", "gdn_a_log_2", "gdn_dt_bias_2", "gdn_o_norm_g_2", "gdn_w_out_2",
        "final_norm_g_2"]


def kernel(**inputs):
    import concourse.bacc as bacc
    from concourse.bass_utils import run_bass_kernel_spmd

    nc = bacc.Bacc("TRN2", target_bir_lowering=False, num_devices=1)
    arrays = {name: np.ascontiguousarray(inputs[name]) for name in USED}
    arrays.update(shape_constants())
    I = {name: nc.dram_tensor(name, a.shape, mybir.dt.from_np(a.dtype), kind="ExternalInput").ap()
         for name, a in arrays.items()}
    out = nc.dram_tensor("y", (1, T, D), F32, kind="ExternalOutput").ap()
    build(nc, I, out)
    result = run_bass_kernel_spmd(nc, [arrays], core_ids=[0])
    return result.results[0]["y"]
```

```python
import math

import numpy as np
import concourse.bass as bass
import concourse.mybir as mybir

F32 = mybir.dt.float32
F32R = mybir.dt.float32r
U8 = mybir.dt.uint8
ALU = mybir.AluOpType
ACT = mybir.ActivationFunctionType
AX = mybir.AxisListType

P = 128
D = 1024
KD = D // P
T = 512
TC = 256
TT = T // P
CT = TC // P
TA = T + TC
AT = TA // P
COLS = 512
GRID_W = 64
HEADS = 4
HD = 64
LAMBDA_INIT = 0.8 - 0.6 * math.exp(0.0)
EPS = 1e-6
EXPERTS = 16
CAP = 2 * T // EXPERTS
FF = 1024
D_FF = 4096
GH = 8
CONV_W = 4
LEVELS = [1, 2, 4, 8, 16, 32, 64]
KB = 1024

V_C, V_CCTX, V_PREMIX, V_PREFFN, V_MIX2, V_MLP2, V_BADA, V_LB = 0, 8, 16, 24, 32, 40, 48, 96
V_ROWS = 112
V_CONV = V_ROWS
V_ALL = V_ROWS + CONV_W * 24

S_ADA, S_IN, S_REST, S_OUT, S_EXP, S_GIN, S_GOUT, S_MLP, S_END = 0, 4, 12, 20, 22, 118, 126, 128, 144
RING = 4


def shape_constants():
    i = np.arange(P)
    ident = np.eye(P, dtype=np.float32)
    rot = np.zeros((P, P), np.float32)
    for m in range(P):
        if m % 32 < 16:
            rot[m + 16, m] = -1.0
        else:
            rot[m - 16, m] = 1.0
    upto = (i[:, None] <= i[None, :]).astype(np.float32)
    after = (i[:, None] > i[None, :]).astype(np.float32)
    half = HD // 2
    inv_freq = (np.float32(1.0) / (np.float32(10000.0) ** (np.arange(0, half, 2, dtype=np.float32) / np.float32(half))))
    t = np.arange(T)
    ang_r = (t // GRID_W).astype(np.float32)[:, None] * inv_freq
    ang_c = (t % GRID_W).astype(np.float32)[:, None] * inv_freq
    ang = np.concatenate([ang_r, ang_r, ang_c, ang_c] * 2, axis=-1).T.astype(np.float32)
    slot = np.broadcast_to(np.arange(1, CAP + 1, dtype=np.float32), (P, CAP))
    slot_col = (i % CAP + 1).astype(np.float32)[:, None]
    table = np.concatenate([ident, rot, upto, after, np.cos(ang), np.sin(ang), slot, slot_col], axis=1)
    pairs = np.zeros((EXPERTS, EXPERTS // 2, P), np.float32)
    for e in range(EXPERTS):
        pairs[e, e // 2, (e % 2) * CAP:(e % 2 + 1) * CAP] = 1.0
    masks = []
    for L in LEVELS:
        b = i // L
        masks.append((b[:, None] % 2 == 0) & (b[None, :] == b[:, None] + 1))
    up = np.stack(masks, axis=1).astype(np.float32)
    low = np.stack([m.T for m in masks], axis=1).astype(np.float32)
    return {
        "k_table": np.ascontiguousarray(table.astype(np.float32)),
        "k_pairs": pairs.reshape(EXPERTS, -1),
        "k_masks": np.ascontiguousarray(np.concatenate([up, low], axis=1).reshape(P, -1)),
    }


class Shared:
    pass


TABLE = 4 * P + 2 * T + CAP + 1


def allocate(nc):
    base = (nc.sbuf_base + 31) // 32 * 32

    def place(name, shape, at, dtype=F32):
        return nc.alloc_sbuf_tensor_at(name, shape, dtype, offset=base + at)

    m = Shared()
    m.ring = place("ring", [P, RING, KD, COLS], 0)
    m.table = place("table", [P, TABLE], 64 * KB)
    m.ident = m.table[:, 0:P]
    m.rot = m.table[:, P:2 * P]
    m.upto = m.table[:, 2 * P:3 * P]
    m.after = m.table[:, 3 * P:4 * P]
    m.cos = m.table[:, 4 * P:4 * P + T]
    m.sin = m.table[:, 4 * P + T:4 * P + 2 * T]
    m.slot = m.table[:, 4 * P + 2 * T:4 * P + 2 * T + CAP]
    m.slot_col = m.table[:, TABLE - 1:TABLE]
    at = 64 * KB + (TABLE * 4 + 31) // 32 * 32
    m.masks = place("masks", [P, 2 * len(LEVELS), P], at, U8)
    at += 2 * len(LEVELS) * P
    m.vecs = place("vecs", [P, V_ALL], at)
    at += V_ALL * 4
    m.mod = place("mod", [P, 32, 2], at)
    at += 256
    m.a1 = place("a1", [P, KD, 2], at)
    m.a2 = place("a2", [P, KD], at + 64)
    m.silu_c = place("silu_c", [P, KD, 2], at + 96)
    m.ones = place("ones", [P, P], at + 160)
    at += 160 + 512
    gates = at
    m.gate1 = place("gate1", [P, D], at)
    m.gate2 = place("gate2", [P, D], at + 4 * KB)
    at += 8 * KB
    m.eps = place("eps", [P, 1], at)
    m.neg_lam = place("neg_lam", [P, 1], at + 32)
    at += 64
    work = (at + 31) // 32 * 32
    assert base + work + 122 * KB <= nc.sbuf_usable_end, (base + work, nc.sbuf_usable_end)

    def arena(name, shape, kb, dtype=F32):
        size = int(np.prod(shape[1:])) * (1 if dtype == U8 else 4)
        assert kb * KB + size <= 122 * KB + 0, name
        return place(name, shape, work + int(kb * KB), dtype)

    def scratch(name, shape, kb, dtype=F32):
        return place(name, shape, kb * KB, dtype)

    def small(name, shape, at, dtype=F32):
        return place(name, shape, gates + at, dtype)

    m.arena, m.scratch, m.small = arena, scratch, small
    m.bank = nc.alloc_psum_tensor("bank", [P, 8, COLS], F32)
    return m


def slab_source(I, s):
    def cut(w, n, r=0):
        return w[r * D:(r + 1) * D, n * COLS:(n + 1) * COLS].rearrange("(k p) n -> p k n", p=P)

    if s < S_IN:
        return cut(I["w_ada"][0], s)
    if s < S_REST:
        return cut(I["w_in"][0], s - S_IN)
    if s < S_OUT:
        return cut(I["w_ada"][0], s - S_REST + 4)
    if s < S_EXP:
        return cut(I["w_out"][0], s - S_OUT)
    if s < S_GIN:
        e, j = divmod(s - S_EXP, 6)
        return cut(I[("w_gate", "w_up", "w_down")[j // 2]][0, e], j % 2)
    if s < S_GOUT:
        return cut(I["gdn_w_in_2"][0], s - S_GIN)
    if s < S_MLP:
        return cut(I["gdn_w_out_2"][0], s - S_GOUT)
    r, n = divmod(s - S_MLP, 4)
    return cut(I["mlp_w1_2"][0], 2 * r + n) if n < 2 else cut(I["mlp_w2_2"][0], n - 2, r)


def slot_of(s):
    return s % 2 if S_IN <= s < S_REST else s % RING


def loads_of(s):
    if s < S_IN:
        return 1
    if s < S_REST:
        return 2 + (s - S_IN) // 2
    return s // RING + 1 + (2 if s % RING < 2 else -2)


def slab_before(s):
    return s - RING if s < S_IN + 2 or s >= S_REST + 2 else s - 2


def stream(eng, m, I, first, last, freed=None):
    for s in range(first, last):
        if s >= RING:
            eng.wait_ge(*freed(slab_before(s)))
        eng.dma_start(m.ring[:, slot_of(s)], slab_source(I, s)).then_inc(m.slab_loaded[slot_of(s)], 16)


def slab_wait(eng, m, s):
    eng.wait_ge(m.slab_loaded[slot_of(s)], 16 * loads_of(s))


def slab_part(m, s, i, by_rows):
    w = m.ring[:, slot_of(s)]
    return w[:, 2 * i:2 * i + 2, :] if by_rows else w[:, :, i * P:(i + 1) * P]


def split_buffers(m, tag, places):
    return [[m.arena(f"{tag}_{n}{b}", [P, KD * P], kb + off, F32R) for n, off in (("hi", 0), ("lo", 4))]
            for b, kb in enumerate(places)]


def shaped(part, by_rows):
    return part[:, :].rearrange("p (k n) -> p k n", n=COLS if by_rows else P)


def product3(pe, out, a, b, start, stop):
    for i, (x, y) in enumerate(((a[0], b[0]), (a[0], b[1]), (a[1], b[0]))):
        mm = pe.matmul(out, x, y, start=(start and i == 0), stop=(stop and i == 2))
    return mm


def chain(eng, sem):
    count = [0]

    def link(ins):
        count[0] += 1
        ins.then_inc(sem, 1)
        eng.wait_ge(sem, count[0])

    return link


def shift_scale(pe, m, out, w, j):
    for q in range(4):
        n = 4 * j + q
        for k in range(KD):
            mm = pe.matmul(out[:, 2 * n:2 * n + 2], w[:, k, q * P:(q + 1) * P], m.silu_c[:, k, :],
                           start=(k == 0), stop=(k == KD - 1))
    return mm


def add_bias(dve, m, src, half):
    b = m.vecs[:, V_BADA + 24 * half:V_BADA + 24 * half + 16].unsqueeze(2).to_broadcast([P, 16, 2])
    return dve.tensor_tensor(m.mod[:, 16 * half:16 * half + 16, :], src.rearrange("p (n s) -> p n s", s=2), b, ALU.add)


def modulation(nc, m, I):
    rows = m.arena("vec_rows", [V_ROWS, P], 72)
    conv_rows = m.arena("conv_rows", [CONV_W * 24, P], 72.5)
    sig = m.arena("sig_c", [P, 16], 73)
    sc = m.silu_c
    wide_masks = m.arena("wide_masks", [P, 2 * len(LEVELS), P], 88)
    x = m.arena("x_rows", [P, AT, D], 0)
    xn = m.xn1
    junk = m.arena("square1", [P, 2, D], 78)
    ss = m.arena("ss1", [P, AT], 86)
    sd = m.arena("sd1", [P, AT], 86.125)
    rstd = m.arena("rstd1", [P, AT], 86.25)
    bank = m.bank

    rows_in = m.sem("rows_in")
    table_in = m.sem("table_in")
    masks_in = m.sem("masks_in")
    x_in = [m.sem(f"x_in{t}") for t in range(2)]
    consts_set = m.sem("consts_set")
    vecs_turned = m.sem("vecs_turned")
    vecs_ready = m.sem("vecs_ready")
    sig_ready = m.sem("sig_ready")
    ada_done = m.sem("ada_done")
    silu_ready = m.sem("silu_ready")
    squares = m.sem("squares1")
    roots = m.sem("roots1")
    dve_step = m.sem("dve_step1")
    with nc.Block() as block:
        @block.sync
        def _(sp):
            spans = [("c", V_C), ("norm_pre_mix", V_PREMIX), ("norm_pre_ffn", V_PREFFN),
                     ("norm_mix_g_2", V_MIX2), ("norm_mlp_g_2", V_MLP2), ("b_ada", V_BADA)]
            for name, at in spans:
                src = I[name].rearrange("o (k p) -> (o k) p", p=P)
                sp.dma_start(rows[at:at + src.shape[0], :], src).then_inc(rows_in, 16)
            sp.dma_start(rows[V_CCTX:V_CCTX + KD, :], I["c_ctx"].rearrange("(k p) -> k p", p=P)).then_inc(rows_in, 16)
            sp.dma_start(rows[V_LB:V_ROWS, :], I["hg_lower_bound"].rearrange("l d (h p) -> (l d h) p", p=P)).then_inc(rows_in, 16)
            sp.dma_start(conv_rows[:, :], I["gdn_conv_w_2"][0].rearrange("j (k p) -> (j k) p", p=P)).then_inc(rows_in, 16)
            sp.dma_start(m.table[:, :], I["k_table"]).then_inc(table_in, 16)
            stream(sp, m, I, 0, 2)
            sp.dma_start(x[:, 0:CT, :], I["ctx"][0].rearrange("(t p) d -> p t d", p=P)).then_inc(x_in[0], 16)
            sp.dma_start(x[:, CT:AT, :], I["x"][0].rearrange("(t p) d -> p t d", p=P)).then_inc(x_in[1], 16)
            stream(sp, m, I, 2, 4)
            sp.dma_start(wide_masks[:, :, :], I["k_masks"].rearrange("p (n q) -> p n q", q=P)).then_inc(masks_in, 16)
            stream(sp, m, I, S_IN, S_IN + 2, lambda s: (ada_done, s + 1))

        @block.gpsimd
        def _(pool):
            pool.memset(m.eps[:, :], EPS).then_inc(consts_set, 1)
            pool.memset(m.ones[:, :], 1.0).then_inc(consts_set, 1)
            pool.wait_ge(masks_in, 16)
            pool.tensor_copy(m.masks[:, :, :], wide_masks[:, :, :])

        @block.tensor
        def _(pe):
            pe.wait_ge(rows_in, 9 * 16)
            pe.wait_ge(table_in, 16)
            pe.transpose(bank[:, 0, 0:V_ROWS], rows[:, :], m.ident[0:V_ROWS, 0:V_ROWS])
            pe.transpose(bank[:, 0, V_CONV:V_ALL], conv_rows[:, :], m.ident[0:CONV_W * 24, 0:CONV_W * 24]).then_inc(vecs_turned, 1)
            pe.wait_ge(silu_ready, 1)
            for s in range(S_IN):
                slab_wait(pe, m, s)
                shift_scale(pe, m, bank[:, 1, :], m.ring[:, s % RING], s).then_inc(ada_done, 1)

        @block.scalar
        def _(act):
            act.wait_ge(vecs_ready, 1)
            act.activation(sig[:, :], m.vecs[:, V_C:V_C + 16], ACT.Sigmoid).then_inc(sig_ready, 1)
            for t in range(AT):
                act.wait_ge(x_in[0 if t < CT else 1], 16)
                act.activation(junk[:, t % 2, :], x[:, t, :], ACT.Square, accum_out=ss[:, t:t + 1]).then_inc(squares, 1)
                if t >= 1:
                    act.wait_ge(squares, t)
            act.wait_ge(squares, AT)
            act.wait_ge(consts_set, 2)
            act.activation(sd[:, :], ss[:, :], ACT.Sqrt, bias=m.eps[:, :], scale=1.0 / D).then_inc(roots, 1)

        @block.vector
        def _(dve):
            link = chain(dve, dve_step)
            dve.wait_ge(vecs_turned, 1)
            dve.tensor_copy(m.vecs[:, :], bank[:, 0, 0:V_ALL]).then_inc(vecs_ready, 1)
            dve.wait_ge(sig_ready, 1)
            dve.wait_ge(vecs_ready, 1)
            dve.tensor_tensor(sc[:, :, :].rearrange("p k s -> p s k"),
                              m.vecs[:, V_C:V_C + 16].rearrange("p (s k) -> p s k", s=2),
                              sig[:, :].rearrange("p (s k) -> p s k", s=2), ALU.mult).then_inc(silu_ready, 1)
            dve.wait_ge(roots, 1)
            link(dve.reciprocal(rstd[:, :], sd[:, :]))
            for t in range(AT):
                dve.tensor_scalar(xn[:, t, :], x[:, t, :], rstd[:, t:t + 1], None, ALU.mult)
            dve.wait_ge(ada_done, S_IN)
            link(add_bias(dve, m, bank[:, 1, 0:32], 0))
            g = m.vecs[:, V_PREMIX:V_PREMIX + KD].unsqueeze(2).to_broadcast([P, KD, 2])
            dve.scalar_tensor_tensor(out=m.a1[:, :, :], in0=m.mod[:, 8:16, :], scalar=1.0, in1=g,
                                     op0=ALU.add, op1=ALU.mult)


def hidden_transposed(nc, m, I):
    bank, hT, xn = m.bank, m.hT, m.xn1
    turned = m.sem("h_turned")
    lat_out = m.sem("h_lat_out")
    ctx_out = m.sem("h_ctx_out")
    with nc.Block() as block:
        @block.tensor
        def _(pe):
            for k in range(KD):
                b = 2 * (k % 4)
                if k >= 4:
                    pe.wait_ge(lat_out, k - 3)
                    pe.wait_ge(ctx_out, k - 3)
                for t in range(AT):
                    o = bank[:, b + 1, t * P:(t + 1) * P] if t < CT else bank[:, b, (t - CT) * P:(t - CT + 1) * P]
                    mm = pe.transpose(o, xn[:, t, k * P:(k + 1) * P], m.ident)
                mm.then_inc(turned, 1)

        @block.vector
        def _(dve):
            for k in range(KD):
                dve.wait_ge(turned, k + 1)
                dve.tensor_scalar(hT[:, k, TC:TA], bank[:, 2 * (k % 4), :], m.a1[:, k, 0:1], m.mod[:, k, 0:1],
                                  ALU.mult, ALU.add).then_inc(lat_out, 1)

        @block.scalar
        def _(act):
            for k in range(KD):
                act.wait_ge(turned, k + 1)
                act.activation(hT[:, k, 0:TC], bank[:, 2 * (k % 4) + 1, 0:TC], ACT.Identity,
                               scale=m.a1[:, k, 1:2], bias=m.mod[:, k, 1:2]).then_inc(ctx_out, 1)


def project_in(nc, m, I):
    bank = m.bank
    h = (m.arena("hT_hi", [P, KD, TA], 98, F32R), m.scratch("hT_lo", [P, KD, TA], 32, F32R))
    bufs = [(m.scratch("in_w_hi0", [P, KD * P], 56, F32R), m.scratch("in_w_lo0", [P, KD * P], 60, F32R)),
            (m.small("in_w_hi1", [P, KD * P], 0, F32R), m.small("in_w_lo1", [P, KD * P], 4 * KB, F32R))]
    NB = len(bufs)
    units = []
    quarters = []
    for s, (name, major, ctx) in enumerate((("qT", 1, 0), ("kT", 1, 1), ("v", 0, 1), ("zf", 1, 1), ("zb", 1, 1),
                                            ("hv", 0, 1), ("hqT", 1, 0), ("hg", 0, 0))):
        dst = m.proj[name]
        off = 0 if ctx else TC
        made = [len(units) + t for t in range(AT if ctx else TT)]
        if not major:
            units += [(off + t * P, COLS, dst[:, t, :]) for t in range(len(made))]
        for i in range(4):
            if major:
                made = [len(units) + n for n in range(2 if ctx else 1)]
                units.append((TC, T, dst[:, i, TC - off:TC - off + T]))
                if ctx:
                    units.append((0, TC, dst[:, i, 0:TC]))
            quarters.append((S_IN + s, i, not major, made))
    NQ = len(quarters)
    h_hi, h_lo = m.sem("h_hi_ready"), m.sem("h_lo_ready")
    w_hi, w_lo = m.sem("in_w_hi_ready"), m.sem("in_w_lo_ready")
    part_done = m.sem("in_part_done")
    product = m.sem("in_product")
    act_out = m.sem("in_act_out")
    dve_out = m.sem("in_dve_out")

    def completes(q):
        return not quarters[q][2] or quarters[q][1] == 3

    def used(q):
        if completes(q):
            return product, quarters[q][3][-1] + 1
        return part_done, sum(not completes(j) for j in range(q + 1))

    with nc.Block() as block:
        @block.sync
        def _(sp):
            stream(sp, m, I, S_IN + 2, S_REST + 2, lambda s: (w_lo, 4 * (s - S_IN + 1)))
            stream(sp, m, I, S_REST + 2, S_REST + RING, lambda s: (product, len(units)))

        @block.tensor
        def _(pe):
            for q, (s, i, by_rows, made) in enumerate(quarters):
                pe.wait_ge(w_lo, q + 1)
                hi, lo = [shaped(b, by_rows) for b in bufs[q % NB]]
                for u in made:
                    t0, n, _ = units[u]
                    if u >= 8 and not (by_rows and i):
                        pe.wait_ge((act_out, dve_out)[u % 2], u // 2 - 3)
                    if by_rows:
                        for k in range(2):
                            tok = slice(t0, t0 + P)
                            mm = product3(pe, bank[:, u % 8, :], (h[0][:, 2 * i + k, tok], h[1][:, 2 * i + k, tok]),
                                          (hi[:, k, :], lo[:, k, :]), i == 0 and k == 0, i == 3 and k == 1)
                    else:
                        for k in range(KD):
                            if u == 0:
                                pe.wait_ge(h_lo, k + 1)
                            mm = product3(pe, bank[:, u % 8, 0:n], (hi[:, k, :], lo[:, k, :]),
                                          (h[0][:, k, t0:t0 + n], h[1][:, k, t0:t0 + n]), k == 0, k == KD - 1)
                    if completes(q):
                        mm.then_inc(product, 1)
                if not completes(q):
                    mm.then_inc(part_done, 1)

        @block.scalar
        def _(act):
            def leading(q):
                s, i, by_rows, _ = quarters[q]
                slab_wait(act, m, s)
                if q >= NB:
                    act.wait_ge(*used(q - NB))
                act.activation(shaped(bufs[q % NB][0], by_rows), slab_part(m, s, i, by_rows), ACT.Copy).then_inc(w_hi, 1)

            leading(0)
            for k in range(KD):
                act.activation(h[0][:, k, :], m.hT[:, k, :], ACT.Copy).then_inc(h_hi, 1)
            leading(1)
            for q in range(NQ):
                if q + NB < NQ:
                    leading(q + NB)
                for u in quarters[q][3] if completes(q) else []:
                    if u % 2 == 0:
                        act.wait_ge(product, u + 1)
                        act.activation(units[u][2], bank[:, u % 8, 0:units[u][1]], ACT.Copy).then_inc(act_out, 1)

        @block.vector
        def _(dve):
            def rest(q):
                s, i, by_rows, _ = quarters[q]
                dve.wait_ge(w_hi, q + 1)
                hi, lo = [shaped(b, by_rows) for b in bufs[q % NB]]
                dve.tensor_tensor(lo, slab_part(m, s, i, by_rows), hi, ALU.subtract).then_inc(w_lo, 1)

            rest(0)
            for k in range(KD):
                dve.wait_ge(h_hi, k + 1)
                dve.tensor_tensor(h[1][:, k, :], m.hT[:, k, :], h[0][:, k, :], ALU.subtract).then_inc(h_lo, 1)
            rest(1)
            for q in range(NQ):
                if q + NB < NQ:
                    rest(q + NB)
                for u in quarters[q][3] if completes(q) else []:
                    if u % 2 == 1:
                        dve.wait_ge(product, u + 1)
                        dve.tensor_copy(units[u][2], bank[:, u % 8, 0:units[u][1]]).then_inc(dve_out, 1)


def rotary(nc, m, I):
    bank, q, k = m.bank, m.proj["qT"], m.proj["kT"]
    tmp = m.arena("rot_sin", [P, 2, T], 92)
    lv = m.arena("lambda_vecs", [P, 4, HD], 96)
    lp = m.arena("lambda_prod", [P, 2, HD], 97)
    le = m.arena("lambda_exp", [P, 4], 97.5)
    units = [q[:, h, :] for h in range(HEADS)] + [k[:, h, TC:TA] for h in range(HEADS)]
    lam_in = m.sem("lam_in")
    turned = m.sem("rot_turned")
    by_cos = m.sem("rot_by_cos")
    by_sin = m.sem("rot_by_sin")
    lam_step = m.sem("lam_step")
    lam_exp = m.sem("lam_exp")
    with nc.Block() as block:
        @block.sync
        def _(sp):
            for n, name in enumerate(("q1", "k1", "q2", "k2")):
                sp.dma_start(lv[:, n, :], I["da_lambda_" + name].partition_broadcast(P)).then_inc(lam_in, 16)
            sp.wait_ge(lam_in, 64)

        @block.tensor
        def _(pe):
            for u, x in enumerate(units):
                pe.matmul(bank[:, u, :], m.rot, x, start=True, stop=True).then_inc(turned, 1)

        @block.gpsimd
        def _(pool):
            for u, x in enumerate(units):
                pool.wait_ge(turned, u + 1)
                pool.tensor_tensor(x, x, m.cos, ALU.mult).then_inc(by_cos, 1)

        @block.vector
        def _(dve):
            dve.wait_ge(lam_in, 64)
            pairs = lv[:, :, :].rearrange("p (a b) d -> p b a d", b=2)
            dve.tensor_tensor(lp[:, :, :], pairs[:, 0], pairs[:, 1], ALU.mult).then_inc(lam_step, 1)
            dve.wait_ge(lam_step, 1)
            dve.tensor_reduce(le[:, 0:2], lp[:, :, :], AX.X, ALU.add).then_inc(lam_step, 1)
            for u, x in enumerate(units):
                dve.wait_ge(turned, u + 1)
                dve.tensor_tensor(tmp[:, u % 2, :], bank[:, u, :], m.sin, ALU.mult).then_inc(by_sin, 1)
                dve.wait_ge(by_sin, u + 1)
                dve.wait_ge(by_cos, u + 1)
                dve.tensor_tensor(x, x, tmp[:, u % 2, :], ALU.add)
            dve.wait_ge(lam_exp, 1)
            dve.tensor_tensor(m.neg_lam[:, :], le[:, 3:4], le[:, 2:3], ALU.subtract).then_inc(lam_step, 1)
            dve.wait_ge(lam_step, 3)
            dve.tensor_scalar(m.neg_lam[:, :], m.neg_lam[:, :], -LAMBDA_INIT, None, ALU.add)

        @block.scalar
        def _(act):
            act.wait_ge(lam_step, 2)
            act.activation(le[:, 2:4], le[:, 0:2], ACT.Exp).then_inc(lam_exp, 1)


def attention(nc, m, I):
    bank, q, k, v, out = m.bank, m.proj["qT"], m.proj["kT"], m.proj["v"], m.mix_da
    HALF = TA // 2
    SCALE = HD ** -0.5
    units = [(h, t) for h in range(HEADS) for t in range(TT)]
    N = len(units)
    e = m.arena("exp_scores", [P, 2, 2, TA], 92)
    a2 = m.arena("second_softmax", [P, TA], 104)
    a = m.arena("softmax_diff", [P, 2, TA], 107)
    aT = m.arena("softmax_diff_T", [P, 2, TA], 113)
    st = m.arena("softmax_stats", [P, 5, N, 2], 119)
    mx, nb, rs, ri, rl = [st[:, i] for i in range(5)]
    scores_ready = m.sem("scores_ready")
    max_ready = m.sem("max_ready")
    bias_ready = m.sem("bias_ready")
    exp_ready = m.sem("exp_ready")
    inv_ready = m.sem("inv_ready")
    second_ready = m.sem("second_ready")
    diff_ready = m.sem("diff_ready")
    turned = m.sem("diff_turned")
    diffT_ready = m.sem("diffT_ready")
    pv_ready = m.sem("pv_ready")
    pv_out = m.sem("pv_out")
    with nc.Block() as block:
        @block.tensor
        def _(pe):
            for n in range(-1, N + 2):
                if n + 1 < N:
                    h, t = units[n + 1]
                    for i in range(2):
                        r = slice(HD * i, HD * (i + 1))
                        if n >= 0:
                            pe.wait_ge(exp_ready, 2 * n + 1 + i)
                        for half in range(2):
                            mm = pe.matmul(bank[:, 2 * i + half, 0:HALF], q[r, h, t * P:(t + 1) * P],
                                           k[r, h, half * HALF:(half + 1) * HALF], start=True, stop=True)
                        mm.then_inc(scores_ready, 1)
                if n >= 2:
                    w = n - 2
                    h = units[w][0]
                    pe.wait_ge(diffT_ready, w + 1)
                    if w >= 2:
                        pe.wait_ge(pv_out, w - 1)
                    for j in range(AT):
                        mm = pe.matmul(bank[:, 6 + w % 2, 0:P], aT[:, w % 2, j * P:(j + 1) * P], v[:, j, h * P:(h + 1) * P],
                                       start=(j == 0), stop=(j == AT - 1))
                    mm.then_inc(pv_ready, 1)
                if 1 <= n <= N:
                    w = n - 1
                    pe.wait_ge(diff_ready, w + 1)
                    for j in range(AT):
                        mm = pe.transpose(bank[:, 4 + j // 3, (j % 3) * P:(j % 3 + 1) * P], a[:, w % 2, j * P:(j + 1) * P], m.ident)
                    mm.then_inc(turned, 1)

        @block.scalar
        def _(act):
            def exp_of(n, i):
                act.wait_ge(bias_ready, 2 * n + i + 1)
                if n >= 2:
                    act.wait_ge(diff_ready, n - 1)
                act.activation(e[:, n % 2, i, :].rearrange("p (a n) -> p a n", a=2), bank[:, 2 * i:2 * i + 2, 0:HALF],
                               ACT.Exp, bias=nb[:, n, i:i + 1], scale=SCALE,
                               accum_out=rs[:, n, i:i + 1]).then_inc(exp_ready, 1)

            for n in range(-1, N + 2):
                if n + 1 < N:
                    exp_of(n + 1, 0)
                if 0 <= n < N:
                    act.wait_ge(inv_ready, 2 * n + 2)
                    if n >= 1:
                        act.wait_ge(diff_ready, n)
                    act.activation(a2[:, :], e[:, n % 2, 1, :], ACT.Copy, scale=rl[:, n, 1:2]).then_inc(second_ready, 1)
                if n + 1 < N:
                    exp_of(n + 1, 1)
                if n >= 2:
                    w = n - 2
                    h, t = units[w]
                    act.wait_ge(pv_ready, w + 1)
                    act.activation(out[:, t, h * P:(h + 1) * P], bank[:, 6 + w % 2, 0:P], ACT.Copy).then_inc(pv_out, 1)
                if 1 <= n <= N:
                    w = n - 1
                    act.wait_ge(turned, w + 1)
                    act.activation(aT[:, w % 2, :].rearrange("p (a n) -> p a n", a=2), bank[:, 4:6, 0:HALF],
                                   ACT.Copy).then_inc(diffT_ready, 1)

        @block.vector
        def _(dve):
            def bias_of(n, i):
                dve.wait_ge(scores_ready, 2 * n + i + 1)
                dve.tensor_reduce(mx[:, n, i:i + 1], bank[:, 2 * i:2 * i + 2, 0:HALF], AX.XY, ALU.max).then_inc(max_ready, 1)
                dve.wait_ge(max_ready, 2 * n + i + 1)
                dve.tensor_scalar(nb[:, n, i:i + 1], mx[:, n, i:i + 1], -SCALE, None, ALU.mult).then_inc(bias_ready, 1)

            for n in range(-1, N):
                if n + 1 < N:
                    bias_of(n + 1, 0)
                if n >= 0:
                    dve.wait_ge(exp_ready, 2 * n + 2)
                    dve.reciprocal(ri[:, n, :], rs[:, n, :]).then_inc(inv_ready, 1)
                    dve.wait_ge(inv_ready, 2 * n + 1)
                    dve.tensor_scalar(rl[:, n, 1:2], ri[:, n, 1:2], m.neg_lam[:, :], None, ALU.mult).then_inc(inv_ready, 1)
                if n + 1 < N:
                    bias_of(n + 1, 1)
                if n >= 0:
                    dve.wait_ge(second_ready, n + 1)
                    if n >= 2:
                        dve.wait_ge(turned, n - 1)
                    dve.scalar_tensor_tensor(out=a[:, n % 2, :], in0=e[:, n % 2, 0, :], scalar=ri[:, n, 0:1], in1=a2[:, :],
                                             op0=ALU.mult, op1=ALU.add).then_inc(diff_ready, 1)



def forget_gates(nc, m, I):
    z = (m.proj["zf"], m.proj["zb"])
    diff = m.arena("lb_diff", [P, 8], 0)
    lb = m.arena("lb", [P, 8], 0.125)
    rest = m.arena("lb_rest", [P, 8], 0.25)
    diff_ready = m.sem("lb_diff_ready")
    sig_ready = m.sem("forget_sig_ready")
    lb_step = m.sem("lb_step")
    scb = m.arena("silu_c_wide", [P, KD, P], 2)
    gb = m.arena("gate_bias", [P, 2, D], 6)
    gp = m.arena("gate_norm", [P, 2, D], 14)
    gates_in = m.sem("gates_in")
    wide_ready = m.sem("silu_wide_ready")
    rest_done = m.sem("rest_done")
    rest_step = m.sem("rest_step")
    bank = m.bank
    with nc.Block() as block:
        @block.sync
        def _(sp):
            for n, (at, name) in enumerate(((2, "norm_post_mix"), (5, "norm_post_ffn"))):
                sp.dma_start(gb[:, n, :], I["b_ada"][0:1, at * D:(at + 1) * D].partition_broadcast(P)).then_inc(gates_in, 16)
                sp.dma_start(gp[:, n, :], I[name][0:1, :].partition_broadcast(P)).then_inc(gates_in, 16)
            stream(sp, m, I, S_REST + RING, S_OUT + RING, lambda s: (rest_done, s - S_REST + 1))

        @block.tensor
        def _(pe):
            pe.wait_ge(wide_ready, 1)
            for s in range(S_REST, S_OUT):
                j = s - S_REST
                w = m.ring[:, s % RING]
                slab_wait(pe, m, s)
                if 2 <= j < 6:
                    mm = shift_scale(pe, m, bank[:, 4, :], w, j - 2)
                else:
                    for k in range(KD):
                        mm = pe.matmul(bank[:, j if j < 2 else j - 4, :], scb[:, k, :], w[:, k, :],
                                       start=(k == 0), stop=(k == KD - 1))
                mm.then_inc(rest_done, 1)

        @block.scalar
        def _(act):
            act.wait_ge(diff_ready, 1)
            act.activation(lb[:, :], diff[:, :], ACT.Sigmoid).then_inc(sig_ready, 1)
            for d in range(2):
                act.activation(z[d][:, :, :], z[d][:, :, :], ACT.Sigmoid).then_inc(sig_ready, 1)

        @block.vector
        def _(dve):
            dve.tensor_copy(scb[:, :, :], m.silu_c[:, :, 0:1].to_broadcast([P, KD, P])).then_inc(wide_ready, 1)
            dve.tensor_tensor(diff[:, :], m.vecs[:, V_LB:V_LB + 8], m.vecs[:, V_LB + 8:V_LB + 16], ALU.subtract).then_inc(diff_ready, 1)
            dve.wait_ge(sig_ready, 1)
            dve.tensor_scalar(rest[:, :], lb[:, :], -1.0, 1.0, ALU.mult, ALU.add).then_inc(lb_step, 1)
            dve.wait_ge(lb_step, 1)
            for d in range(2):
                dve.wait_ge(sig_ready, 2 + d)
                for h in range(HEADS):
                    n = HEADS * d + h
                    dve.tensor_scalar(z[d][:, h, :], z[d][:, h, :], rest[:, n:n + 1], lb[:, n:n + 1], ALU.mult, ALU.add)
            link = chain(dve, rest_step)
            dve.wait_ge(gates_in, 4 * 16)
            for half, (gate, b, slabs) in enumerate(((m.gate1, 0, 2), (m.gate2, 2, 8))):
                dve.wait_ge(rest_done, slabs)
                link(dve.tensor_tensor(gate[:, :], bank[:, b:b + 2, :].rearrange("p a n -> p (a n)"), gb[:, half, :], ALU.add))
                dve.tensor_tensor(gate[:, :], gate[:, :], gp[:, half, :], ALU.mult)
            link(add_bias(dve, m, bank[:, 4, 0:32], 1))
            dve.scalar_tensor_tensor(out=m.a2[:, :], in0=m.mod[:, 24:32, 0], scalar=1.0,
                                     in1=m.vecs[:, V_PREFFN:V_PREFFN + KD], op0=ALU.add, op1=ALU.mult)


def recurrence(nc, m, I, d):
    bank, q, hv = m.bank, m.proj["hqT"], m.proj["hv"]
    reach, other = (m.proj["zf"], m.proj["zb"]) if d == 0 else (m.proj["zb"], m.proj["zf"])
    k = m.arena(f"hk{d}", [P, HEADS, TA], 0)
    left = m.arena(f"left{d}", [P, HEADS, TA], 12)
    scores = m.scores
    X = m.arena(f"hX{d}", [P, 2, HEADS, T], 92)
    ends = m.arena(f"ends{d}", [P, HEADS, AT], 118.5 + d * 0.25)
    kT = m.arena(f"hkT{d}", [P, AT, COLS], 12)
    S = m.states[d]
    qh, kh = (1, 0) if d == 0 else (0, 1)
    nL = len(LEVELS)
    diag = 1 if d == 0 else 0
    rounds = diag + nL
    order = [0, 1, 2, 3, 4] if d == 0 else [1, 0, 5, 4, 3]

    def halves(t, L):
        return t[:, :, :].rearrange("p h t -> p (h t)").rearrange("p (n two l) -> p n two l", two=2, l=L)

    def lat_halves(t, L, at=0):
        return t[:, :, at:at + T].rearrange("p h (n two l) -> p h n two l", two=2, l=L)

    def total(t, L, half):
        at = L - 1 if d == 0 else 0
        v = halves(t, L)[:, :, half, at:at + 1]
        return v.to_broadcast([P, v.shape[1], L])

    def name(x):
        return m.sem(f"{x}{d}")

    k_ready, ones_set, diag_ready = name("hk_ready"), name("left_ones"), name("diag_ready")
    q_side, k_side, product, read_out = name("q_side"), name("k_side"), name("h_product"), name("h_read_out")
    left_grown, reach_grown, ends_kept = name("left_grown"), name("reach_grown"), name("ends_kept")
    k_last, k_turned, kT_ready, q_last = name("k_last"), name("k_turned"), name("hkT_ready"), name("q_last")
    gain, state = name("state_gain"), name("state_ready")
    with nc.Block() as block:
        @block.gpsimd
        def _(pool):
            pool.memset(left[:, :, :], 1.0).then_inc(ones_set, 1)
            pool.wait_ge(ones_set, 1)
            pool.wait_ge(k_ready, 1)
            for l, L in enumerate(LEVELS):
                r = l + diag
                if l >= 1:
                    pool.wait_ge(left_grown, l)
                if r >= 2:
                    pool.wait_ge(product, r - 1)
                x = X[:, r % 2].rearrange("p h (n two l) -> p h n two l", two=2, l=L)
                for h in range(HEADS):
                    ins = pool.tensor_tensor(x[:, h, :, kh, :], lat_halves(k, L, TC)[:, h, :, kh, :],
                                             lat_halves(left, L, TC)[:, h, :, kh, :], ALU.mult)
                ins.then_inc(k_side, 1)
                pool.wait_ge(k_side, l + 1)
                if l >= 1:
                    pool.wait_ge(reach_grown, l)
                pool.tensor_tensor(halves(left, L)[:, :, kh, :], halves(left, L)[:, :, kh, :],
                                   total(reach, L, qh), ALU.mult).then_inc(left_grown, 1)
            pool.wait_ge(left_grown, nL)
            pool.tensor_tensor(k[:, :, :], k[:, :, :], left[:, :, :], ALU.mult).then_inc(k_last, 1)

        @block.vector
        def _(dve):
            dve.tensor_scalar(k[:, :, :], reach[:, :, :], -1.0, 1.0, ALU.mult, ALU.add).then_inc(k_ready, 1)
            if diag:
                dve.wait_ge(k_ready, 1)
                dve.tensor_tensor(X[:, 0], k[:, :, TC:TA], other[:, :, TC:TA], ALU.subtract).then_inc(diag_ready, 1)
                dve.wait_ge(diag_ready, 1)
                dve.tensor_scalar(X[:, 0], X[:, 0], 1.0, None, ALU.add).then_inc(diag_ready, 1)

            def read(r):
                dve.wait_ge(product, r + 1)
                if r >= 1:
                    dve.wait_ge(read_out, r)
                for h in range(HEADS):
                    src = bank[:, 4 * (r % 2) + h, :].rearrange("p (c t) -> p c t", c=TT)
                    dst = scores[:, h, :].rearrange("p (c t) -> p c t", c=TT)
                    if r < diag:
                        ins = dve.tensor_tensor(dst, src, m.ident.unsqueeze(1).to_broadcast([P, TT, P]), ALU.mult)
                    else:
                        mask = m.masks[:, nL * d + r - diag, :].unsqueeze(1).to_broadcast([P, TT, P])
                        ins = dve.copy_predicated(dst, mask, src)
                ins.then_inc(read_out, 1)

            for l, L in enumerate(LEVELS):
                r = l + diag
                if l >= 1:
                    dve.wait_ge(reach_grown, l)
                if r >= 2:
                    dve.wait_ge(product, r - 1)
                x = X[:, r % 2].rearrange("p h (n two l) -> p h n two l", two=2, l=L)
                dve.tensor_tensor(x[:, :, :, qh, :], lat_halves(q, L)[:, :, :, qh, :],
                                  lat_halves(reach, L, TC)[:, :, :, qh, :], ALU.mult).then_inc(q_side, 1)
                if r >= 1:
                    read(r - 1)
                dve.wait_ge(left_grown, l + 1)
                dve.wait_ge(q_side, l + 1)
                dve.tensor_tensor(halves(reach, L)[:, :, qh, :], halves(reach, L)[:, :, qh, :],
                                  total(reach, L, kh), ALU.mult).then_inc(reach_grown, 1)
            read(rounds - 1)
            dve.wait_ge(reach_grown, nL)
            at = P - 1 if d == 0 else 0
            dve.tensor_copy(ends[:, :, :], reach[:, :, :].rearrange("p h (c t) -> p h c t", t=P)[:, :, :, at]).then_inc(ends_kept, 1)
            dve.wait_ge(ends_kept, 1)
            dve.tensor_tensor(reach[:, :, TC:TA], reach[:, :, TC:TA], q[:, :, :], ALU.mult).then_inc(q_last, 1)
            for j, c in enumerate(order):
                dve.wait_ge(gain, j + 1)
                if j == 0:
                    dve.tensor_copy(S[:, 0], bank[:, j, :]).then_inc(state, 1)
                    continue
                dve.wait_ge(state, j)
                for h in range(HEADS):
                    cut = slice(h * P, (h + 1) * P)
                    ins = dve.scalar_tensor_tensor(out=S[:, j, cut], in0=S[:, j - 1, cut], scalar=ends[:, h, c:c + 1],
                                                   in1=bank[:, j, cut], op0=ALU.mult, op1=ALU.add)
                ins.then_inc(state, 1)

        @block.tensor
        def _(pe):
            for r in range(rounds):
                if r < diag:
                    pe.wait_ge(diag_ready, 2)
                else:
                    pe.wait_ge(q_side, r - diag + 1)
                    pe.wait_ge(k_side, r - diag + 1)
                if r >= 2:
                    pe.wait_ge(read_out, r - 1)
                for h in range(HEADS):
                    for c in range(TT):
                        cut = slice(c * P, (c + 1) * P)
                        x = X[:, r % 2, h, cut]
                        mm = pe.matmul(bank[:, 4 * (r % 2) + h, cut], x, q[:, h, cut] if r < diag else x,
                                       start=True, stop=True)
                mm.then_inc(product, 1)
            pe.wait_ge(k_last, 1)
            pe.wait_ge(read_out, rounds)
            for c in range(AT):
                for h in range(HEADS):
                    mm = pe.transpose(bank[:, c, h * P:(h + 1) * P], k[:, h, c * P:(c + 1) * P], m.ident)
                mm.then_inc(k_turned, 1)
            for j, c in enumerate(order):
                pe.wait_ge(kT_ready, AT)
                for h in range(HEADS):
                    cut = slice(h * P, (h + 1) * P)
                    mm = pe.matmul(bank[:, j, cut], kT[:, c, cut], hv[:, c, cut], start=True, stop=True)
                mm.then_inc(gain, 1)

        @block.scalar
        def _(act):
            for c in range(AT):
                act.wait_ge(k_turned, c + 1)
                act.activation(kT[:, c, :], bank[:, c, :], ACT.Copy).then_inc(kT_ready, 1)


def recurrence_forward(nc, m, I):
    recurrence(nc, m, I, 0)


def recurrence_backward(nc, m, I):
    recurrence(nc, m, I, 1)


def mix_outputs(nc, m, I):
    bank, hv, hg, da = m.bank, m.proj["hv"], m.proj["hg"], m.mix_da
    nu = TT * HEADS
    sq = m.arena("mix_square", [P, 2, TT, COLS], 0)
    sg = m.arena("mix_sig", [P, TT, COLS], 16)
    o = m.arena("mix_o", [P, TT, COLS], 24)
    w = m.arena("mix_norm_w", [P, 2, P], 119.5)
    ss = m.arena("mix_ss", [P, 2, nu], 120.5)
    sd = m.arena("mix_sd", [P, 2, nu], 120.75)
    rstd = m.arena("mix_rstd", [P, 2, nu], 121)
    w_in = m.sem("mix_w_in")
    w_ready = m.sem("mix_w_ready")
    o_ready = m.sem("mix_o_ready")
    squared = m.sem("mix_squared")
    summed = m.sem("mix_summed")
    rooted = m.sem("mix_rooted")
    rstd_ready = m.sem("mix_rstd_ready")
    silu_ready = m.sem("mix_silu_ready")
    step = m.sem("mix_step")

    def heads(t):
        return t.rearrange("p t (h v) -> p (t h) v", v=P)

    def wide(v):
        return v.unsqueeze(2).to_broadcast([P, nu, P])

    with nc.Block() as block:
        @block.sync
        def _(sp):
            sp.dma_start(w[:, 0, :], I["da_subln"].partition_broadcast(P)).then_inc(w_in, 16)
            sp.dma_start(w[:, 1, :], I["hg_norm"].partition_broadcast(P)).then_inc(w_in, 16)
            sp.wait_ge(w_in, 32)

        @block.tensor
        def _(pe):
            for c in range(TT):
                lat = slice(TC + c * P, TC + (c + 1) * P)
                for h in range(HEADS):
                    cut = slice(h * P, (h + 1) * P)
                    pe.matmul(bank[:, c, cut], m.scores[:, h, c * P:(c + 1) * P], hv[:, CT + c, cut], start=True, stop=False)
                    pe.matmul(bank[:, c, cut], m.proj["zf"][:, h, lat], m.states[0][:, 1 + c, cut], start=False, stop=False)
                    mm = pe.matmul(bank[:, c, cut], m.proj["zb"][:, h, lat], m.states[1][:, 1 + TT - 1 - c, cut], start=False, stop=True)
            mm.then_inc(o_ready, 1)

        @block.scalar
        def _(act):
            act.activation(sq[:, 0], da[:, :, :], ACT.Square).then_inc(squared, 1)
            act.activation(sg[:, :, :], hg[:, :, :], ACT.Sigmoid).then_inc(silu_ready, 1)
            act.wait_ge(o_ready, 1)
            act.activation(sq[:, 1], bank[:, 0:TT, :], ACT.Square).then_inc(squared, 1)
            act.wait_ge(summed, 2)
            act.activation(sd[:, :, :], ss[:, :, :], ACT.Sqrt, bias=m.eps[:, :], scale=1.0 / P).then_inc(rooted, 1)

        @block.gpsimd
        def _(pool):
            pool.wait_ge(silu_ready, 1)
            pool.tensor_tensor(hg[:, :, :], hg[:, :, :], sg[:, :, :], ALU.mult).then_inc(silu_ready, 1)

        @block.vector
        def _(dve):
            link = chain(dve, step)
            dve.wait_ge(w_in, 32)
            dve.tensor_scalar(w[:, 0, :], w[:, 0, :], 1.0 - LAMBDA_INIT, None, ALU.mult).then_inc(w_ready, 1)
            for i in range(2):
                dve.wait_ge(squared, i + 1)
                dve.tensor_reduce(ss[:, i, :], heads(sq[:, i]), AX.X, ALU.add).then_inc(summed, 1)
            dve.wait_ge(rooted, 1)
            link(dve.reciprocal(rstd[:, :, :], sd[:, :, :]))
            dve.wait_ge(w_ready, 1)
            for src, dst, i in ((bank[:, 0:TT, :], o[:, :, :], 1), (da[:, :, :], da[:, :, :], 0)):
                link(dve.tensor_tensor(heads(dst), heads(src), wide(rstd[:, i, :]), ALU.mult))
                link(dve.tensor_tensor(heads(dst), heads(dst), w[:, i, :].unsqueeze(1).to_broadcast([P, nu, P]), ALU.mult))
            dve.wait_ge(silu_ready, 2)
            dve.tensor_tensor(hg[:, :, :], hg[:, :, :], o[:, :, :], ALU.mult)


def turn_features(nc, m, tag, sources, dst, scale=None, shift=None, loads=None):
    bank = m.bank
    turned = m.sem(f"{tag}_turned")
    out = [m.sem(f"{tag}_out{i}") for i in range(2)]
    with nc.Block() as block:
        if loads is not None:
            @block.sync
            def _(sp):
                loads(sp)

        @block.tensor
        def _(pe):
            for k, tiles in enumerate(sources):
                for t, src in enumerate(tiles):
                    mm = pe.transpose(bank[:, k, t * P:(t + 1) * P], src, m.ident)
                mm.then_inc(turned, 1)

        @block.scalar
        def _(act):
            for k in range(0, KD, 2):
                act.wait_ge(turned, k + 1)
                if scale is None:
                    act.activation(dst[:, k, :], bank[:, k, :], ACT.Copy).then_inc(out[0], 1)
                elif shift is None:
                    act.activation(dst[:, k, :], bank[:, k, :], ACT.Copy, scale=scale[:, k:k + 1]).then_inc(out[0], 1)
                else:
                    act.activation(dst[:, k, :], bank[:, k, :], ACT.Identity, scale=scale[:, k:k + 1],
                                   bias=shift[:, k:k + 1]).then_inc(out[0], 1)

        @block.vector
        def _(dve):
            for k in range(1, KD, 2):
                dve.wait_ge(turned, k + 1)
                if scale is None:
                    dve.tensor_copy(dst[:, k, :], bank[:, k, :]).then_inc(out[1], 1)
                elif shift is None:
                    dve.tensor_scalar(dst[:, k, :], bank[:, k, :], scale[:, k:k + 1], None, ALU.mult).then_inc(out[1], 1)
                else:
                    dve.tensor_scalar(dst[:, k, :], bank[:, k, :], scale[:, k:k + 1], shift[:, k:k + 1],
                                      ALU.mult, ALU.add).then_inc(out[1], 1)


def rows_of(t, k):
    return [t[:, i, k * P:(k + 1) * P] for i in range(TT)]


def turn_mix(nc, m, I):
    turn_features(nc, m, "mixT", [rows_of(m.mix_da, k) for k in range(4)] + [rows_of(m.proj["hg"], k) for k in range(4)], m.mixT)


def residual(nc, m, I, tag, x, xn, products, loads, x_in=None, gate=None):
    bank = m.bank
    junk = m.arena(f"{tag}_square", [P, 2, D], 16)
    st = m.arena(f"{tag}_stats", [P, 6, TT], 121.5)
    add = m.arena(f"{tag}_add", [P, 2, D], 24)

    def name(n):
        return m.sem(f"{tag}_{n}")

    ready, squared, rooted, inverse, scaled, added = map(name, ("ready", "squared", "rooted", "inverse", "scaled", "added"))
    squared2, rooted2, inverse2 = map(name, ("squared2", "rooted2", "inverse2"))
    with nc.Block() as block:
        @block.sync
        def _(sp):
            loads(sp, ready)

        @block.tensor
        def _(pe):
            products(pe, ready)

        @block.scalar
        def _(act):
            def norm(t, src, row, squares, roots):
                act.activation(junk[:, t % 2, :], src, ACT.Square, accum_out=st[:, row, t:t + 1]).then_inc(squares, 1)
                act.wait_ge(squares, t + 1)
                act.activation(st[:, row + 1, t:t + 1], st[:, row, t:t + 1], ACT.Sqrt, bias=m.eps[:, :],
                               scale=1.0 / D).then_inc(roots, 1)

            for t in range(TT):
                if gate is not None:
                    act.wait_ge(ready, t + 1)
                    norm(t, bank[:, 2 * t:2 * t + 2, :].rearrange("p a n -> p (a n)"), 0, squared, rooted)
                if t >= 1:
                    act.wait_ge(added, t)
                    norm(t - 1, x[:, t - 1, :], 3, squared2, rooted2)
            act.wait_ge(added, TT)
            norm(TT - 1, x[:, TT - 1, :], 3, squared2, rooted2)

        @block.vector
        def _(dve):
            def normal(t):
                dve.wait_ge(rooted2, t + 1)
                dve.reciprocal(st[:, 5, t:t + 1], st[:, 4, t:t + 1]).then_inc(inverse2, 1)
                dve.wait_ge(inverse2, t + 1)
                dve.tensor_scalar(xn[:, t, :], x[:, t, :], st[:, 5, t:t + 1], None, ALU.mult)

            if x_in is not None:
                dve.wait_ge(*x_in)
            for t in range(TT):
                src = bank[:, 2 * t:2 * t + 2, :].rearrange("p a n -> p (a n)")
                dve.wait_ge(ready, t + 1)
                if gate is not None:
                    dve.wait_ge(rooted, t + 1)
                    dve.reciprocal(st[:, 2, t:t + 1], st[:, 1, t:t + 1]).then_inc(inverse, 1)
                    dve.wait_ge(inverse, t + 1)
                    dve.scalar_tensor_tensor(out=add[:, t % 2, :], in0=src, scalar=st[:, 2, t:t + 1], in1=gate[:, :],
                                             op0=ALU.mult, op1=ALU.mult).then_inc(scaled, 1)
                    dve.wait_ge(scaled, t + 1)
                    src = add[:, t % 2, :]
                dve.tensor_tensor(x[:, t, :], x[:, t, :], src, ALU.add).then_inc(added, 1)
                if t >= 1:
                    normal(t - 1)
            normal(TT - 1)


def project_out(nc, m, I):
    x_in = m.sem("x_again")

    def products(pe, ready):
        for t in range(TT):
            for n in range(2):
                slab_wait(pe, m, S_OUT + n)
                for k in range(KD):
                    mm = pe.matmul(m.bank[:, 2 * t + n, :], m.mixT[:, k, t * P:(t + 1) * P], m.ring[:, (S_OUT + n) % RING, k, :],
                                   start=(k == 0), stop=(k == KD - 1))
            mm.then_inc(ready, 1)

    def loads(sp, ready):
        sp.dma_start(m.x[:, :, :], I["x"][0].rearrange("(t p) d -> p t d", p=P)).then_inc(x_in, 16)
        stream(sp, m, I, S_OUT + RING, S_EXP + RING, lambda s: (ready, TT))

    residual(nc, m, I, "out1", m.x, m.xn2, products, loads, (x_in, 16), m.gate1)


def turn_ffn(nc, m, I):
    turn_features(nc, m, "h2T", [rows_of(m.xn2, k) for k in range(KD)], m.h2T, m.a2[:, :], m.mod[:, 16:24, 0])


def route(nc, m, I):
    bank = m.bank
    E = EXPERTS
    wr = m.arena("w_router", [P, KD, E], 80)
    lg = m.arena("logits", [P, TT, E], 81)
    ex = m.arena("logit_exp", [P, TT, E], 81.5)
    aff = m.arena("affinity", [P, TT, E], 82)
    st = m.arena("router_stats", [P, 3, TT], 82.5)
    pairs = m.arena("pair_rows", [E, EXPERTS // 2, P], 112)
    affT = m.arena("affT", [E, T], 116)
    left = m.arena("aff_left", [E, T], 118)
    chosen = m.arena("chosen", [E, T], 120)
    place = m.arena("place", [E, T], 83)
    ones = m.arena("ones_row", [E, T], 85)
    top = m.arena("top8", [E, 8], 87)
    posT = m.arena("placeT", [P, TT, E], 87.5)
    wide = m.arena("aff_wide", [P, 2, T], 88)

    w_in = m.sem("router_in")
    logits = m.sem("logits_ready")
    expd = m.sem("logit_exp_ready")
    step = m.sem("router_step")
    aff_ready = m.sem("aff_ready")
    aff_turned = m.sem("aff_turned")
    affT_ready = m.sem("affT_ready")
    place_ready = m.sem("place_ready")
    place_turned = m.sem("place_turned")
    pair_rows = m.sem("pair_rows_ready")
    wide_ready = m.sem("aff_wide_ready")
    spread_ready = m.sem("spread_ready")
    logit_less = m.sem("logit_less_max")
    with nc.Block() as block:
        @block.sync
        def _(sp):
            sp.dma_start(wr[:, :, :], I["w_router"][0].rearrange("(k p) e -> p k e", p=P)).then_inc(w_in, 16)
            sp.dma_start(pairs[:, :, :], I["k_pairs"].rearrange("e (n p) -> e n p", p=P)).then_inc(w_in, 16)
            sp.wait_ge(w_in, 32)

        @block.tensor
        def _(pe):
            pe.wait_ge(w_in, 32)
            for t in range(TT):
                for k in range(KD):
                    mm = pe.matmul(bank[:, 0, t * E:(t + 1) * E], m.h2T[:, k, t * P:(t + 1) * P], wr[:, k, :],
                                   start=(k == 0), stop=(k == KD - 1))
            mm.then_inc(logits, 1)
            pe.wait_ge(aff_ready, 1)
            for t in range(TT):
                mm = pe.transpose(bank[0:E, 1, t * P:(t + 1) * P], aff[:, t, :], m.ident)
            mm.then_inc(aff_turned, 1)
            pe.wait_ge(place_ready, 1)
            for t in range(TT):
                mm = pe.transpose(bank[:, 2, t * E:(t + 1) * E], place[:, t * P:(t + 1) * P], m.ident[0:E, 0:E])
            mm.then_inc(place_turned, 1)
            for n in range(EXPERTS // 2):
                b = 4 + 2 * (n % 2)
                if n >= 2:
                    pe.wait_ge(spread_ready, n - 1)
                pe.matmul(bank[:, b, :], pairs[:, n, :], place[:, :], start=True, stop=True)
                pe.matmul(bank[:, b + 1, :], pairs[:, n, :], affT[:, :], start=True, stop=True).then_inc(pair_rows, 1)

        @block.scalar
        def _(act):
            act.wait_ge(logit_less, 1)
            act.activation(ex[:, :, :], lg[:, :, :], ACT.Exp).then_inc(expd, 1)
            for n in range(EXPERTS // 2):
                act.wait_ge(pair_rows, n + 1)
                if n >= 2:
                    act.wait_ge(spread_ready, n - 1)
                act.activation(wide[:, n % 2, :], bank[:, 5 + 2 * (n % 2), :], ACT.Copy).then_inc(wide_ready, 1)

        @block.vector
        def _(dve):
            link = chain(dve, step)
            dve.memset(ones[:, :], 1.0)
            dve.wait_ge(logits, 1)
            raw = bank[:, 0, 0:TT * E].rearrange("p (t e) -> p t e", e=E)
            link(dve.tensor_reduce(st[:, 0, :], raw, AX.X, ALU.max))
            dve.tensor_tensor(lg[:, :, :], raw, st[:, 0, :].unsqueeze(2).to_broadcast([P, TT, E]), ALU.subtract).then_inc(logit_less, 1)
            dve.wait_ge(expd, 1)
            link(dve.tensor_reduce(st[:, 1, :], ex[:, :, :], AX.X, ALU.add))
            link(dve.reciprocal(st[:, 2, :], st[:, 1, :]))
            dve.tensor_tensor(aff[:, :, :], ex[:, :, :], st[:, 2, :].unsqueeze(2).to_broadcast([P, TT, E]), ALU.mult).then_inc(aff_ready, 1)
            dve.wait_ge(aff_turned, 1)
            dve.tensor_copy(affT[:, :], bank[0:E, 1, :]).then_inc(affT_ready, 1)
            link(dve.tensor_copy(left[:, :], bank[0:E, 1, :]))
            for _ in range(CAP // 8):
                link(dve.max(top[:, :], left[:, :]))
                link(dve.match_replace(left[:, :], top[:, :], left[:, :], -1.0))
            link(dve.tensor_scalar(chosen[:, :], left[:, :], 0.0, None, ALU.is_lt))
            link(dve.tensor_tensor_scan(place[:, :], ones[:, :], chosen[:, :], 0.0, ALU.mult, ALU.add))
            dve.tensor_tensor(place[:, :], place[:, :], chosen[:, :], ALU.mult).then_inc(place_ready, 1)
            dve.wait_ge(place_turned, 1)
            link(dve.tensor_copy(posT[:, :, :], bank[:, 2, 0:TT * E].rearrange("p (t e) -> p t e", e=E)))
            for t in range(TT):
                dve.tensor_tensor(m.onehot[:, t, :].rearrange("p (e c) -> p e c", c=CAP),
                                  m.slot.unsqueeze(1).to_broadcast([P, E, CAP]),
                                  posT[:, t, :].unsqueeze(2).to_broadcast([P, E, CAP]), ALU.is_equal)
            for n in range(EXPERTS // 2):
                dve.wait_ge(wide_ready, n + 1)
                dve.scalar_tensor_tensor(out=m.spread[:, n, :], in0=bank[:, 4 + 2 * (n % 2), :], scalar=m.slot_col,
                                         in1=wide[:, n % 2, :], op0=ALU.is_equal, op1=ALU.mult).then_inc(spread_ready, 1)


def experts(nc, m, I):
    bank = m.bank
    H = CAP
    PAIRS = EXPERTS // 2
    xin = m.arena("xinT", [P, KD, P], 16)
    sig = m.arena("gate_sig", [P, COLS], 20)
    hid = m.arena("expert_hidden", [P, COLS], 22)
    hidT = m.arena("expert_hiddenT", [P, 4, P], 24)

    gathered = m.sem("gathered")
    xin_a = m.sem("xin_by_act")
    xin_v = m.sem("xin_by_dve")
    g_ready = m.sem("expert_gate")
    u_ready = m.sem("expert_up")
    y_ready = m.sem("expert_down")
    sig_ready = m.sem("expert_sig")
    silu_ready = m.sem("expert_silu")
    hid_ready = m.sem("expert_hid")
    hid_turned = m.sem("expert_hid_turned")
    hidT_ready = m.sem("expert_hidT")
    y_free_a = m.sem("y_free_by_act")
    y_free_v = m.sem("y_free_by_dve")

    def landed(pe, i, j):
        s = S_EXP + j
        pe.wait_ge(m.slab_loaded[s % RING], i * (16 * 12 // RING) + 16 * loads_of(s))

    with nc.Block() as block:
        @block.sync
        def _(sp):
            done = (g_ready, u_ready, y_ready)
            with sp.Fori(0, PAIRS - 1) as i:
                for j in range(12):
                    sp.wait_ge(done[j % 6 // 2], i * 2 + (j // 6 + 1))
                    s = S_EXP + RING + j
                    e, q = divmod(RING + j, 6)
                    w = I[("w_gate", "w_up", "w_down")[q // 2]][0, bass.ds(i * 2 + e, 1), :, (q % 2) * COLS:(q % 2 + 1) * COLS]
                    sp.dma_start(m.ring[:, s % RING], w.rearrange("o (k p) n -> p (o k) n", p=P)).then_inc(m.slab_loaded[s % RING], 16)
            stream(sp, m, I, S_GIN - 12 + RING, S_GIN + RING,
                   lambda s: (done[(s - S_EXP) % 6 // 2], (s - S_EXP) // 6 + 1))

        @block.tensor
        def _(pe):
            def gather(i):
                for k in range(KD):
                    for t in range(TT):
                        mm = pe.matmul(bank[:, k // 4, (k % 4) * P:(k % 4 + 1) * P], m.xn2[:, t, k * P:(k + 1) * P],
                                       m.onehot[:, t, bass.ds(i * P, P)], start=(t == 0), stop=(t == TT - 1))
                mm.then_inc(gathered, 1)

            def pair(i, last):
                pe.wait_ge(xin_a, i + 1)
                pe.wait_ge(xin_v, i + 1)
                for r in range(2):
                    for q, (b, ready) in enumerate(((2, g_ready), (3, u_ready))):
                        landed(pe, i, 6 * r + 2 * q)
                        landed(pe, i, 6 * r + 2 * q + 1)
                        for k in range(KD):
                            for half in range(2):
                                w = m.ring[:, (S_EXP + 6 * r + 2 * q + half) % RING]
                                mm = pe.matmul(bank[half * H:(half + 1) * H, b, :], xin[:, k, r * H:(r + 1) * H], w[:, k, :],
                                               start=(k == 0), stop=(k == KD - 1), skip_group_check=True)
                        mm.then_inc(ready, 1)
                    if r == 1 and not last:
                        gather(i + 1)
                    pe.wait_ge(hid_ready, i * 2 + (r + 1))
                    for c in range(4):
                        mm = pe.transpose(bank[:, 6, c * P:(c + 1) * P], hid[:, c * P:(c + 1) * P], m.ident)
                    mm.then_inc(hid_turned, 1)
                    pe.wait_ge(hidT_ready, i * 2 + (r + 1))
                    landed(pe, i, 6 * r + 4)
                    landed(pe, i, 6 * r + 5)
                    pe.wait_ge(y_free_a, i * 2 + (r + 1))
                    pe.wait_ge(y_free_v, i * 2 + (r + 1))
                    for f in range(KD):
                        for half in range(2):
                            w = m.ring[:, (S_EXP + 6 * r + 4 + half) % RING]
                            mm = pe.matmul(bank[half * H:(half + 1) * H, 7, :], hidT[:, f % 4, (f // 4) * H:(f // 4 + 1) * H], w[:, f, :],
                                           start=(f == 0), stop=(f == KD - 1), skip_group_check=True)
                    mm.then_inc(y_ready, 1)

            gather(0)
            with pe.Fori(0, PAIRS - 1) as i:
                pair(i, False)
            pair(PAIRS - 1, True)

        @block.scalar
        def _(act):
            def take_in(i):
                act.wait_ge(gathered, i + 1)
                for k in range(4):
                    ins = act.activation(xin[:, k, :], bank[:, 0, k * P:(k + 1) * P], ACT.Identity,
                                         scale=m.a2[:, k:k + 1], bias=m.mod[:, 16 + k, 0:1])
                ins.then_inc(xin_a, 1)

            def pair(i, last):
                for r in range(2):
                    act.wait_ge(g_ready, i * 2 + (r + 1))
                    act.activation(sig[:, :], bank[:, 2, :], ACT.Sigmoid).then_inc(sig_ready, 1)
                    if r == 1 and not last:
                        take_in(i + 1)
                    act.wait_ge(hid_turned, i * 2 + (r + 1))
                    act.activation(hidT[:, :, :], bank[:, 6, :].rearrange("p (c n) -> p c n", c=4), ACT.Copy).then_inc(hidT_ready, 1)
                    act.wait_ge(y_ready, i * 2 + (r + 1))
                    act.activation(m.y[r * H:(r + 1) * H, bass.ds(i, 1), 0:COLS], bank[0:H, 7:8, :], ACT.Copy).then_inc(y_free_a, 1)

            act.sem_inc(y_free_a, 1)
            take_in(0)
            with act.Fori(0, PAIRS - 1) as i:
                pair(i, False)
            pair(PAIRS - 1, True)

        @block.vector
        def _(dve):
            def take_in(i):
                dve.wait_ge(gathered, i + 1)
                for k in range(4, KD):
                    ins = dve.tensor_scalar(xin[:, k, :], bank[:, 1, (k - 4) * P:(k - 3) * P], m.a2[:, k:k + 1],
                                            m.mod[:, 16 + k, 0:1], ALU.mult, ALU.add)
                ins.then_inc(xin_v, 1)

            def pair(i, last):
                for r in range(2):
                    dve.wait_ge(sig_ready, i * 2 + (r + 1))
                    dve.tensor_tensor(sig[:, :], sig[:, :], bank[:, 2, :], ALU.mult).then_inc(silu_ready, 1)
                    dve.wait_ge(silu_ready, i * 2 + (r + 1))
                    dve.wait_ge(u_ready, i * 2 + (r + 1))
                    dve.tensor_tensor(hid[:, :], sig[:, :], bank[:, 3, :], ALU.mult).then_inc(hid_ready, 1)
                    if r == 1 and not last:
                        take_in(i + 1)
                    dve.wait_ge(y_ready, i * 2 + (r + 1))
                    dve.tensor_copy(m.y[r * H:(r + 1) * H, bass.ds(i, 1), COLS:D], bank[H:P, 7:8, :]).then_inc(y_free_v, 1)

            dve.sem_inc(y_free_v, 1)
            take_in(0)
            with dve.Fori(0, PAIRS - 1) as i:
                pair(i, False)
            pair(PAIRS - 1, True)


def scatter(nc, m, I):
    def products(pe, ready):
        for t in range(TT):
            for n in range(2):
                for i in range(EXPERTS // 2):
                    mm = pe.matmul(m.bank[:, 2 * t + n, :], m.spread[:, i, t * P:(t + 1) * P], m.y[:, i, n * COLS:(n + 1) * COLS],
                                   start=(i == 0), stop=(i == EXPERTS // 2 - 1))
            mm.then_inc(ready, 1)

    residual(nc, m, I, "out2", m.x, m.xn3, products, lambda sp, ready: None, None, m.gate2)


def turn_gdn(nc, m, I):
    m.spilled = m.sem("x3_spilled")
    turn_features(nc, m, "h3T", [rows_of(m.xn3, k) for k in range(KD)], m.h3T, m.vecs[:, V_MIX2:V_MIX2 + KD],
                  loads=lambda sp: sp.dma_start(m.x_spill, m.x[:, :, :]).then_inc(m.spilled, 16))


def gdn_project(nc, m, I):
    bank = m.bank
    QKV = 3 * GH
    h = (m.arena("h3T_hi", [P, KD, T], 16, F32R), m.arena("h3T_lo", [P, KD, T], 0, F32R))
    bufs = split_buffers(m, "gdn_w", (32, 40))
    NB = len(bufs)
    acc = m.arena("conv_acc", [P, 2, T], 112)
    sig = m.arena("conv_sig", [P, 2, T], 116)
    wab = m.arena("w_rates", [P, KD, 2 * GH], 120)
    wab_parts = (m.arena("w_rates_hi", [P, KD, 2 * GH], 120.5, F32R), m.arena("w_rates_lo", [P, KD, 2 * GH], 121, F32R))
    NQ = QKV + 8
    w_in = m.sem("w_rates_in")
    h_hi, h_lo = m.sem("h3_hi_ready"), m.sem("h3_lo_ready")
    w_hi, w_lo = m.sem("gdn_w_hi_ready"), m.sem("gdn_w_lo_ready")
    used = m.sem("gdn_w_used")
    gate_ready = m.sem("gdn_gate_ready")
    rates_split, rates_ready = m.sem("w_rates_split"), m.sem("rates_ready")
    conv = m.sem("gdn_conv")
    sig_ready = m.sem("gdn_conv_sig")
    stored = m.sem("gdn_conv_stored")
    gate_out = m.sem("gdn_gate_out")
    with nc.Block() as block:
        @block.sync
        def _(sp):
            sp.dma_start(wab[:, :, :], I["gdn_w_in_2"][0, :, 8 * COLS:8 * COLS + 2 * GH].rearrange("(k p) n -> p k n", p=P)).then_inc(w_in, 16)
            stream(sp, m, I, S_GIN + RING, S_GIN + 8, lambda s: (w_lo, 4 * (s - S_GIN + 1)))
            stream(sp, m, I, S_GOUT, S_GOUT + 2, lambda s: (w_lo, 4 * (s - S_GIN + 1)))

        @block.tensor
        def _(pe):
            def both(k, cols):
                return h[0][:, k, cols], h[1][:, k, cols]

            for q in range(QKV):
                hi, lo = [shaped(b, False) for b in bufs[q % NB]]
                pe.wait_ge(w_lo, q + 1)
                if q >= 8:
                    pe.wait_ge(conv, 4 * (q - 7))
                for k in range(KD):
                    if q == 0:
                        pe.wait_ge(h_lo, k + 1)
                    mm = product3(pe, bank[:, q % 8, :], (hi[:, k, :], lo[:, k, :]), both(k, slice(0, T)), k == 0, k == KD - 1)
                mm.then_inc(used, 1)
            for q in range(QKV, NQ):
                n, i = divmod(q - QKV, 4)
                hi, lo = [shaped(b, True) for b in bufs[q % NB]]
                pe.wait_ge(w_lo, q + 1)
                for t in range(TT):
                    if i == 0:
                        pe.wait_ge(conv, 4 * (QKV - 8 + 4 * n + t + 1))
                    for k in range(2):
                        mm = product3(pe, bank[:, 4 * n + t, :], both(2 * i + k, slice(t * P, (t + 1) * P)),
                                      (hi[:, k, :], lo[:, k, :]), i == 0 and k == 0, i == 3 and k == 1)
                    if q == NQ - 1:
                        mm.then_inc(gate_ready, 1)
                if q < NQ - 1:
                    mm.then_inc(used, 1)
            pe.wait_ge(rates_split, 2)
            pe.wait_ge(gate_out, 1)
            for t in range(TT):
                for k in range(KD):
                    mm = product3(pe, bank[:, 0, t * 2 * GH:(t + 1) * 2 * GH], both(k, slice(t * P, (t + 1) * P)),
                                  (wab_parts[0][:, k, :], wab_parts[1][:, k, :]), k == 0, k == KD - 1)
            mm.then_inc(rates_ready, 1)

        @block.vector
        def _(dve):
            def rest(q):
                by_rows = q >= QKV
                dve.wait_ge(w_hi, q + 1)
                hi, lo = [shaped(b, by_rows) for b in bufs[q % NB]]
                dve.tensor_tensor(lo, slab_part(m, S_GIN + q // 4, q % 4, by_rows), hi, ALU.subtract).then_inc(w_lo, 1)

            for k in range(KD):
                if k == 1:
                    rest(0)
                dve.wait_ge(h_hi, k + 1)
                dve.tensor_tensor(h[1][:, k, :], m.h3T[:, k, :], h[0][:, k, :], ALU.subtract).then_inc(h_lo, 1)
            rest(1)
            for u in range(QKV):
                x, a = bank[:, u % 8, :], acc[:, u % 2, :]
                dve.wait_ge(used, u + 1)
                if u >= 2:
                    dve.wait_ge(stored, u - 1)

                def tap(j):
                    return m.vecs[:, V_CONV + j * QKV + u:V_CONV + j * QKV + u + 1]

                dve.tensor_scalar(a, x, tap(CONV_W - 1), None, ALU.mult).then_inc(conv, 1)
                for d in range(1, CONV_W):
                    dve.wait_ge(conv, 4 * u + d)
                    dve.scalar_tensor_tensor(out=a[:, d:], in0=x[:, :T - d], scalar=tap(CONV_W - 1 - d), in1=a[:, d:],
                                             op0=ALU.mult, op1=ALU.add).then_inc(conv, 1)
                    if d == 1:
                        rest(u + NB)
            for q in range(QKV + NB, NQ):
                rest(q)
            dve.wait_ge(rates_split, 1)
            dve.tensor_tensor(wab_parts[1][:, :, :], wab[:, :, :], wab_parts[0][:, :, :], ALU.subtract).then_inc(rates_split, 1)

        @block.scalar
        def _(act):
            def leading(q):
                slab_wait(act, m, S_GIN + q // 4)
                if q >= NB:
                    act.wait_ge(used, q - NB + 1)
                act.activation(shaped(bufs[q % NB][0], q >= QKV), slab_part(m, S_GIN + q // 4, q % 4, q >= QKV),
                               ACT.Copy).then_inc(w_hi, 1)

            for k in range(KD):
                if k == 1:
                    act.wait_ge(m.spilled, 16)
                    leading(0)
                act.activation(h[0][:, k, :], m.h3T[:, k, :], ACT.Copy).then_inc(h_hi, 1)
            leading(1)
            for u in range(QKV):
                leading(u + NB)
                act.wait_ge(conv, 4 * u + 4)
                if u >= 2:
                    act.wait_ge(stored, u - 1)
                act.activation(sig[:, u % 2, :], acc[:, u % 2, :], ACT.Sigmoid).then_inc(sig_ready, 1)
            for q in range(QKV + NB, NQ):
                leading(q)
            act.wait_ge(w_in, 16)
            act.activation(wab_parts[0][:, :, :], wab[:, :, :], ACT.Copy).then_inc(rates_split, 1)
            for n in range(2):
                for t in range(TT):
                    if n == 0:
                        act.wait_ge(used, QKV + 4)
                    else:
                        act.wait_ge(gate_ready, t + 1)
                    act.activation(m.gate[:, t, n * COLS:(n + 1) * COLS], bank[:, 4 * n + t, :], ACT.Copy).then_inc(gate_out, 1)
            act.wait_ge(rates_ready, 1)
            act.activation(m.rates[:, :, :], bank[:, 0, 0:TT * 2 * GH].rearrange("p (t n) -> p t n", t=TT), ACT.Copy).then_inc(gate_out, 1)

        @block.gpsimd
        def _(pool):
            for u in range(QKV):
                pool.wait_ge(sig_ready, u + 1)
                pool.tensor_tensor(m.qkvT[:, u, :], acc[:, u % 2, :], sig[:, u % 2, :], ALU.mult).then_inc(stored, 1)


def gdn_norms(nc, m, I):
    bank = m.bank
    sq = m.arena("gdn_square", [P, 2, T], 112)
    sd = m.arena("gdn_length", [P, 2, T], 116)
    rb = m.arena("rate_bias", [P, 2, GH], 120)
    tm = m.arena("rate_tmp", [P, 4, TT, GH], 120.125)
    NQ = 2 * GH
    order = list(range(GH, 2 * GH)) + list(range(GH))
    rb_in = m.sem("rate_bias_in")
    squared = m.sem("gdn_squared")
    sums = m.sem("gdn_sums")
    rooted = m.sem("gdn_rooted")
    normed = m.sem("gdn_normed")
    turned = m.sem("gdn_turned")
    tok_out = m.sem("gdn_tok_out")
    step = m.sem("rate_step")
    act_step = m.sem("rate_act_step")
    g_ready = m.sem("g_ready")
    g_sums = m.sem("g_sums")
    g_exp = m.sem("g_exp")
    abs_ready = m.sem("rate_abs")
    with nc.Block() as block:
        @block.sync
        def _(sp):
            sp.dma_start(rb[:, 0, :], I["gdn_a_log_2"].partition_broadcast(P)).then_inc(rb_in, 16)
            sp.dma_start(rb[:, 1, :], I["gdn_dt_bias_2"].partition_broadcast(P)).then_inc(rb_in, 16)
            sp.wait_ge(rb_in, 32)

        @block.scalar
        def _(act):
            a, b = m.rates[:, :, 0:GH], m.rates[:, :, GH:2 * GH]
            act.wait_ge(rb_in, 32)
            act.activation(rb[:, 0, :], rb[:, 0, :], ACT.Exp).then_inc(act_step, 1)
            act.activation(m.beta[:, :, :], b, ACT.Sigmoid).then_inc(act_step, 1)
            act.wait_ge(abs_ready, 1)
            act.activation(tm[:, 2], tm[:, 1], ACT.Exp, scale=-1.0).then_inc(act_step, 1)
            act.wait_ge(act_step, 3)
            act.activation(tm[:, 3], tm[:, 2], ACT.Ln, bias=m.ones[:, 0:1]).then_inc(act_step, 1)
            act.wait_ge(g_sums, TT)
            act.activation(m.decays[:, :, :, :], bank[:, 7, 0:3 * TT * GH].rearrange("p (t s n) -> p s t n", t=TT, s=3),
                           ACT.Exp).then_inc(g_exp, 1)
            for u in range(NQ):
                if u >= 2:
                    act.wait_ge(sums, u - 1)
                act.activation(sq[:, u % 2, :], m.qkvT[:, order[u], :], ACT.Square).then_inc(squared, 1)
                act.wait_ge(sums, u + 1)
                if u >= 2:
                    act.wait_ge(normed, u - 1)
                act.activation(sd[:, u % 2, :], bank[:, u % 2, :], ACT.Sqrt, bias=m.eps[:, :]).then_inc(rooted, 1)
                if u < GH:
                    act.wait_ge(turned, 2 * u + 1)
                    act.activation(m.vtok[:, :, u * P:(u + 1) * P], bank[:, 2 + u % 2, :].rearrange("p (t n) -> p t n", t=TT),
                                   ACT.Copy).then_inc(tok_out, 1)
                    act.wait_ge(turned, 2 * u + 2)
                    act.activation(m.ktok[:, :, u * P:(u + 1) * P], bank[:, 4 + u % 2, :].rearrange("p (t n) -> p t n", t=TT),
                                   ACT.Copy).then_inc(tok_out, 1)

        @block.tensor
        def _(pe):
            pe.wait_ge(g_ready, 1)
            for t in range(TT):
                for i, tri in enumerate((m.upto, m.after, m.ones[:, :])):
                    at = (3 * t + i) * GH
                    mm = pe.matmul(bank[:, 7, at:at + GH], tri, m.g[:, t, :], start=True, stop=True)
                mm.then_inc(g_sums, 1)
            for u in range(NQ):
                pe.wait_ge(squared, u + 1)
                if u >= 2:
                    pe.wait_ge(rooted, u - 1)
                pe.matmul(bank[:, u % 2, :], m.ones[:, :], sq[:, u % 2, :], start=True, stop=True).then_inc(sums, 1)
                if u < GH:
                    if u >= 2:
                        pe.wait_ge(tok_out, 2 * u - 2)
                    for t in range(TT):
                        mm = pe.transpose(bank[:, 2 + u % 2, t * P:(t + 1) * P], m.qkvT[:, 2 * GH + u, t * P:(t + 1) * P], m.ident)
                    mm.then_inc(turned, 1)
                    pe.wait_ge(normed, u + 1)
                    for t in range(TT):
                        mm = pe.transpose(bank[:, 4 + u % 2, t * P:(t + 1) * P], m.qkvT[:, GH + u, t * P:(t + 1) * P], m.ident)
                    mm.then_inc(turned, 1)

        @block.vector
        def _(dve):
            link = chain(dve, step)
            dve.wait_ge(rb_in, 32)
            link(dve.tensor_tensor(tm[:, 0], m.rates[:, :, 0:GH], rb[:, 1, :].unsqueeze(1).to_broadcast([P, TT, GH]), ALU.add))
            dve.scalar_tensor_tensor(out=tm[:, 1], in0=tm[:, 0], scalar=-1.0, in1=tm[:, 0], op0=ALU.mult,
                                     op1=ALU.max).then_inc(abs_ready, 1)
            dve.wait_ge(abs_ready, 1)
            link(dve.tensor_scalar(tm[:, 0], tm[:, 0], 0.0, None, ALU.max))
            dve.wait_ge(act_step, 4)
            link(dve.tensor_tensor(tm[:, 0], tm[:, 0], tm[:, 3], ALU.add))
            link(dve.tensor_scalar(tm[:, 0], tm[:, 0], -1.0, None, ALU.mult))
            dve.tensor_tensor(m.g[:, :, :], tm[:, 0], rb[:, 0, :].unsqueeze(1).to_broadcast([P, TT, GH]), ALU.mult).then_inc(g_ready, 1)
            link(dve.tensor_scalar(m.neg_beta[:, :, :], m.beta[:, :, :], -1.0, None, ALU.mult))
            dve.wait_ge(g_exp, 1)
            dve.tensor_tensor(m.neg_beta_decay[:, :, :], m.neg_beta[:, :, :], m.decays[:, 0], ALU.mult)
            for u in range(NQ):
                x = m.qkvT[:, order[u], :]
                dve.wait_ge(rooted, u + 1)
                link(dve.reciprocal(sd[:, u % 2, :], sd[:, u % 2, :]))
                dve.scalar_tensor_tensor(out=x, in0=x, scalar=1.0 if order[u] >= GH else P ** -0.5, in1=sd[:, u % 2, :],
                                         op0=ALU.mult, op1=ALU.mult).then_inc(normed, 1)


def gdn_pairs(nc, m, I):
    bank = m.bank
    NB = TT * 2
    gm = m.arena("g_after", [P, 2, COLS], 112)
    ee = m.arena("pair_decay", [P, 2, COLS], 116)
    gm_ready = m.sem("g_after_ready")
    d_ready = m.sem("pair_sums")
    kk_ready = m.sem("pair_dots")
    e_ready = m.sem("pair_exp")
    nb_ready = m.sem("pair_neg_beta")
    step = m.sem("pair_step")
    done = m.sem("pair_done")
    masked = m.sem("pair_masked")

    def heads(v):
        return v.rearrange("p (h n) -> p h n", h=4)

    with nc.Block() as block:
        @block.gpsimd
        def _(pool):
            for b in range(NB):
                c, hh = divmod(b, 2)
                hs = slice(4 * hh, 4 * hh + 4)
                if b >= 2:
                    pool.wait_ge(d_ready, b - 1)
                pool.tensor_tensor(heads(gm[:, b % 2, :]), m.after.unsqueeze(1).to_broadcast([P, 4, P]),
                                   m.g[:, c, hs].unsqueeze(2).to_broadcast([P, 4, P]), ALU.mult).then_inc(gm_ready, 1)
                pool.tensor_tensor(m.negA[:, b], m.after.unsqueeze(1).to_broadcast([P, 4, P]),
                                   m.neg_beta[:, c, hs].unsqueeze(2).to_broadcast([P, 4, P]), ALU.mult).then_inc(nb_ready, 1)
                pool.wait_ge(done, 2 * b + 2)
                pool.tensor_tensor(m.qkT[:, b], m.qkT[:, b], m.upto.unsqueeze(1).to_broadcast([P, 4, P]), ALU.mult).then_inc(masked, 1)
                rows = m.vtok[:, c, hh * COLS:(hh + 1) * COLS]
                pool.tensor_tensor(heads(rows), heads(rows), m.beta[:, c, hs].unsqueeze(2).to_broadcast([P, 4, P]), ALU.mult)

        @block.tensor
        def _(pe):
            for b in range(NB):
                c, hh = divmod(b, 2)
                o = 4 * (b % 2)
                pe.wait_ge(gm_ready, b + 1)
                if b >= 2:
                    pe.wait_ge(done, 2 * b - 2)
                pe.matmul(bank[:, o, :], m.upto, gm[:, b % 2, :], start=True, stop=True)
                for h in range(4):
                    mm = pe.matmul(bank[:, o + 1, h * P:(h + 1) * P], gm[:, b % 2, h * P:(h + 1) * P], m.upto, start=True, stop=True)
                mm.then_inc(d_ready, 1)
                for h in range(4):
                    q = m.qkvT[:, 4 * hh + h, c * P:(c + 1) * P]
                    k = m.qkvT[:, GH + 4 * hh + h, c * P:(c + 1) * P]
                    pe.matmul(bank[:, o + 2, h * P:(h + 1) * P], k, k, start=True, stop=True)
                    mm = pe.matmul(bank[:, o + 3, h * P:(h + 1) * P], k, q, start=True, stop=True)
                mm.then_inc(kk_ready, 1)

        @block.scalar
        def _(act):
            for b in range(NB):
                o = 4 * (b % 2)
                act.wait_ge(d_ready, b + 1)
                for i in range(2):
                    if b >= 1:
                        act.wait_ge(done, 2 * b - 1 + i)
                    act.activation(ee[:, i, :], bank[:, o + i, :], ACT.Exp).then_inc(e_ready, 1)

        @block.vector
        def _(dve):
            link = chain(dve, step)
            for b in range(NB):
                o = 4 * (b % 2)
                dve.wait_ge(kk_ready, b + 1)
                dve.wait_ge(nb_ready, b + 1)
                dve.wait_ge(e_ready, 2 * b + 1)
                neg = m.negA[:, b].rearrange("p h n -> p (h n)")
                link(dve.tensor_tensor(neg, neg, bank[:, o + 2, :], ALU.mult))
                dve.tensor_tensor(neg, neg, ee[:, 0, :], ALU.mult).then_inc(done, 1)
                dve.wait_ge(e_ready, 2 * b + 2)
                dve.tensor_tensor(m.qkT[:, b].rearrange("p h n -> p (h n)"), ee[:, 1, :], bank[:, o + 3, :], ALU.mult).then_inc(done, 1)


def gdn_inverse(nc, m, I):
    bank = m.bank
    NB = TT * 2
    X = m.arena("inv_X", [P, 2, COLS], 112)
    nL = len(LEVELS)
    rounds = [(l, b) for l in range(nL) for b in range(NB)]
    id_set = m.sem("inv_identity")
    x_ready = m.sem("inv_x_ready")
    x_out = m.sem("inv_x_out")
    delta = m.sem("inv_delta")
    merged = m.sem("inv_merged")

    def flat(v):
        return v.rearrange("p h n -> p (h n)")

    with nc.Block() as block:
        @block.gpsimd
        def _(pool):
            for dst in (m.inv, m.invT):
                pool.tensor_copy(dst[:, :, :, :].rearrange("p b h n -> p (b h) n"),
                                 m.ident.unsqueeze(1).to_broadcast([P, 4 * NB, P])).then_inc(id_set, 1)

        @block.tensor
        def _(pe):
            pe.wait_ge(id_set, 2)

            def first(r):
                l, b = rounds[r]
                if l >= 1:
                    pe.wait_ge(merged, r - NB + 1)
                if r >= 2:
                    pe.wait_ge(x_out, r - 1)
                for h in range(4):
                    mm = pe.matmul(bank[:, r % 2, h * P:(h + 1) * P], m.negA[:, b, h, :], m.invT[:, b, h, :], start=True, stop=True)
                mm.then_inc(x_ready, 1)

            first(0)
            for r, (l, b) in enumerate(rounds):
                if r + 1 < len(rounds):
                    first(r + 1)
                pe.wait_ge(x_out, r + 1)
                if r >= 2:
                    pe.wait_ge(merged, r - 1)
                o = 2 + 2 * (r % 2)
                for h in range(4):
                    cut = slice(h * P, (h + 1) * P)
                    mm = pe.matmul(bank[:, o, cut], m.inv[:, b, h, :], X[:, r % 2, cut], start=True, stop=True)
                if l < nL - 1:
                    for h in range(4):
                        cut = slice(h * P, (h + 1) * P)
                        mm = pe.matmul(bank[:, o + 1, cut], X[:, r % 2, cut], m.inv[:, b, h, :], start=True, stop=True)
                mm.then_inc(delta, 1)

        @block.scalar
        def _(act):
            for r in range(len(rounds)):
                act.wait_ge(x_ready, r + 1)
                if r >= 2:
                    act.wait_ge(delta, r - 1)
                act.activation(X[:, r % 2, :], bank[:, r % 2, :], ACT.Copy).then_inc(x_out, 1)

        @block.vector
        def _(dve):
            dve.wait_ge(id_set, 2)
            for r, (l, b) in enumerate(rounds):
                o = 2 + 2 * (r % 2)
                dve.wait_ge(delta, r + 1)
                up = m.masks[:, l, :].unsqueeze(1).to_broadcast([P, 4, P])
                low = m.masks[:, nL + l, :].unsqueeze(1).to_broadcast([P, 4, P])
                ins = dve.copy_predicated(m.invT[:, b], up, bank[:, o, :].rearrange("p (h n) -> p h n", h=4))
                if l < nL - 1:
                    ins = dve.copy_predicated(m.inv[:, b], low, bank[:, o + 1, :].rearrange("p (h n) -> p h n", h=4))
                ins.then_inc(merged, 1)


def gdn_scan(nc, m, I):
    bank = m.bank
    NB = TT * 2
    S = m.arena("gdn_state", [P, 2, COLS], 112)
    new = m.arena("gdn_new", [P, 2, COLS], 116)
    oi = m.scratch("gdn_o_state", [P, 2, COLS], 0)
    late = m.scratch("gdn_new_decayed", [P, 2, COLS], 4)
    ks_ready, r_ready, new_ready, new_out, late_ready, qs_ready, o_ready, ds_ready, oi_ready, o_out, s_ready = [
        m.sem(f"scan_{n}") for n in ("ks", "r", "new", "new_out", "late", "qs", "o", "ds", "oi", "o_out", "s")]

    def cut(h):
        return slice(h * P, (h + 1) * P)

    with nc.Block() as block:
        @block.tensor
        def _(pe):
            for c in range(TT):
                tok = slice(c * P, (c + 1) * P)
                for g in range(2 if c else 0):
                    pe.wait_ge(s_ready, 2 * (c - 1) + g + 1)
                    for h in range(4):
                        mm = pe.matmul(bank[:, g, cut(h)], m.qkvT[:, GH + 4 * g + h, tok], S[:, g, cut(h)], start=True, stop=True)
                    mm.then_inc(ks_ready, 1)
                for g in range(2 if c else 0):
                    if c >= 2:
                        pe.wait_ge(oi_ready, 2 * (c - 2) + g + 1)
                    for h in range(4):
                        mm = pe.matmul(bank[:, 2 + g, cut(h)], m.qkvT[:, 4 * g + h, tok], S[:, g, cut(h)], start=True, stop=True)
                    mm.then_inc(qs_ready, 1)
                for g in range(2):
                    n = 2 * c + g
                    if c:
                        pe.wait_ge(r_ready, n - 1)
                    for h in range(4):
                        mm = pe.matmul(bank[:, 4 + g, cut(h)], m.invT[:, n, h, :], m.vtok[:, c, cut(4 * g + h)], start=True, stop=True)
                    mm.then_inc(new_ready, 1)
                for g in range(2):
                    n = 2 * c + g
                    pe.wait_ge(late_ready, n + 1)
                    for h in range(4):
                        mm = pe.matmul(bank[:, g, cut(h)], m.ktok[:, c, cut(4 * g + h)], late[:, g, cut(h)], start=True, stop=True)
                    mm.then_inc(ds_ready, 1)
                for g in range(2):
                    n = 2 * c + g
                    pe.wait_ge(new_out, n + 1)
                    if c:
                        pe.wait_ge(o_out, n - 1)
                    for h in range(4):
                        mm = pe.matmul(bank[:, 6 + g, cut(h)], m.qkT[:, n, h, :], new[:, g, cut(h)], start=True, stop=True)
                    mm.then_inc(o_ready, 1)

        @block.scalar
        def _(act):
            for c in range(TT):
                for g in range(2):
                    n = 2 * c + g
                    act.wait_ge(late_ready, n + 1)
                    if c:
                        act.wait_ge(o_ready, n - 1)
                    act.activation(new[:, g, :], bank[:, 4 + g, :], ACT.Copy).then_inc(new_out, 1)
                for g in range(2 if c else 0):
                    act.wait_ge(qs_ready, 2 * (c - 1) + g + 1)
                    if c >= 2:
                        act.wait_ge(o_out, 2 * (c - 1) + g + 1)
                    for h in range(4):
                        ins = act.activation(oi[:, g, cut(h)], bank[:, 2 + g, cut(h)], ACT.Copy,
                                             scale=m.decays[:, 0, c, 4 * g + h:4 * g + h + 1])
                    ins.then_inc(oi_ready, 1)

        @block.vector
        def _(dve):
            for c in range(TT):
                for g in range(2 if c else 0):
                    dve.wait_ge(ks_ready, 2 * (c - 1) + g + 1)
                    for h in range(4):
                        v = m.vtok[:, c, cut(4 * g + h)]
                        ins = dve.scalar_tensor_tensor(out=v, in0=bank[:, g, cut(h)],
                                                       scalar=m.neg_beta_decay[:, c, 4 * g + h:4 * g + h + 1], in1=v,
                                                       op0=ALU.mult, op1=ALU.add)
                    ins.then_inc(r_ready, 1)
                for g in range(2):
                    n = 2 * c + g
                    dve.wait_ge(new_ready, n + 1)
                    dve.tensor_tensor(late[:, g, :].rearrange("p (h n) -> p h n", h=4),
                                      bank[:, 4 + g, :].rearrange("p (h n) -> p h n", h=4),
                                      m.decays[:, 1, c, 4 * g:4 * g + 4].unsqueeze(2).to_broadcast([P, 4, P]),
                                      ALU.mult).then_inc(late_ready, 1)
                for g in range(2):
                    n = 2 * c + g
                    dve.wait_ge(ds_ready, n + 1)
                    if c == 0:
                        dve.tensor_copy(S[:, g, :], bank[:, g, :]).then_inc(s_ready, 1)
                    elif c < TT - 1:
                        dve.wait_ge(qs_ready, n - 1)
                        dve.wait_ge(s_ready, n - 1)
                        for h in range(4):
                            ins = dve.scalar_tensor_tensor(out=S[:, g, cut(h)], in0=S[:, g, cut(h)],
                                                           scalar=m.decays[:, 2, c, 4 * g + h:4 * g + h + 1],
                                                           in1=bank[:, g, cut(h)], op0=ALU.mult, op1=ALU.add)
                        ins.then_inc(s_ready, 1)
                for g in range(2):
                    n = 2 * c + g
                    dve.wait_ge(o_ready, n + 1)
                    o = m.vtok[:, c, 4 * g * P:4 * (g + 1) * P]
                    if c:
                        dve.wait_ge(oi_ready, n - 1)
                        dve.tensor_tensor(o, bank[:, 6 + g, :], oi[:, g, :], ALU.add).then_inc(o_out, 1)
                    else:
                        dve.tensor_copy(o, bank[:, 6 + g, :]).then_inc(o_out, 1)


def gdn_gate(nc, m, I):
    nu = TT * GH
    o, gate = m.vtok, m.gate
    sq = m.arena("gdn_o_square", [P, TT, D], 16)
    sg = m.arena("gdn_gate_sig", [P, TT, D], 48)
    w = m.arena("gdn_norm_w", [P, P], 112)
    ss = m.arena("gdn_o_ss", [P, TT, GH], 113)
    sd = m.arena("gdn_o_sd", [P, TT, GH], 114)
    rstd = m.arena("gdn_o_rstd", [P, TT, GH], 115)
    w_in, squared, summed, rooted, inverse, sig, gated, scaled = [
        m.sem(f"gdn_gate_{n}") for n in ("w_in", "squared", "summed", "rooted", "inverse", "sig", "gated", "scaled")]

    def heads(v):
        return v.rearrange("p (h n) -> p h n", n=P)

    with nc.Block() as block:
        @block.sync
        def _(sp):
            sp.dma_start(w[:, :], I["gdn_o_norm_g_2"].partition_broadcast(P)).then_inc(w_in, 16)
            sp.wait_ge(w_in, 16)

        @block.scalar
        def _(act):
            for t in range(TT):
                act.activation(sq[:, t, :], o[:, t, :], ACT.Square).then_inc(squared, 1)
            for t in range(TT):
                act.activation(sg[:, t, :], gate[:, t, :], ACT.Sigmoid).then_inc(sig, 1)
            act.wait_ge(summed, TT)
            act.activation(sd[:, :, :], ss[:, :, :], ACT.Sqrt, bias=m.eps[:, :], scale=1.0 / P).then_inc(rooted, 1)

        @block.gpsimd
        def _(pool):
            pool.wait_ge(w_in, 16)
            for t in range(TT):
                pool.wait_ge(sig, t + 1)
                pool.tensor_tensor(gate[:, t, :], gate[:, t, :], sg[:, t, :], ALU.mult).then_inc(gated, 1)
                pool.wait_ge(gated, 2 * t + 1)
                pool.tensor_tensor(heads(gate[:, t, :]), heads(gate[:, t, :]), w[:, :].unsqueeze(1).to_broadcast([P, GH, P]),
                                   ALU.mult).then_inc(gated, 1)

        @block.vector
        def _(dve):
            for t in range(TT):
                dve.wait_ge(squared, t + 1)
                dve.tensor_reduce(ss[:, t, :], heads(sq[:, t, :]), AX.X, ALU.add).then_inc(summed, 1)
            dve.wait_ge(rooted, 1)
            dve.reciprocal(rstd[:, :, :], sd[:, :, :]).then_inc(inverse, 1)
            dve.wait_ge(inverse, 1)
            for t in range(TT):
                dve.tensor_tensor(heads(o[:, t, :]), heads(o[:, t, :]), rstd[:, t, :].unsqueeze(2).to_broadcast([P, GH, P]),
                                  ALU.mult).then_inc(scaled, 1)
            for t in range(TT):
                dve.wait_ge(scaled, t + 1)
                dve.wait_ge(gated, 2 * t + 2)
                dve.tensor_tensor(o[:, t, :], o[:, t, :], gate[:, t, :], ALU.mult)


def turn_gdn_out(nc, m, I):
    turn_features(nc, m, "ogT", [rows_of(m.vtok, k) for k in range(KD)], m.ogT)


def gdn_project_out(nc, m, I):
    x_in = m.sem("x3_again")

    def products(pe, ready):
        for t in range(TT):
            for n in range(2):
                slab_wait(pe, m, S_GOUT + n)
                for k in range(KD):
                    mm = pe.matmul(m.bank[:, 2 * t + n, :], m.ogT[:, k, t * P:(t + 1) * P], m.ring[:, (S_GOUT + n) % RING, k, :],
                                   start=(k == 0), stop=(k == KD - 1))
            mm.then_inc(ready, 1)

    def loads(sp, ready):
        sp.dma_start(m.x[:, :, :], m.x_spill).then_inc(x_in, 16)
        stream(sp, m, I, S_MLP, S_MLP + 2, lambda s: (x_in, 16))
        stream(sp, m, I, S_MLP + 2, S_MLP + 4, lambda s: (ready, TT))

    residual(nc, m, I, "out3", m.x, m.xn4, products, loads, (x_in, 16))


def turn_mlp(nc, m, I):
    turn_features(nc, m, "h4T", [rows_of(m.xn4, k) for k in range(KD)], m.h4T, m.vecs[:, V_MLP2:V_MLP2 + KD])


def mlp(nc, m, I, out):
    bank, x = m.bank, m.x
    GROUPS = D_FF // D
    h_parts = (m.arena("h4T_hi", [P, KD, T], 16, F32R), m.arena("h4T_lo", [P, KD, T], 48, F32R))
    up = (m.arena("up_hi", [P, KD, T], 64, F32R), m.arena("up_lo", [P, KD, T], 80, F32R))
    bufs = split_buffers(m, "mlp_w", (0, 8, 96, 104))
    NB = len(bufs)
    r = m.arena("mlp_relu", [P, 2, T], 112)
    sq = m.arena("mlp_relu2", [P, 2, T], 116)
    junk = m.arena("final_square", [P, 2, D], 112)
    w = m.small("final_norm_w", [P, D], 0)
    st = m.small("final_stats", [P, 3, TT], 4 * KB)
    quarters = [(S_MLP + 4 * g + j, i, g, j - 2 if j >= 2 else None) for g in range(GROUPS) for j in range(4) for i in range(4)]
    NQ = len(quarters)
    h_hi, h_lo = m.sem("h4_hi_ready"), m.sem("h4_lo_ready")
    w_hi, w_lo = m.sem("mlp_w_hi_ready"), m.sem("mlp_w_lo_ready")
    used = m.sem("mlp_w_used")
    relu, squared = m.sem("mlp_relu_ready"), m.sem("mlp_squared")
    up_hi, up_lo = m.sem("up_hi_ready"), m.sem("up_lo_ready")
    added = m.sem("mlp_added")
    w_in, sums, roots, inverse = m.sem("final_w_in"), m.sem("final_sums"), m.sem("final_roots"), m.sem("final_inverse")
    done, stored = m.sem("final_done"), m.sem("y_stored")
    y = out[0].rearrange("(t p) d -> p t d", p=P)

    def ups(q):
        return sum(n is None for _, _, _, n in quarters[:q])

    with nc.Block() as block:
        @block.sync
        def _(sp):
            sp.dma_start(w[:, :], I["final_norm_g_2"].rearrange("(o d) -> o d", o=1).partition_broadcast(P)).then_inc(w_in, 16)
            stream(sp, m, I, S_MLP + RING, S_END, lambda s: (w_lo, 4 * (s - S_MLP + 1)))
            for t in range(TT):
                sp.wait_ge(done, t + 1)
                sp.dma_start(y[:, t, :], x[:, t, :]).then_inc(stored, 16)
            sp.wait_ge(stored, 16 * TT)

        @block.tensor
        def _(pe):
            for q, (s, i, g, n) in enumerate(quarters):
                pe.wait_ge(w_lo, q + 1)
                hi, lo = [shaped(b, n is not None) for b in bufs[q % NB]]
                if n is None:
                    u = ups(q)
                    if u >= 4:
                        pe.wait_ge(relu, u - 3)
                    for k in range(KD):
                        if u == 0:
                            pe.wait_ge(h_lo, k + 1)
                        mm = product3(pe, bank[:, u % 4, :], (hi[:, k, :], lo[:, k, :]),
                                      (h_parts[0][:, k, :], h_parts[1][:, k, :]), k == 0, k == KD - 1)
                else:
                    pe.wait_ge(up_lo, 8 * g + 2 * i + 2)
                    for t in range(TT):
                        if i == 0 and 2 * g + n:
                            pe.wait_ge(added, (2 * g + n - 1) * TT + t + 1)
                        for k in range(2):
                            tok = slice(t * P, (t + 1) * P)
                            mm = product3(pe, bank[:, 4 + t, :], (up[0][:, 2 * i + k, tok], up[1][:, 2 * i + k, tok]),
                                          (hi[:, k, :], lo[:, k, :]), i == 0 and k == 0, i == 3 and k == 1)
                mm.then_inc(used, 1)

        @block.scalar
        def _(act):
            def leading(q):
                s, i, _, n = quarters[q]
                slab_wait(act, m, s)
                if q >= NB:
                    act.wait_ge(used, q - NB + 1)
                act.activation(shaped(bufs[q % NB][0], n is not None), slab_part(m, s, i, n is not None), ACT.Copy).then_inc(w_hi, 1)

            leading(0)
            for k in range(KD):
                act.activation(h_parts[0][:, k, :], m.h4T[:, k, :], ACT.Copy).then_inc(h_hi, 1)
            for q in range(1, NB):
                leading(q)
            for q, (s, i, g, n) in enumerate(quarters):
                if n is None:
                    u = ups(q)
                    act.wait_ge(used, q + 1)
                    if u >= 2:
                        act.wait_ge(squared, u - 1)
                    act.activation(r[:, u % 2, :], bank[:, u % 4, :], ACT.Relu).then_inc(relu, 1)
                if q + NB < NQ:
                    leading(q + NB)
                if n is None:
                    act.wait_ge(squared, u + 1)
                    act.activation(up[0][:, u % KD, :], sq[:, u % 2, :], ACT.Copy).then_inc(up_hi, 1)
            for t in range(TT):
                act.wait_ge(added, (2 * GROUPS - 1) * TT + t + 1)
                if t == 0:
                    act.wait_ge(up_lo, GROUPS * KD)
                if t >= 2:
                    act.wait_ge(sums, t - 1)
                act.activation(junk[:, t % 2, :], x[:, t, :], ACT.Square, accum_out=st[:, 0, t:t + 1]).then_inc(sums, 1)
                act.wait_ge(sums, t + 1)
                act.activation(st[:, 1, t:t + 1], st[:, 0, t:t + 1], ACT.Sqrt, bias=m.eps[:, :], scale=1.0 / D).then_inc(roots, 1)

        @block.gpsimd
        def _(pool):
            for u in range(GROUPS * KD):
                pool.wait_ge(relu, u + 1)
                if u >= 2:
                    pool.wait_ge(up_lo, u - 1)
                pool.tensor_tensor(sq[:, u % 2, :], r[:, u % 2, :], r[:, u % 2, :], ALU.mult).then_inc(squared, 1)

        @block.vector
        def _(dve):
            def rest(q):
                s, i, _, n = quarters[q]
                dve.wait_ge(w_hi, q + 1)
                hi, lo = [shaped(b, n is not None) for b in bufs[q % NB]]
                dve.tensor_tensor(lo, slab_part(m, s, i, n is not None), hi, ALU.subtract).then_inc(w_lo, 1)

            rest(0)
            for k in range(KD):
                dve.wait_ge(h_hi, k + 1)
                dve.tensor_tensor(h_parts[1][:, k, :], m.h4T[:, k, :], h_parts[0][:, k, :], ALU.subtract).then_inc(h_lo, 1)
            for q in range(1, NB):
                rest(q)
            for q, (s, i, g, n) in enumerate(quarters):
                if n is None:
                    u = ups(q)
                    dve.wait_ge(up_hi, u + 1)
                    dve.tensor_tensor(up[1][:, u % KD, :], sq[:, u % 2, :], up[0][:, u % KD, :], ALU.subtract).then_inc(up_lo, 1)
                elif i == 3:
                    dve.wait_ge(used, q + 1)
                    for t in range(TT):
                        o = x[:, t, n * COLS:(n + 1) * COLS]
                        dve.tensor_tensor(o, o, bank[:, 4 + t, :], ALU.add).then_inc(added, 1)
                if q + NB < NQ:
                    rest(q + NB)
            dve.wait_ge(w_in, 16)
            for t in range(TT):
                dve.wait_ge(roots, t + 1)
                dve.reciprocal(st[:, 2, t:t + 1], st[:, 1, t:t + 1]).then_inc(inverse, 1)
                dve.wait_ge(inverse, t + 1)
                dve.scalar_tensor_tensor(out=x[:, t, :], in0=x[:, t, :], scalar=st[:, 2, t:t + 1], in1=w[:, :],
                                         op0=ALU.mult, op1=ALU.mult).then_inc(done, 1)


def build(nc, I, out, stop=None, dump=None):
    m = allocate(nc)
    m.slab_loaded = [nc.alloc_semaphore(f"slab_loaded{i}") for i in range(RING)]
    m.xn1 = m.arena("xn1", [P, AT, D], 24)
    m.hT = m.arena("hT", [P, KD, TA], 60)
    m.proj = {
        "qT": m.arena("qT", [P, HEADS, T], 0), "kT": m.arena("kT", [P, HEADS, TA], 8),
        "v": m.arena("v", [P, AT, COLS], 20), "zf": m.arena("zf", [P, HEADS, TA], 32),
        "zb": m.arena("zb", [P, HEADS, TA], 44), "hv": m.arena("hv", [P, AT, COLS], 56),
        "hqT": m.arena("hqT", [P, HEADS, T], 68), "hg": m.arena("hg", [P, TT, COLS], 76),
    }
    m.mix_da = m.arena("mix_da", [P, TT, COLS], 84)
    m.scores = m.arena("scores", [P, HEADS, T], 24)
    m.states = (m.arena("states0", [P, 5, COLS], 108), m.arena("states1", [P, 5, COLS], 92))
    m.mixT = m.arena("mixT", [P, KD, T], 0)
    m.x = m.arena("x", [P, TT, D], 32)
    m.xn2 = m.arena("xn2", [P, TT, D], 48)
    m.h2T = m.arena("h2T", [P, KD, T], 64)
    m.onehot = m.arena("onehot", [P, TT, D], 0)
    m.spread = m.arena("spread", [P, EXPERTS // 2, T], 96)
    m.y = m.arena("expert_out", [P, EXPERTS // 2, D], 64)
    m.xn3 = m.arena("xn3", [P, TT, D], 48)
    NB = 2 * TT
    m.x_spill = nc.dram_tensor("x3_spill", (P, TT, D), F32).ap()
    m.h3T = m.arena("h3T", [P, KD, T], 96)
    m.qkvT = m.arena("qkvT", [P, 3 * GH, T], 48)
    m.gate = m.arena("gdn_gate", [P, TT, D], 96)
    m.vtok = m.arena("gdn_vtok", [P, TT, D], 0)
    m.ktok = m.arena("gdn_ktok", [P, TT, D], 16)
    m.qkT = m.arena("gdn_qkT", [P, NB, 4, P], 32)
    m.invT = m.arena("gdn_invT", [P, NB, 4, P], 80)
    m.negA = m.scratch("gdn_negA", [P, NB, 4, P], 0)
    m.inv = m.scratch("gdn_inv", [P, NB, 4, P], 16)
    m.rates = m.small("rates", [P, TT, 2 * GH], 0)
    m.beta = m.small("beta", [P, TT, GH], 256)
    m.neg_beta = m.small("neg_beta", [P, TT, GH], 384)
    m.neg_beta_decay = m.small("neg_beta_decay", [P, TT, GH], 512)
    m.g = m.small("g_log", [P, TT, GH], 640)
    m.decays = m.small("decays", [P, 3, TT, GH], 768)
    m.ogT = m.arena("ogT", [P, KD, T], 64)
    m.xn4 = m.arena("xn4", [P, TT, D], 80)
    m.h4T = m.arena("h4T", [P, KD, T], 64)
    held = []

    def sem(name):
        held.append(nc.alloc_semaphore(name))
        return held[-1]

    m.sem = sem
    for stage in STAGES:
        stage(nc, m, I)
        if stage in RELEASE:
            nc.clear_and_free_semaphores(held)
            nc.all_engine_barrier()
            held.clear()
        if stop == stage.__name__:
            dump(nc, m)
            return
    mlp(nc, m, I, out)


STAGES = [modulation, hidden_transposed, project_in, rotary, attention, forget_gates,
          recurrence_forward, recurrence_backward, mix_outputs, turn_mix, project_out, turn_ffn, route,
          experts, scatter, turn_gdn, gdn_project, gdn_norms, gdn_pairs, gdn_inverse, gdn_scan, gdn_gate,
          turn_gdn_out, gdn_project_out, turn_mlp]
RELEASE = (mix_outputs, scatter, gdn_pairs)


USED = ["x", "c", "ctx", "c_ctx", "w_ada", "b_ada", "norm_pre_mix", "norm_post_mix", "norm_pre_ffn", "norm_post_ffn",
        "w_in", "da_lambda_q1", "da_lambda_k1", "da_lambda_q2", "da_lambda_k2", "da_subln", "hg_lower_bound",
        "hg_norm", "w_out", "w_router", "w_gate", "w_up", "w_down", "norm_mix_g_2", "norm_mlp_g_2", "mlp_w1_2",
        "mlp_w2_2", "gdn_w_in_2", "gdn_conv_w_2", "gdn_a_log_2", "gdn_dt_bias_2", "gdn_o_norm_g_2", "gdn_w_out_2",
        "final_norm_g_2"]


def kernel(**inputs):
    import concourse.bacc as bacc
    from concourse.bass_utils import run_bass_kernel_spmd

    nc = bacc.Bacc("TRN2", target_bir_lowering=False, num_devices=1)
    arrays = {name: np.ascontiguousarray(inputs[name]) for name in USED}
    arrays.update(shape_constants())
    I = {name: nc.dram_tensor(name, a.shape, mybir.dt.from_np(a.dtype), kind="ExternalInput").ap()
         for name, a in arrays.items()}
    out = nc.dram_tensor("y", (1, T, D), F32, kind="ExternalOutput").ap()
    build(nc, I, out)
    result = run_bass_kernel_spmd(nc, [arrays], core_ids=[0])
    return result.results[0]["y"]
```
